# Optimizing a Trainium2 kernel written in Bass

```python
import math
import jax, jax.numpy as jnp
from jax import lax
import numpy as np

D_MODEL = 1024
BATCH = 1
SEQ = 256
DEPTH = 1

SSM_D_INNER = D_MODEL
SSM_HEAD_DIM = 64
SSM_HEADS = SSM_D_INNER // SSM_HEAD_DIM
SSM_GROUPS = 4
SSM_D_STATE = 128
SSM_CONV = 4
SSM_CHUNK = 128
SSM_CONV_DIM = SSM_D_INNER + 2 * SSM_GROUPS * SSM_D_STATE
SB_HEAD_DIM = 128
SB_HEADS = 4
SB_QBLK = 128
NSA_HEAD_DIM = 64
NSA_Q_HEADS = 8
NSA_KV_HEADS = 2
CMP_STRIDE = 16
CMP_LEN = 2 * CMP_STRIDE
SEL_BLOCK = 64
N_SEL = 8
WINDOW = 512
NSA_QBLK = 32
D_FF = 11 * D_MODEL // 4
FFN_CONV = 3

NORM_EPS = 1e-6
NEG = -1e30
BIG = 1e30

IN_SPLIT_SIZES = (SSM_D_INNER, SSM_CONV_DIM, SSM_HEADS, 3 * SB_HEADS * SB_HEAD_DIM,
                  NSA_Q_HEADS * NSA_HEAD_DIM, 6 * NSA_KV_HEADS * NSA_HEAD_DIM, 3 * NSA_Q_HEADS, 3 * D_MODEL)
D_IN = sum(IN_SPLIT_SIZES)


def rms_norm(x, w):
    xf = x.astype(jnp.float32)
    y = xf * lax.rsqrt(jnp.mean(xf * xf, axis=-1, keepdims=True) + NORM_EPS)
    return (y * w.astype(jnp.float32)).astype(x.dtype)

def causal_dwconv(x, w, b):
    k, c = w.shape
    out = lax.conv_general_dilated(x, w[:, None, :].astype(x.dtype), window_strides=(1,),
                                   padding=[(k - 1, 0)], dimension_numbers=('NWC', 'WIO', 'NWC'),
                                   feature_group_count=c)
    return out + b.astype(x.dtype)

def masked_softmax(s, mask):
    p = jax.nn.softmax(jnp.where(mask, s, NEG), axis=-1)
    return jnp.where(mask, p, 0.0)

def alibi_slopes(n):
    return jnp.asarray(2.0 ** (-8.0 * np.arange(1, n + 1) / n), dtype=jnp.float32)

def split_points():
    return np.cumsum(np.array(IN_SPLIT_SIZES))[:-1].tolist()

def ssd_chunked(x, dt, a, bmat, cmat):
    bsz, s, h, p = x.shape
    g, n = bmat.shape[2], bmat.shape[3]
    hg = h // g
    nc = s // SSM_CHUNK

    def chunks(t, tail):
        return jnp.moveaxis(t.reshape((bsz, nc, SSM_CHUNK) + tail), 1, 0)

    xc = chunks(x, (g, hg, p))
    dtc = chunks(dt, (g, hg))
    bc = chunks(bmat, (g, n))
    cc = chunks(cmat, (g, n))
    a = a.reshape(g, hg)
    tri = jnp.tril(jnp.ones((SSM_CHUNK, SSM_CHUNK), dtype=bool))[None, :, :, None, None]

    def step(state, inp):
        x_c, dt_c, b_c, c_c = inp
        acum = jnp.cumsum(dt_c * a, axis=1)
        seg = acum[:, :, None] - acum[:, None, :]
        decay = jnp.exp(jnp.where(tri, seg, -jnp.inf))
        cb = jnp.einsum('btgn,bsgn->btsg', c_c, b_c)
        w = cb[..., None] * decay * dt_c[:, None]
        y = jnp.einsum('btsgh,bsghp->btghp', w, x_c)
        y = y + jnp.einsum('btgn,bghpn->btghp', c_c, state) * jnp.exp(acum)[..., None]
        to_end = jnp.exp(acum[:, -1:] - acum) * dt_c
        state = (state * jnp.exp(acum[:, -1])[..., None, None]
                 + jnp.einsum('bsgh,bsghp,bsgn->bghpn', to_end, x_c, b_c))
        return state, y

    state0 = jnp.zeros((bsz, g, hg, p, n), jnp.float32)
    _, ys = lax.scan(step, state0, (xc, dtc, bc, cc))
    return jnp.moveaxis(ys, 0, 1).reshape(bsz, s, h, p)

def ssm_mixer(z, xbc, dt_raw, conv_w, conv_b, dt_bias, a_log, d_skip, norm_w):
    bsz, s, _ = z.shape
    xbc = jax.nn.silu(causal_dwconv(xbc, conv_w, conv_b))
    xs, bm, cm = jnp.split(xbc, [SSM_D_INNER, SSM_D_INNER + SSM_GROUPS * SSM_D_STATE], axis=-1)
    xs = xs.reshape(bsz, s, SSM_HEADS, SSM_HEAD_DIM).astype(jnp.float32)
    bm = bm.reshape(bsz, s, SSM_GROUPS, SSM_D_STATE).astype(jnp.float32)
    cm = cm.reshape(bsz, s, SSM_GROUPS, SSM_D_STATE).astype(jnp.float32)
    dt = jax.nn.softplus(dt_raw.astype(jnp.float32) + dt_bias.astype(jnp.float32))
    a = -jnp.exp(a_log.astype(jnp.float32))
    y = ssd_chunked(xs, dt, a, bm, cm) + d_skip.astype(jnp.float32)[:, None] * xs
    y = y.reshape(bsz, s, SSM_D_INNER) * jax.nn.silu(z.astype(jnp.float32))
    yg = y.reshape(bsz, s, SSM_GROUPS, SSM_D_INNER // SSM_GROUPS)
    yg = yg * lax.rsqrt(jnp.mean(yg * yg, axis=-1, keepdims=True) + NORM_EPS)
    return (yg.reshape(bsz, s, SSM_D_INNER) * norm_w.astype(jnp.float32)).astype(z.dtype)

def stick_breaking_attention(qkv):
    bsz, s, _ = qkv.shape
    q, k, v = [jnp.moveaxis(t.reshape(bsz, s, SB_HEADS, SB_HEAD_DIM), 2, 1)
               for t in jnp.split(qkv, 3, axis=-1)]
    scale = SB_HEAD_DIM ** -0.5
    outs = []
    for i in range(s // SB_QBLK):
        q0 = i * SB_QBLK
        kl = q0 + SB_QBLK
        qb = q[:, :, q0:kl]
        zl = jnp.einsum('bhqd,bhkd->bhqk', qb, k[:, :, :kl]).astype(jnp.float32) * scale
        mask = jnp.arange(kl)[None, :] < (q0 + jnp.arange(SB_QBLK))[:, None]
        ls = jax.nn.log_sigmoid(zl)
        lk = jnp.where(mask, ls - zl, 0.0)
        later = lax.cumsum(lk, axis=3, reverse=True) - lk
        w = jnp.where(mask, jnp.exp(ls + later), 0.0)
        outs.append(jnp.einsum('bhqk,bhkd->bhqd', w.astype(v.dtype), v[:, :, :kl]))
    out = jnp.concatenate(outs, axis=2)
    return out.transpose(0, 2, 1, 3).reshape(bsz, s, SB_HEADS * SB_HEAD_DIM)

def compress_blocks(kraw, pos_emb, w1, w2):
    bsz, s, g, dh = kraw.shape
    chunks = kraw.reshape(bsz, s // CMP_STRIDE, CMP_STRIDE, g, dh)
    blocks = jnp.concatenate([chunks[:, :-1], chunks[:, 1:]], axis=2) + pos_emb[None, None, :, None, :].astype(kraw.dtype)
    blocks = blocks.transpose(0, 1, 3, 2, 4).reshape(bsz, s // CMP_STRIDE - 1, g, CMP_LEN * dh)
    return jax.nn.silu(blocks @ w1) @ w2

def nsa_attention(q, kv, gate, cmp_pos_k, cmp_w1_k, cmp_w2_k, cmp_pos_v, cmp_w1_v, cmp_w2_v):
    bsz, s, _ = q.shape
    g, hg, dh = NSA_KV_HEADS, NSA_Q_HEADS // NSA_KV_HEADS, NSA_HEAD_DIM
    q = q.reshape(bsz, s, g, hg, dh)
    k_cmp, v_cmp, k_sel, v_sel, k_win, v_win = [t.reshape(bsz, s, g, dh) for t in jnp.split(kv, 6, axis=-1)]
    gate = jax.nn.sigmoid(gate.astype(jnp.float32)).reshape(bsz, s, 3, g, hg)
    kc = compress_blocks(k_cmp, cmp_pos_k, cmp_w1_k, cmp_w2_k)
    vc = compress_blocks(v_cmp, cmp_pos_v, cmp_w1_v, cmp_w2_v)
    nc = kc.shape[1]
    cmp_end = jnp.arange(nc) * CMP_STRIDE + CMP_LEN - 1
    nb = s // SEL_BLOCK
    n_sel = min(N_SEL, nb)
    ratio = SEL_BLOCK // CMP_STRIDE
    ks_blk = k_sel.reshape(bsz, nb, SEL_BLOCK, g, dh).transpose(0, 3, 1, 2, 4)
    vs_blk = v_sel.reshape(bsz, nb, SEL_BLOCK, g, dh).transpose(0, 3, 1, 2, 4)
    kw = jnp.pad(k_win, ((0, 0), (WINDOW, 0), (0, 0), (0, 0)))
    vw = jnp.pad(v_win, ((0, 0), (WINDOW, 0), (0, 0), (0, 0)))
    slopes = alibi_slopes(NSA_Q_HEADS).reshape(g, hg)
    scale = dh ** -0.5
    bi = jnp.arange(bsz)[:, None, None, None]
    gi = jnp.arange(g)[None, :, None, None]
    blk_ids = jnp.arange(nb)

    def block(q0):
        qb = lax.dynamic_slice_in_dim(q, q0, NSA_QBLK, axis=1)
        gb = lax.dynamic_slice_in_dim(gate, q0, NSA_QBLK, axis=1)
        tpos = q0 + jnp.arange(NSA_QBLK)
        dist_c = tpos[:, None] - cmp_end[None, :]
        sc = (jnp.einsum('bqghd,bngd->bghqn', qb, kc).astype(jnp.float32) * scale
              - slopes[:, :, None, None] * dist_c.astype(jnp.float32))
        p_cmp = masked_softmax(sc, dist_c >= 0)
        o_cmp = jnp.einsum('bghqn,bngd->bqghd', p_cmp.astype(vc.dtype), vc)
        imp_pad = jnp.pad(p_cmp.sum(axis=2), ((0, 0), (0, 0), (0, 0), (1, 0)))
        imp = (imp_pad.reshape(bsz, g, NSA_QBLK, nb, ratio).sum(axis=-1)
               + jnp.pad(imp_pad[..., ratio::ratio], ((0, 0), (0, 0), (0, 0), (0, 1))))
        cur = tpos // SEL_BLOCK
        forced = ((blk_ids[None, :] == 0) | (blk_ids[None, :] == cur[:, None])
                  | (blk_ids[None, :] == cur[:, None] - 1))
        valid = blk_ids[None, :] * SEL_BLOCK <= tpos[:, None]
        imp = jnp.where(valid, jnp.where(forced, BIG, imp), NEG)
        _, idx = lax.top_k(imp, n_sel)
        ks = ks_blk[bi, gi, idx]
        vs = vs_blk[bi, gi, idx]
        pos = idx[..., None] * SEL_BLOCK + jnp.arange(SEL_BLOCK)
        dist_s = tpos[None, None, :, None, None] - pos
        ss = (jnp.einsum('bqghd,bgqnkd->bghqnk', qb, ks).astype(jnp.float32) * scale
              - slopes[None, :, :, None, None, None] * dist_s[:, :, None].astype(jnp.float32))
        ss = ss.reshape(bsz, g, hg, NSA_QBLK, n_sel * SEL_BLOCK)
        p_sel = masked_softmax(ss, (dist_s >= 0).reshape(bsz, g, 1, NSA_QBLK, n_sel * SEL_BLOCK))
        o_sel = jnp.einsum('bghqm,bgqmd->bqghd', p_sel.astype(vs.dtype),
                           vs.reshape(bsz, g, NSA_QBLK, n_sel * SEL_BLOCK, dh))
        kwb = lax.dynamic_slice_in_dim(kw, q0, WINDOW + NSA_QBLK, axis=1)
        vwb = lax.dynamic_slice_in_dim(vw, q0, WINDOW + NSA_QBLK, axis=1)
        wpos = q0 - WINDOW + jnp.arange(WINDOW + NSA_QBLK)
        dist_w = tpos[:, None] - wpos[None, :]
        wmask = (dist_w >= 0) & (dist_w < WINDOW) & (wpos[None, :] >= 0)
        sw = (jnp.einsum('bqghd,bkgd->bghqk', qb, kwb).astype(jnp.float32) * scale
              - slopes[:, :, None, None] * dist_w.astype(jnp.float32))
        o_win = jnp.einsum('bghqk,bkgd->bqghd', masked_softmax(sw, wmask).astype(vwb.dtype), vwb)
        out = (gb[:, :, 0, :, :, None] * o_cmp + gb[:, :, 1, :, :, None] * o_sel
               + gb[:, :, 2, :, :, None] * o_win)
        return out.astype(q.dtype)

    out = lax.map(block, jnp.arange(0, s, NSA_QBLK))
    return jnp.moveaxis(out, 0, 1).reshape(bsz, s, NSA_Q_HEADS * NSA_HEAD_DIM)

def first_inputs(seed: int = 0) -> dict:
    key = jax.random.key(seed)
    ks = iter(jax.random.split(key, 40))
    L = DEPTH
    f32 = jnp.float32

    def nrm(shape, scale):
        return jax.random.normal(next(ks), shape, f32) * scale

    def gain(shape):
        return 1.0 + nrm(shape, 0.02)

    dt0 = jnp.exp(jax.random.uniform(next(ks), (L, SSM_HEADS), f32)
                  * (math.log(0.1) - math.log(1e-3)) + math.log(1e-3))
    dt_bias = dt0 + jnp.log(-jnp.expm1(-dt0))
    a_log = jnp.log(jax.random.uniform(next(ks), (L, SSM_HEADS), f32, minval=1.0, maxval=16.0))
    return {
        "x": nrm((BATCH, SEQ, D_MODEL), 1.0),
        "pre_mix_norm": gain((L, D_MODEL)),
        "w_in": nrm((L, D_MODEL, D_IN), D_MODEL ** -0.5),
        "ssm_conv_w": nrm((L, SSM_CONV, SSM_CONV_DIM), SSM_CONV ** -0.5),
        "ssm_conv_b": nrm((L, SSM_CONV_DIM), 0.01),
        "ssm_dt_bias": dt_bias,
        "ssm_a_log": a_log,
        "ssm_d": 1.0 + nrm((L, SSM_HEADS), 0.1),
        "ssm_norm": gain((L, SSM_D_INNER)),
        "cmp_pos_k": nrm((L, CMP_LEN, NSA_HEAD_DIM), 0.02),
        "cmp_w1_k": nrm((L, CMP_LEN * NSA_HEAD_DIM, NSA_HEAD_DIM), (CMP_LEN * NSA_HEAD_DIM) ** -0.5),
        "cmp_w2_k": nrm((L, NSA_HEAD_DIM, NSA_HEAD_DIM), NSA_HEAD_DIM ** -0.5),
        "cmp_pos_v": nrm((L, CMP_LEN, NSA_HEAD_DIM), 0.02),
        "cmp_w1_v": nrm((L, CMP_LEN * NSA_HEAD_DIM, NSA_HEAD_DIM), (CMP_LEN * NSA_HEAD_DIM) ** -0.5),
        "cmp_w2_v": nrm((L, NSA_HEAD_DIM, NSA_HEAD_DIM), NSA_HEAD_DIM ** -0.5),
        "w_br_ssm": nrm((L, SSM_D_INNER, D_MODEL), SSM_D_INNER ** -0.5),
        "w_br_sb": nrm((L, SB_HEADS * SB_HEAD_DIM, D_MODEL), (SB_HEADS * SB_HEAD_DIM) ** -0.5),
        "w_br_nsa": nrm((L, NSA_Q_HEADS * NSA_HEAD_DIM, D_MODEL), (NSA_Q_HEADS * NSA_HEAD_DIM) ** -0.5),
        "w_out": nrm((L, D_MODEL, D_MODEL), D_MODEL ** -0.5),
        "post_mix_norm": gain((L, D_MODEL)),
        "pre_ffn_norm": gain((L, D_MODEL)),
        "ffn_w_up": nrm((L, D_MODEL, 2 * D_FF), D_MODEL ** -0.5),
        "ffn_conv_w": nrm((L, FFN_CONV, 2 * D_FF), FFN_CONV ** -0.5),
        "ffn_conv_b": nrm((L, 2 * D_FF), 0.01),
        "ffn_w_down": nrm((L, D_FF, D_MODEL), D_FF ** -0.5),
        "post_ffn_norm": gain((L, D_MODEL)),
    }

def first_block(x, pre_mix_norm, w_in, ssm_conv_w, ssm_conv_b, ssm_dt_bias, ssm_a_log, ssm_d, ssm_norm,
              cmp_pos_k, cmp_w1_k, cmp_w2_k, cmp_pos_v, cmp_w1_v, cmp_w2_v,
              w_br_ssm, w_br_sb, w_br_nsa, w_out, post_mix_norm, pre_ffn_norm,
              ffn_w_up, ffn_conv_w, ffn_conv_b, ffn_w_down, post_ffn_norm):
    bsz, s, _ = x.shape
    for l in range(DEPTH):
        h = rms_norm(x, pre_mix_norm[l])
        proj = h @ w_in[l]
        z, xbc, dt_raw, sb_qkv, nsa_q, nsa_kv, nsa_gate, merge_gate = jnp.split(proj, split_points(), axis=-1)
        y_ssm = ssm_mixer(z, xbc, dt_raw, ssm_conv_w[l], ssm_conv_b[l], ssm_dt_bias[l],
                          ssm_a_log[l], ssm_d[l], ssm_norm[l])
        y_sb = stick_breaking_attention(sb_qkv)
        y_nsa = nsa_attention(nsa_q, nsa_kv, nsa_gate, cmp_pos_k[l], cmp_w1_k[l], cmp_w2_k[l],
                              cmp_pos_v[l], cmp_w1_v[l], cmp_w2_v[l])
        gm = jax.nn.sigmoid(merge_gate.astype(jnp.float32)).reshape(bsz, s, 3, D_MODEL)
        mixed = (gm[:, :, 0] * (y_ssm @ w_br_ssm[l]) + gm[:, :, 1] * (y_sb @ w_br_sb[l])
                 + gm[:, :, 2] * (y_nsa @ w_br_nsa[l])).astype(x.dtype)
        x = x + rms_norm(mixed @ w_out[l], post_mix_norm[l])
        h = rms_norm(x, pre_ffn_norm[l])
        u = causal_dwconv(h @ ffn_w_up[l], ffn_conv_w[l], ffn_conv_b[l])
        gate, val = jnp.split(u, 2, axis=-1)
        f = (jax.nn.gelu(gate, approximate=True) * val) @ ffn_w_down[l]
        x = x + rms_norm(f, post_ffn_norm[l])
    return x


DIFF_HEADS = 4
DIFF_HEAD_DIM = 64
DIFF_WIDTH = DIFF_HEADS * 2 * DIFF_HEAD_DIM
FOX_HEADS = 8
FOX_HEAD_DIM = 64
FOX_WIDTH = FOX_HEADS * FOX_HEAD_DIM
MIX_WIDTH = DIFF_WIDTH + FOX_WIDTH
IN_COLS = 3 * DIFF_WIDTH + 3 * FOX_WIDTH + FOX_HEADS
D_FF_2 = 4 * D_MODEL
N_BUCKETS = 32
MAX_DISTANCE = 128
Q_BLOCK = 128
EPS = 1e-6
NEG_2 = -1e30


def rmsnorm(x, g):
    xf = x.astype(jnp.float32)
    y = xf * lax.rsqrt(jnp.mean(xf * xf, axis=-1, keepdims=True) + EPS)
    return (y * g.astype(jnp.float32)).astype(x.dtype)

def t5_bucket(dist):
    max_exact = N_BUCKETS // 2
    d = jnp.maximum(dist, 1).astype(jnp.float32)
    large = max_exact + (jnp.log(d / max_exact) / math.log(MAX_DISTANCE / max_exact)
                         * (N_BUCKETS - max_exact))
    large = jnp.minimum(large.astype(jnp.int32), N_BUCKETS - 1)
    return jnp.where(dist < max_exact, dist, large)

def token_mixer(h, w_in, b_f, lam_q1, lam_k1, lam_q2, lam_k2, subln_g, rel_bias, lambda_init):
    B, S, _ = h.shape
    proj = h @ w_in
    o = 0
    dq = proj[..., o:o + DIFF_WIDTH].reshape(B, S, 2 * DIFF_HEADS, DIFF_HEAD_DIM); o += DIFF_WIDTH
    dk = proj[..., o:o + DIFF_WIDTH].reshape(B, S, 2 * DIFF_HEADS, DIFF_HEAD_DIM); o += DIFF_WIDTH
    dv = proj[..., o:o + DIFF_WIDTH].reshape(B, S, DIFF_HEADS, 2 * DIFF_HEAD_DIM); o += DIFF_WIDTH
    fq = proj[..., o:o + FOX_WIDTH].reshape(B, S, FOX_HEADS, FOX_HEAD_DIM); o += FOX_WIDTH
    fk = proj[..., o:o + FOX_WIDTH].reshape(B, S, FOX_HEADS, FOX_HEAD_DIM); o += FOX_WIDTH
    fv = proj[..., o:o + FOX_WIDTH].reshape(B, S, FOX_HEADS, FOX_HEAD_DIM); o += FOX_WIDTH
    f_logit = proj[..., o:o + FOX_HEADS].astype(jnp.float32) + b_f.astype(jnp.float32)
    cum = jnp.cumsum(jax.nn.log_sigmoid(f_logit), axis=1)
    cum_k = jnp.transpose(cum, (0, 2, 1))

    lam = (jnp.exp(jnp.sum(lam_q1.astype(jnp.float32) * lam_k1.astype(jnp.float32)))
           - jnp.exp(jnp.sum(lam_q2.astype(jnp.float32) * lam_k2.astype(jnp.float32)))
           + lambda_init)

    dist_bias = rel_bias[t5_bucket(jnp.arange(S))]
    kpos = jnp.arange(S)
    nb = S // Q_BLOCK

    def to_blocks(a):
        return jnp.swapaxes(a.reshape(B, nb, Q_BLOCK, *a.shape[2:]), 0, 1)

    def block(args):
        i, qd, qf, cq = args
        qpos = i * Q_BLOCK + jnp.arange(Q_BLOCK)
        rel = qpos[:, None] - kpos[None, :]
        causal = rel >= 0
        sd = jnp.einsum('bqhd,bkhd->bhqk', qd, dk).astype(jnp.float32) * (DIFF_HEAD_DIM ** -0.5)
        bias = jnp.transpose(dist_bias[jnp.maximum(rel, 0)], (2, 0, 1)).astype(jnp.float32)
        sd = sd.reshape(B, DIFF_HEADS, 2, Q_BLOCK, S) + bias[:, None]
        pd = jax.nn.softmax(jnp.where(causal, sd, NEG_2), axis=-1)
        ad = pd[:, :, 0] - lam * pd[:, :, 1]
        od = jnp.einsum('bhqk,bkhe->bqhe', ad.astype(dv.dtype), dv)
        od = rmsnorm(od, subln_g) * (1.0 - lambda_init)
        sf = jnp.einsum('bqhd,bkhd->bhqk', qf, fk).astype(jnp.float32) * (FOX_HEAD_DIM ** -0.5)
        sf = sf + jnp.transpose(cq, (0, 2, 1))[..., :, None] - cum_k[..., None, :]
        pf = jax.nn.softmax(jnp.where(causal, sf, NEG_2), axis=-1)
        of = jnp.einsum('bhqk,bkhd->bqhd', pf.astype(fv.dtype), fv)
        return jnp.concatenate([od.reshape(B, Q_BLOCK, DIFF_WIDTH),
                                of.reshape(B, Q_BLOCK, FOX_WIDTH)], axis=-1)

    out = lax.map(block, (jnp.arange(nb), to_blocks(dq), to_blocks(fq), to_blocks(cum)))
    return jnp.swapaxes(out, 0, 1).reshape(B, S, MIX_WIDTH)

def second_inputs(seed: int = 0) -> dict:
    key = jax.random.key(seed)
    ks = jax.random.split(key, 20)
    f32 = jnp.float32
    nrm = lambda k, shape, s: jax.random.normal(k, shape, f32) * s
    return {
        "x": jax.random.normal(ks[0], (BATCH, SEQ, D_MODEL), f32),
        "ln_attn_pre": 1.0 + nrm(ks[1], (DEPTH, D_MODEL), 0.05),
        "w_in": nrm(ks[2], (DEPTH, D_MODEL, IN_COLS), D_MODEL ** -0.5),
        "b_f": 2.0 + nrm(ks[3], (DEPTH, FOX_HEADS), 0.1),
        "lam_q1": nrm(ks[4], (DEPTH, DIFF_HEAD_DIM), 0.1),
        "lam_k1": nrm(ks[5], (DEPTH, DIFF_HEAD_DIM), 0.1),
        "lam_q2": nrm(ks[6], (DEPTH, DIFF_HEAD_DIM), 0.1),
        "lam_k2": nrm(ks[7], (DEPTH, DIFF_HEAD_DIM), 0.1),
        "subln_g": 1.0 + nrm(ks[8], (DEPTH, 2 * DIFF_HEAD_DIM), 0.05),
        "rel_bias": nrm(ks[9], (N_BUCKETS, DIFF_HEADS), 0.5),
        "w_out": nrm(ks[10], (DEPTH, MIX_WIDTH, D_MODEL), MIX_WIDTH ** -0.5),
        "ln_attn_post": 1.0 + nrm(ks[11], (DEPTH, D_MODEL), 0.05),
        "ln_mlp_pre": 1.0 + nrm(ks[12], (DEPTH, D_MODEL), 0.05),
        "w_up": nrm(ks[13], (DEPTH, D_MODEL, D_FF_2), D_MODEL ** -0.5),
        "w_down": nrm(ks[14], (DEPTH, D_FF_2, D_MODEL), D_FF_2 ** -0.5),
        "ln_mlp_post": 1.0 + nrm(ks[15], (DEPTH, D_MODEL), 0.05),
    }

def second_block(x, ln_attn_pre, w_in, b_f, lam_q1, lam_k1, lam_q2, lam_k2, subln_g, rel_bias,
              w_out, ln_attn_post, ln_mlp_pre, w_up, w_down, ln_mlp_post):
    for l in range(DEPTH):
        lambda_init = 0.8 - 0.6 * math.exp(-0.3 * l)
        h = rmsnorm(x, ln_attn_pre[l])
        mix = token_mixer(h, w_in[l], b_f[l], lam_q1[l], lam_k1[l], lam_q2[l], lam_k2[l],
                          subln_g[l], rel_bias, lambda_init)
        x = x + rmsnorm(mix @ w_out[l], ln_attn_post[l])
        h = rmsnorm(x, ln_mlp_pre[l])
        u = jnp.square(jax.nn.relu(h @ w_up[l]))
        x = x + rmsnorm(u @ w_down[l], ln_mlp_post[l])
    return x


def setup_inputs(seed=0):
    out = dict(first_inputs(seed))
    for name, value in second_inputs(seed + 1).items():
        if name != "x":
            out[name + "_2"] = value
    return out


def reference(
    x, pre_mix_norm, w_in, ssm_conv_w, ssm_conv_b, ssm_dt_bias, ssm_a_log, ssm_d, ssm_norm,
    cmp_pos_k, cmp_w1_k, cmp_w2_k, cmp_pos_v, cmp_w1_v, cmp_w2_v, w_br_ssm, w_br_sb, w_br_nsa,
    w_out, post_mix_norm, pre_ffn_norm, ffn_w_up, ffn_conv_w, ffn_conv_b, ffn_w_down,
    post_ffn_norm, ln_attn_pre_2, w_in_2, b_f_2, lam_q1_2, lam_k1_2, lam_q2_2, lam_k2_2,
    subln_g_2, rel_bias_2, w_out_2, ln_attn_post_2, ln_mlp_pre_2, w_up_2, w_down_2,
    ln_mlp_post_2,
):
    x = first_block(
        x, pre_mix_norm, w_in, ssm_conv_w, ssm_conv_b, ssm_dt_bias, ssm_a_log, ssm_d, ssm_norm,
        cmp_pos_k, cmp_w1_k, cmp_w2_k, cmp_pos_v, cmp_w1_v, cmp_w2_v, w_br_ssm, w_br_sb,
        w_br_nsa, w_out, post_mix_norm, pre_ffn_norm, ffn_w_up, ffn_conv_w, ffn_conv_b,
        ffn_w_down, post_ffn_norm,
    )
    return second_block(
        x, ln_attn_pre_2, w_in_2, b_f_2, lam_q1_2, lam_k1_2, lam_q2_2, lam_k2_2, subln_g_2,
        rel_bias_2, w_out_2, ln_attn_post_2, ln_mlp_pre_2, w_up_2, w_down_2, ln_mlp_post_2,
    )


_drawn_inputs = setup_inputs


def setup_inputs(seed=0):
    import zlib

    import numpy as np

    out = dict(_drawn_inputs(seed))
    spreads = {}
    factors = {'ssm_conv_b': 4.544,
     'ssm_norm': 3.914,
     'cmp_pos_k': 64.0,
     'cmp_pos_v': 30.805,
     'post_mix_norm': 2.853,
     'pre_ffn_norm': 3.006,
     'ffn_conv_b': 13.972,
     'post_ffn_norm': 13.892,
     'b_f_2': 44.312,
     'lam_q1_2': 200.0,
     'lam_k1_2': 3.288,
     'lam_q2_2': 22.4,
     'cmp_w1_k': 3.688,
     'cmp_w2_k': 3.757,
     'ln_attn_pre_2': 3.599,
     'lam_k2_2': 8.0,
     'subln_g_2': 23.929,
     'ln_attn_post_2': 15.787,
     'ln_mlp_pre_2': 5.159,
     'ln_mlp_post_2': 18.785}
    for name, (base, spread) in spreads.items():
        noise = np.random.default_rng([zlib.crc32(name.encode()), seed]).standard_normal(out[name].shape)
        drawn = base * np.exp(spread * noise) if base else spread * noise
        out[name] = __import__('jax').numpy.asarray(drawn.astype(out[name].dtype))
    for name, factor in factors.items():
        out[name] = (out[name] * factor).astype(out[name].dtype)
    return out
```

```python
import math
from contextlib import ExitStack

import numpy as np

import concourse.bass as bass
from concourse import mybir

F32 = mybir.dt.float32
F32R = mybir.dt.float32r
ALU = mybir.AluOpType
ACT = mybir.ActivationFunctionType
AX = mybir.AxisListType

T, D, P = 256, 1024, 128
KC = D // P
UNIT = 2048
NEG = -1e30
EPS = 1e-6
SSM_H, SB_H, NSA_H, CMP_N = 16, 4, 8, 15
FF1, FF2 = 2816, 4096
UP1, DOWN1 = FF1 // P, FF1 // (2 * P)
UP2, DOWN2 = FF2 // (2 * P), FF2 // (2 * P)
SLOTS = 3
LAMBDA_INIT = 0.8 - 0.6 * math.exp(0.0)
SLOPES = [2.0 ** (-8.0 * (h + 1) / NSA_H) for h in range(NSA_H)]

UNITS = ([("sbq", i) for i in range(2)] + [("sbk", i) for i in range(2)] + [("sbv", i) for i in range(2)]
         + [("xbc", i) for i in range(8)] + [("kk", 0), ("kv", 0), ("vv", 0), ("nq", 0), ("nq", 1)]
         + [("z", i) for i in range(4)] + [("gm", i) for i in range(12)] + [("br", i) for i in range(8)]
         + [("wo", i) for i in range(4)])
U_FFN1 = len(UNITS)
U_FFN1_END = U_FFN1 + UP1 + DOWN1
UNITS2 = ([("dq", i) for i in range(2)] + [("dk", i) for i in range(2)] + [("dv", i) for i in range(2)]
          + [("fq", i) for i in range(2)] + [("fk", i) for i in range(2)] + [("fv", i) for i in range(2)]
          + [("wo2", i) for i in range(4)])
U_FFN2 = U_FFN1_END + len(UNITS2)
N_UNITS = U_FFN2 + UP2 + DOWN2
UIDX = {name: i for i, name in enumerate(UNITS)}
UIDX.update({name: U_FFN1_END + i for i, name in enumerate(UNITS2)})

BANK, _uses = {}, [0, 0, 0]
for _n, _name in enumerate(UNITS):
    BANK[_name] = (_n % 3, _uses[_n % 3])
    _uses[_n % 3] += 1
FFN1_BANK0 = list(_uses)
_uses[0] += UP1 // 2
_uses[1] += UP1 // 2
for _n, _name in enumerate(UNITS2):
    BANK[_name] = (_n % 3, _uses[_n % 3])
    _uses[_n % 3] += 1
FFN2_BANK0 = list(_uses)

PCOLS, PW = {}, 0
for _name, _w in (("g_mix1", 8), ("g_postmix1", 8), ("g_ffn1", 8), ("g_postffn1", 8), ("g_mix2", 8),
                  ("g_postmix2", 8), ("g_ffn2", 8), ("g_postffn2", 8), ("cw", 64), ("cb", 16), ("ssm_norm", 8),
                  ("dt_bias", 16), ("a_log", 16), ("ssm_d", 16), ("fw", 132), ("fb", 44), ("pos", 32),
                  ("w2", 128), ("subln", 1), ("lam", 256), ("b_f", 8), ("rel", 4), ("ws1", 320), ("ws2", 64)):
    PCOLS[_name] = (PW, _w)
    PW += _w

CCOLS, CW = {}, 0
for _name, _w in (("ident", 128), ("le", 128), ("ones", 128), ("gt", 128), ("sbmask", 384), ("cbmask", 384),
                  ("causal", 384), ("alibi", 384), ("cmpbias", 256), ("rowvalid", 2), ("cmpmask", 8),
                  ("onehot", 384)):
    CCOLS[_name] = (CW, _w)
    CW += _w


def constants():
    c = np.zeros((P, CW), np.float32)
    p, i = np.arange(P)[:, None], np.arange(P)[None, :]

    def put(name, a):
        o, w = CCOLS[name]
        c[:a.shape[0], o:o + w] = a

    le, gt, lt = p <= i, p > i, p < i
    one = np.ones((P, P))
    put("ident", p == i)
    put("le", le)
    put("ones", one)
    put("gt", gt)
    put("sbmask", np.hstack([lt, one, lt]))
    put("cbmask", np.hstack([le, one, le]))
    dist = np.hstack([p - i, P + p - np.arange(T)[None, :]]).astype(np.float64)
    put("causal", np.where(dist >= 0, 0.0, NEG))
    put("alibi", np.where(dist >= 0, -dist, NEG))
    cmp_bias = np.full((P, 2, 2, 4, 16), NEG)
    for tb in range(2):
        for hb in range(2):
            for j in range(4):
                for n in range(CMP_N):
                    d = tb * P + np.arange(P) - (16 * n + 31)
                    cmp_bias[:, tb, hb, j, n] = np.where(d >= 0, -SLOPES[hb * 4 + j] * d, NEG)
    put("cmpbias", cmp_bias.reshape(P, -1))
    put("rowvalid", np.hstack([p >= 31, p >= 0]))
    mask = np.zeros((P, 4, 2))
    for q in range(P):
        mask[q, (q // 16) % 4, q // 64] = 1.0
    put("cmpmask", mask.reshape(P, 8))
    hot = np.zeros((33, 384))
    for m in range(383):
        d = 255 - m
        if d < 0:
            hot[32, m] = 1.0
        elif d < 16:
            hot[d, m] = 1.0
        else:
            hot[min(16 + int(math.log(d / 16) / math.log(8) * 16), 31), m] = 1.0
    put("onehot", hot)
    return c


def program(nc, stream, params, consts, cmpw, x_in, out):
    ctx = ExitStack()
    with ctx:
        sems = {}

        def S(name):
            if name not in sems:
                sems[name] = ctx.enter_context(nc.semaphore(name))
            return sems[name]

        def sb(name, shape, dt=F32):
            return ctx.enter_context(nc.sbuf_tensor(name, shape, dt))

        def pb(name, shape):
            return ctx.enter_context(nc.psum_tensor(name, shape, F32))

        w_raw = sb("w_raw", [P, SLOTS, UNIT])
        w_hi = sb("w_hi", [P, SLOTS, UNIT], F32R)
        w_lo = sb("w_lo", [P, SLOTS, UNIT], F32R)
        a_hi = sb("a_hi", [P, 24, T], F32R)
        a_lo = sb("a_lo", [P, 24, T], F32R)
        xT = sb("xT", [P, KC, T])
        prm = sb("prm", [P, PW])
        cst = sb("cst", [P, CW])
        area = sb("area", [P, 58 * 256])
        tiny = sb("tiny", [P, 1024])
        ws_hi = a_hi[:, 22:24, :].rearrange("p a b -> p (a b)")[:, 0:320]
        ws_lo = a_lo[:, 22:24, :].rearrange("p a b -> p (a b)")[:, 0:320]
        rbc = sb("rbc", [P, T])
        scratch = nc.dram_tensor("t5_rows", (4, P, 384), F32, kind="Internal").ap()

        pj = [pb(f"pj{i}", [P, 512]) for i in range(3)]
        ps = pb("ps", [P, 2, 512])
        pt = pb("pt", [P, 2, 512])
        po = pb("po", [P, 512])

        def V(kib, *dims):
            n = int(np.prod(dims))
            o = int(kib * 256)
            ap = area[:, o:o + n]
            if len(dims) == 1:
                return ap
            names = "abcd"[:len(dims)]
            return ap.rearrange(f"p ({' '.join(names)}) -> p {' '.join(names)}",
                                **dict(zip(names[1:], dims[1:])))

        _t = [0]

        def small(*dims):
            n = int(np.prod(dims))
            ap = tiny[:, _t[0]:_t[0] + n]
            _t[0] += n
            if len(dims) == 1:
                return ap
            names = "abcd"[:len(dims)]
            return ap.rearrange(f"p ({' '.join(names)}) -> p {' '.join(names)}",
                                **dict(zip(names[1:], dims[1:])))

        def prm_(name):
            o, w = PCOLS[name]
            return prm[:, o:o + w]

        def cst_(name):
            o, w = CCOLS[name]
            return cst[:, o:o + w]

        ident, ones, gt, le = cst_("ident"), cst_("ones"), cst_("gt"), cst_("le")
        o_le = CCOLS["le"][0]
        le_ones = cst[:, o_le:o_le + 256]
        ones_gt = cst[:, o_le + 128:o_le + 384]

        x_tok, sq = V(0, 2, D), V(8, KC, T)
        sbq, sbk, sbv = V(0, 4, T), V(4, 4, T), V(8, 2, 512)
        sb_l = [V(12, 2, 384), V(24, 2, 384)]
        sb_ls = [V(15, 2, 384), V(27, 2, 384)]
        sb_lk = [V(18, 2, 384), V(30, 2, 384)]
        sb_w = [V(21, 2, 384), V(33, 2, 384)]
        xbc = V(36, 16, T)
        xc = [V(52, 2, T), V(54, 2, T)]
        xs_tok, xdt = V(0, 2, D), V(8, 2, D)
        gdt, E = V(16, 2, 4, P), V(20, 4, 384)
        cmp_w1 = V(26, 2, 16, 64)
        nq, cb = V(34, 4, T), V(38, 4, 384)
        kk, cm, vv = V(52, 2, T), V(54, 2, T), V(56, 2, T)
        ck, ckp = V(44, 2, 2, P), V(46, 2, 2, 2 * P)
        z = V(8, 2, D)
        vc, pct, cmp_e, y_sq = V(46, 4, P), V(48, T), V(49, 2, P), V(50, T)
        sm = [V(16, 2, 384), V(19, 2, 384)]
        pr = [V(22, 2, 384), V(25, 2, 384)]
        ptr = [V(28, 2, 384), V(31, 2, 384)]
        gm_at = list(range(38, 46)) + list(range(8, 16)) + list(range(0, 8))
        gm = [V(k, T) for k in gm_at]
        mixt = [V(16, 3, T), V(19, 3, T)]
        yT, sqy = V(20, KC, T), V(28, KC, T)
        sq_ffn = V(36, KC, T)
        fx, facc, fg, fu = V(0, 2, T), V(4, 2, T), V(8, T), V(10, 2, T)
        upd = [V(16, T), V(17, T)]
        dq, dk, dv = V(0, 4, T), V(4, 4, T), V(8, 2, 512)
        fq, fk, fv = V(12, 4, T), V(16, 4, T), V(20, 2, 512)
        t5 = V(24, 4, 384)
        sm2 = [V(30, 2, 384), V(33, 2, 384)]
        pr2 = [V(36, 2, 384), V(39, 2, 384)]
        ptr2 = [V(42, 2, 384), V(45, 2, 384)]
        od, odsq, dg8, odn = V(48, 4, T), V(0, 4, T), V(4, 8, P), V(0, 4, T)
        lfle = [V(52, 2, 2, P), V(54, 2, 2, P)]
        t5_sb = V(56, 384)
        y_tok = x_tok

        rt, rcol, eps_t = small(2), small(2), small(1)
        dgr = sb("dgr", [P, 2, P])
        small40 = small(2, 40)
        dtx, dt_, dta = small(2, 16), small(2, 16), small(2, 16)
        dt_e, ea = small(2, 16), small(16)
        gate = small(2, 24)
        ssy, ry = small(2, 4), small(2, 4)
        hid, hid_t = small(2, 32), small(2, 64)
        hrep = small(P)
        kct = small(16)
        vrep = small(64)
        cmx, csm, crc = small(16), small(16), small(16)
        mx = [small(4), small(4)]
        sums = [small(4), small(4)]
        rcp = [small(4), small(4)]
        lamt = small(128)
        lamv, lm = small(8), small(4)
        lf, lf_e, fl = small(2, 8), small(2, 8), small(2, 8)
        ods = small(8)
        assert _t[0] <= 1024

        class Order:

            def __init__(self, eng, name):
                self.eng, self.sem, self.n = eng, S(name), 0

            def did(self, ins):
                ins.then_inc(self.sem, 1)
                self.n = self.n + 1

            def sync(self):
                self.eng.wait_ge(self.sem, self.n)

        S_USE = ["x", "sb0", "sb1", "xs", "cb", "seg0", "seg1", "seg2", "seg3", "cmp", "yt"] \
            + [f"n{r}" for r in range(8)] + [f"d{r}" for r in range(4)] \
            + [f"f{r}" for r in range(4)] + ["odn"]
        T_USE = ["x", "sb0", "sb1", "xs", "cb", "seg0", "seg1", "seg2", "seg3", "cmp", "yt"] \
            + [f"n{r}" for r in range(8)] + [f"d{r}" for r in range(4)] + [f"f{r}" for r in range(4)]
        O_USE = ["norm0", "rbc0", "sb0", "sb1", "dt", "y0", "y1", "y2", "y3", "hid", "kc"] \
            + [f"n{j}" for j in range(4)] + ["norm1", "rbc1", "norm2", "rbc2", "norm3", "rbc3", "norm4", "rbc4",
               "flog", "t5", "d0", "d1", "odn", "f0", "f1", "f2", "f3", "norm5", "rbc5", "norm6", "rbc6",
               "norm7", "rbc7"]
        USE = {"S": S_USE, "T": T_USE, "O": O_USE}

        def claim(pe, region, name):
            k = USE[region].index(name)
            if k:
                pe.wait_ge(S(f"{region}_read"), k)

        def written(ins, region):
            ins.then_inc(S(f"{region}_written"), 1)

        def await_psum(eng, region, name):
            eng.wait_ge(S(f"{region}_written"), USE[region].index(name) + 1)

        def read(ins, region):
            ins.then_inc(S(f"{region}_read"), 1)

        def await_read(eng, region, name):
            eng.wait_ge(S(f"{region}_read"), USE[region].index(name) + 1)

        def await_value(eng, name):
            b, n = BANK[name]
            eng.wait_ge(S(f"pj_read{b}"), n + 1)

        block = ctx.enter_context(nc.Block())

        @block.sync
        def _(sp):
            sp.dma_start(x_tok, x_in.rearrange("b (tb p) d -> (b p) tb d", p=P)).then_inc(S("x_loaded"), 16)
            sp.dma_start(cst[:, :], consts).then_inc(S("cst_loaded"), 16)
            sp.dma_start(prm[:, :], params).then_inc(S("prm_loaded"), 16)
            for r in range(SLOTS):
                sp.dma_start(w_raw[:, r, :], stream[r]).then_inc(S(f"w_loaded{r}"), 16)
            rounds = N_UNITS // SLOTS
            with sp.Fori(1, rounds) as i:
                for r in range(SLOTS):
                    sp.wait_ge(S("w_hi_done"), i * SLOTS + (r - SLOTS + 1))
                    sp.wait_ge(S("w_lo_done"), i * SLOTS + (r - SLOTS + 1))
                    sp.dma_start(w_raw[:, r, :], stream[bass.ds(i * SLOTS + r, 1), :, :].rearrange("a p n -> (a p) n"))\
                      .then_inc(S(f"w_loaded{r}"), 16)
            for u in range(rounds * SLOTS, N_UNITS):
                sp.wait_ge(S("w_hi_done"), u - SLOTS + 1)
                sp.wait_ge(S("w_lo_done"), u - SLOTS + 1)
                sp.dma_start(w_raw[:, u % SLOTS, :], stream[u]).then_inc(S(f"w_loaded{u % SLOTS}"), 16)
            sp.wait_ge(S("out_ready"), 4)
            sp.dma_start(out.rearrange("b (tb p) d -> (b p) tb d", p=P), x_tok).then_inc(S("out_stored"), 16)
            sp.wait_ge(S("out_stored"), 16)

        @block.gpsimd
        def _(gp):
            await_psum(gp, "O", "sb1")
            gp.dma_start(cmp_w1, cmpw.rearrange("v p c e -> p v c e")).then_inc(S("cmpw_loaded"), 16)
            gp.wait_ge(S("xs_tok_ready"), 4)
            gp.tensor_tensor(xs_tok.rearrange("p t (h c) -> p t h c", h=SSM_H),
                             xs_tok.rearrange("p t (h c) -> p t h c", h=SSM_H),
                             prm_("ssm_d").unsqueeze(1).unsqueeze(3).to_broadcast([P, 2, SSM_H, 64]),
                             ALU.mult).then_inc(S("xd_ready"), 1)
            for g in range(4):
                if g == 0:
                    gp.wait_ge(S("dta_ready"), 1)
                else:
                    gp.wait_ge(S("T_written"), USE["T"].index(f"seg{g - 1}") + 1)
                gp.tensor_tensor(gdt, gt.unsqueeze(1).unsqueeze(1).to_broadcast([P, 2, 4, P]),
                                 dta[:, :, 4 * g:4 * g + 4].unsqueeze(3).to_broadcast([P, 2, 4, P]),
                                 ALU.mult).then_inc(S("gdt_ready"), 1)
            await_read(gp, "O", "t5")
            gp.dma_start(scratch, t5_sb[0:4, :].unsqueeze(1).to_broadcast([4, P, 384])).then_inc(S("t5_scratch"), 16)
            gp.wait_ge(S("t5_scratch"), 16)
            for h in range(4):
                gp.dma_start(t5[:, h, 128:384], bass.AP(scratch.tensor, h * P * 384 + 127, [[383, P], [1, 256]]))\
                  .then_inc(S("t5_ready"), 16)
                gp.dma_start(t5[:, h, 0:128], bass.AP(scratch.tensor, h * P * 384 + 255, [[383, P], [1, 128]]))\
                  .then_inc(S("t5_ready"), 16)
            for j in range(4):
                if j == 0:
                    gp.wait_ge(S("lf_ready"), 1)
                elif j >= 2:
                    gp.wait_ge(S("S_written"), USE["S"].index(f"f{j - 2}") + 1)
                gp.tensor_tensor(lfle[j % 2], le.unsqueeze(1).unsqueeze(1).to_broadcast([P, 2, 2, P]),
                                 lf[:, :, 2 * j:2 * j + 2].unsqueeze(3).to_broadcast([P, 2, 2, P]),
                                 ALU.mult).then_inc(S("lfle_ready"), 1)

        @block.tensor
        def _(pe):
            def unit_ready(u):
                pe.wait_ge(S("w_hi_done"), u + 1)
                pe.wait_ge(S("w_lo_done"), u + 1)

            def bank_free(b, n):
                if isinstance(n, int) and n == 0:
                    return
                pe.wait_ge(S(f"pj_read{b}"), n)

            def three(out_, wh, wl, ah, al, first, last, weights_left=True):
                a, b = ((wh, ah), (wl, al)) if weights_left else ((ah, wh), (al, wl))
                pe.matmul(out_, a[0], a[1], start=first, stop=False)
                if weights_left:
                    pe.matmul(out_, wh, al, start=False, stop=False)
                    return pe.matmul(out_, wl, ah, start=False, stop=last)
                pe.matmul(out_, ah, wl, start=False, stop=False)
                return pe.matmul(out_, al, wh, start=False, stop=last)

            def unit_b(slot, b, koff=0, gate=None):
                for nb in range(2):
                    for k in range(KC):
                        if gate and nb == 0:
                            gate(k)
                        c = k * 256 + nb * P
                        mm = three(pj[b][:, nb * T:(nb + 1) * T], w_hi[:, slot, c:c + P], w_lo[:, slot, c:c + P],
                                   a_hi[:, koff + k, :], a_lo[:, koff + k, :], k == 0, k == KC - 1)
                mm.then_inc(S("unit_done"), 1)

            def unit_a(slot, b):
                for tb in range(2):
                    for k in range(KC):
                        c = k * 256
                        mm = three(pj[b][:, tb * 256:(tb + 1) * 256], w_hi[:, slot, c:c + 256],
                                   w_lo[:, slot, c:c + 256], a_hi[:, k, tb * P:(tb + 1) * P],
                                   a_lo[:, k, tb * P:(tb + 1) * P], k == 0, k == KC - 1, weights_left=False)
                mm.then_inc(S("unit_done"), 1)

            def run_unit(name, gate=None):
                u = UIDX[name]
                b, n = BANK[name]
                unit_ready(u)
                bank_free(b, n)
                if name[0] in ("sbv", "vv", "z", "dv", "fv"):
                    unit_a(u % SLOTS, b)
                else:
                    unit_b(u % SLOTS, b, 8 if name[0] == "wo2" else 0, gate)

            def transpose(out_, in_):
                return pe.transpose(out_, in_, ident[0:in_.shape[0], 0:in_.shape[0]])

            def stats(n, sq_t):
                claim(pe, "O", f"norm{n}")
                pe.wait_ge(S("sq_ready"), KC * (n + 1))
                for tb in range(2):
                    for k in range(KC):
                        mm = pe.matmul(po[:, tb:tb + 1], sq_t[:, k, tb * P:(tb + 1) * P], ones[:, 0:1],
                                       start=(k == 0), stop=(k == KC - 1))
                written(mm, "O")
                claim(pe, "O", f"rbc{n}")
                pe.wait_ge(S("diag_ready"), n + 1)
                written(pe.matmul(po[:, 256:512], ones, dgr[:, :, :], start=True, stop=True), "O")

            def operand_gate(n):
                def gate(k):
                    pe.wait_ge(S("opnd_hi"), KC * n + k + 1)
                    pe.wait_ge(S("opnd_lo"), KC * n + k + 1)
                return gate

            pe.wait_ge(S("x_loaded"), 16)
            pe.wait_ge(S("cst_loaded"), 16)
            claim(pe, "S", "x")
            for k in range(KC):
                bank = (ps, pt)[k // 4][:, (k // 2) % 2, :]
                for tb in range(2):
                    o = (k % 2) * T + tb * P
                    mm = transpose(bank[:, o:o + P], x_tok[:, tb, k * P:(k + 1) * P])
                if k == 3:
                    written(mm, "S")
            written(mm, "T")

            def scores(q, kT_, o, kpart=slice(0, P)):
                pe.matmul(o[:, 0:128], q[:, 0:P], kT_[:, 0:P], start=True, stop=True)
                return pe.matmul(o[:, 128:384], q[:, P:T], kT_[:, 0:T], start=True, stop=True)

            def turn(src, region_bank):
                transpose(region_bank[:, 0:128], src[:, 0:128])
                transpose(region_bank[:, 128:256], src[:, 128:256])
                return transpose(region_bank[:, 256:384], src[:, 256:384])

            def weigh(o, v0, v1, p, first=True, last=True):
                pe.matmul(o, v0, p[:, 0:256], start=first, stop=last, skip_group_check=True)
                return pe.matmul(o[:, 128:256], v1, p[:, 256:384], start=False, stop=last, skip_group_check=True)

            def sb_scores(p):
                claim(pe, "S", f"sb{p}")
                for hh in range(2):
                    h = 2 * p + hh
                    pe.matmul(ps[:, hh, 0:256], sbk[:, h, 0:P], sbq[:, h, :], start=True, stop=True)
                    mm = pe.matmul(ps[:, hh, 256:384], sbk[:, h, P:T], sbq[:, h, P:T], start=True, stop=True)
                written(mm, "S")

            def sb_later(p):
                claim(pe, "T", f"sb{p}")
                pe.wait_ge(S("sb_lk_ready"), p + 1)
                for hh in range(2):
                    pe.matmul(pt[:, hh, 0:256], gt, sb_lk[p][:, hh, 0:256], start=True, stop=True)
                    pe.matmul(pt[:, hh, 128:256], ones, sb_lk[p][:, hh, 256:384], start=False, stop=True,
                              skip_group_check=True)
                    mm = pe.matmul(pt[:, hh, 256:384], gt, sb_lk[p][:, hh, 256:384], start=True, stop=True)
                written(mm, "T")

            def sb_apply(p):
                claim(pe, "O", f"sb{p}")
                pe.wait_ge(S("sb_w_ready"), p + 1)
                for hh in range(2):
                    h = 2 * p + hh
                    mm = weigh(po[:, hh * T:(hh + 1) * T], sbv[:, 0, h * P:(h + 1) * P],
                               sbv[:, 1, h * P:(h + 1) * P], sb_w[p][:, hh, :])
                written(mm, "O")

            run_unit(("sbq", 0), operand_gate(0))
            stats(0, sq)
            for n in (("sbq", 1), ("sbk", 0), ("sbk", 1), ("sbv", 0), ("sbv", 1), ("xbc", 0)):
                run_unit(n)
            for n in (("sbq", 0), ("sbq", 1), ("sbk", 0), ("sbk", 1)):
                await_value(pe, n)
            sb_scores(0)
            run_unit(("xbc", 1))
            sb_later(0)
            sb_scores(1)
            run_unit(("xbc", 2))
            await_value(pe, ("sbv", 0))
            await_value(pe, ("sbv", 1))
            sb_apply(0)
            sb_later(1)
            run_unit(("xbc", 3))
            sb_apply(1)
            for i in range(4, 8):
                run_unit(("xbc", i))

            claim(pe, "O", "dt")
            pe.wait_ge(S("ws_ready"), 1)
            for tb in range(2):
                for k in range(KC):
                    mm = three(po[:, tb * 64:tb * 64 + 40], ws_hi[:, k * 40:(k + 1) * 40],
                               ws_lo[:, k * 40:(k + 1) * 40], a_hi[:, k, tb * P:(tb + 1) * P],
                               a_lo[:, k, tb * P:(tb + 1) * P], k == 0, k == KC - 1, weights_left=False)
            written(mm, "O")
            run_unit(("kk", 0))

            pe.wait_ge(S("xbc_silu"), 4)
            claim(pe, "S", "xs")
            claim(pe, "T", "xs")
            for q in range(4):
                for m in range(4):
                    blk = (q % 2) * 4 + m
                    mm = transpose((ps, pt)[q // 2][:, q % 2, m * P:(m + 1) * P],
                                   xbc[:, blk, (q // 2) * P:(q // 2 + 1) * P])
                if q == 1:
                    written(mm, "S")
            written(mm, "T")
            run_unit(("kv", 0))
            claim(pe, "T", "cb")
            claim(pe, "S", "cb")
            for g in range(4):
                mm = pe.matmul(pt[:, g // 2, (g % 2) * T:(g % 2 + 1) * T], xbc[:, 8 + g, 0:P], xbc[:, 12 + g, :],
                               start=True, stop=True)
            written(mm, "T")
            for g in range(4):
                mm = pe.matmul(ps[:, 0, g * P:(g + 1) * P], xbc[:, 8 + g, P:T], xbc[:, 12 + g, P:T],
                               start=True, stop=True)
            written(mm, "S")

            def seg(g):
                claim(pe, "S", f"seg{g}")
                claim(pe, "T", f"seg{g}")
                pe.wait_ge(S("gdt_ready"), g + 1)
                for m in range(4):
                    bank = (ps, pt)[m // 2][:, m % 2, :]
                    pe.matmul(bank[:, 0:256], gdt[:, 0, m, :], le_ones, start=True, stop=True)
                    pe.matmul(bank[:, 128:256], dta[:, 1, 4 * g + m:4 * g + m + 1].to_broadcast([P, P]), le,
                              start=False, stop=True, skip_group_check=True)
                    mm = pe.matmul(bank[:, 256:384], gdt[:, 1, m, :], le, start=True, stop=True)
                    if m == 1:
                        written(mm, "S")
                written(mm, "T")

            def ssm_y(g):
                claim(pe, "O", f"y{g}")
                pe.wait_ge(S("ssm_w_ready"), 2 * (g + 1))
                for m in range(4):
                    c = (4 * g + m) * 64
                    pe.matmul(po[:, m * 64:(m + 1) * 64], E[:, m, 0:128], xdt[:, 0, c:c + 64], start=True, stop=True)
                    pe.matmul(po[:, 256 + m * 64:256 + (m + 1) * 64], E[:, m, 128:256], xdt[:, 0, c:c + 64],
                              start=True, stop=False)
                    mm = pe.matmul(po[:, 256 + m * 64:256 + (m + 1) * 64], E[:, m, 256:384], xdt[:, 1, c:c + 64],
                                   start=False, stop=True)
                written(mm, "O")

            seg(0)
            for g, n in enumerate((("vv", 0), ("nq", 0), ("nq", 1), ("z", 0))):
                run_unit(n)
                ssm_y(g)
                if g < 3:
                    seg(g + 1)
            run_unit(("z", 1))

            claim(pe, "O", "hid")
            pe.wait_ge(S("ckp_ready"), 4)
            pe.wait_ge(S("cmpw_loaded"), 16)
            for v in range(2):
                for c in range(16):
                    src = ckp[:, c // 8, v, :].rearrange("p (g n c) -> p g n c", g=2, c=8)
                    rhs = src[:, :, 0:15, c] if c < 8 else src[:, :, 1:16, c - 8]
                    mm = pe.matmul(po[0:64, v * 64:v * 64 + 30], cmp_w1[:, v, c, :], rhs, start=(c == 0),
                                   stop=(c == 15))
            written(mm, "O")
            run_unit(("z", 2))
            claim(pe, "O", "kc")
            pe.wait_ge(S("hid_ready"), 1)
            o = PCOLS["w2"][0]
            pe.matmul(po[0:64, 0:32], prm[0:64, o:o + 64], hid[0:64, 0, :], start=True, stop=True)
            written(pe.matmul(po[:, 64:128], hrep[0:64, :], prm[0:64, o + 64:o + 128], start=True, stop=True), "O")
            run_unit(("z", 3))
            claim(pe, "S", "cmp")
            await_read(pe, "O", "kc")
            await_value(pe, ("nq", 0))
            await_value(pe, ("nq", 1))
            for tb in range(2):
                for hb in range(2):
                    for j in range(4):
                        mm = pe.matmul(ps[:, hb, tb * 64 + j * 16:tb * 64 + (j + 1) * 16],
                                       nq[hb * 64:hb * 64 + 64, j, tb * P:(tb + 1) * P],
                                       kct[hb * 64:hb * 64 + 64, :], start=True, stop=True)
            written(mm, "S")
            run_unit(("gm", 0))
            claim(pe, "T", "cmp")
            pe.wait_ge(S("cmp_p_ready"), 1)
            for tb in range(2):
                mm = transpose(pt[:, 0, tb * P:(tb + 1) * P], cmp_e[:, tb, :])
            written(mm, "T")
            run_unit(("gm", 1))
            claim(pe, "S", "yt")
            claim(pe, "T", "yt")
            pe.wait_ge(S("y_normed"), 1)
            for k in range(KC):
                for tb in range(2):
                    mm = transpose((ps, pt)[k // 4][:, (k // 2) % 2, (k % 2) * T + tb * P:(k % 2) * T + (tb + 1) * P],
                                   y_tok[:, tb, k * P:(k + 1) * P])
                if k == 3:
                    written(mm, "S")
            written(mm, "T")
            run_unit(("gm", 2))

            def nsa_scores(r):
                j, b = r // 2, r % 2
                claim(pe, "S", f"n{r}")
                if r == 0:
                    await_value(pe, ("kk", 0))
                for hb in range(2):
                    q = slice(hb * 64, hb * 64 + 64)
                    mm = scores(nq[q, j, :], kk[q, b, :], ps[:, hb, :])
                written(mm, "S")

            def round_turn(name, idx, probs):
                claim(pe, "T", name)
                pe.wait_ge(S("probs_ready"), idx + 1)
                for hb in range(2):
                    mm = turn(probs[:, hb, :], pt[:, hb, :])
                written(mm, "T")

            def nsa_apply(r):
                j, b = r // 2, r % 2
                o_ = po[:, (j % 2) * T:(j % 2 + 1) * T]
                if b == 0:
                    claim(pe, "O", f"n{j}")
                    if j == 0:
                        pe.wait_ge(S("cmp_v_ready"), 1)
                        await_read(pe, "T", "cmp")
                        await_value(pe, ("vv", 0))
                    pe.matmul(o_, vc[:, j, :], pct, start=True, stop=False, skip_group_check=True)
                await_read(pe, "T", f"n{r}")
                for hb in range(2):
                    c = b * P + hb * 64
                    mm = weigh(o_[hb * 64:(hb + 1) * 64, :], vv[:, 0, c:c + 64], vv[:, 1, c:c + 64],
                               ptr[r % 2][:, hb, :], first=False, last=(b == 1))
                if b == 1:
                    written(mm, "O")

            nsa_scores(0)
            for r in range(8):
                run_unit(("gm", 3 + r))
                round_turn(f"n{r}", r, pr[r % 2])
                if r < 7:
                    nsa_scores(r + 1)
                if r >= 1:
                    nsa_apply(r - 1)
            run_unit(("gm", 11))
            nsa_apply(7)

            for n in range(8):
                name = ("br", n)
                u = UIDX[name]
                b, k0 = BANK[name]
                unit_ready(u)
                bank_free(b, k0)
                if n == 0:
                    pe.wait_ge(S("y_hi"), 16)
                    await_read(pe, "O", "n3")
                    await_read(pe, "T", "yt")
                    claim(pe, "S", "d0")
                elif n >= 2:
                    pe.wait_ge(S("br_nsa_read"), n - 1)
                for part, (k_lo, k_hi) in enumerate(((0, 8), (8, 12), (12, 16))):
                    o_ = ps[:, n % 2, 0:T] if part == 2 else pj[b][:, part * T:(part + 1) * T]
                    for k in range(k_lo, k_hi):
                        mm = three(o_, w_hi[:, u % SLOTS, k * P:(k + 1) * P], w_lo[:, u % SLOTS, k * P:(k + 1) * P],
                                   a_hi[:, 8 + k, :], a_lo[:, 8 + k, :], k == k_lo, k == k_hi - 1)
                mm.then_inc(S("unit_done"), 1)

            def mixed_gate(k):
                pe.wait_ge(S("mix_hi"), k + 1)
                pe.wait_ge(S("mix_lo"), k + 1)

            run_unit(("wo", 0), mixed_gate)
            for i in range(1, 4):
                run_unit(("wo", i))
            stats(1, sqy)

            acc = [ps[:, 0, :], ps[:, 1, :], pt[:, 0, :], pt[:, 1, :]]

            def down(slot, first, last):
                for kc in range(2):
                    for nb in range(8):
                        c = kc * D + nb * P
                        f = first and kc == 0
                        mm = three_acc(acc[nb // 2][:, (nb % 2) * T:(nb % 2 + 1) * T], slot, c, 8 + kc,
                                       f and nb % 2 == 0, last and kc == 1)
                mm.then_inc(S("unit_done"), 1)

            def three_acc(o_, slot, c, k, first, last):
                pe.matmul(o_, w_hi[:, slot, c:c + P], a_hi[:, k, :], start=first, stop=False, skip_group_check=True)
                pe.matmul(o_, w_hi[:, slot, c:c + P], a_lo[:, k, :], start=False, stop=False, skip_group_check=True)
                return pe.matmul(o_, w_lo[:, slot, c:c + P], a_hi[:, k, :], start=False, stop=last,
                                 skip_group_check=True)

            def up1(u, slot, parity, n, gate=None):
                unit_ready(u)
                bank_free(parity, n)
                unit_b(slot, parity, 0, gate)

            u0 = U_FFN1
            up1(u0, u0 % 3, 0, FFN1_BANK0[0], operand_gate(1))
            stats(2, sq_ffn)
            up1(u0 + 1, (u0 + 1) % 3, 1, FFN1_BANK0[1])

            def down1(u, slot, i, first, last):
                unit_ready(u)
                pe.wait_ge(S("u_hi"), 2 * i + 2)
                pe.wait_ge(S("u_lo"), 2 * i + 2)
                down(slot, first, last)

            def ffn1_step(i, first=False):
                u = u0 + 2 + (i - 1) * 3
                up1(u, (u0 + 2) % 3, 0, FFN1_BANK0[0] + i)
                down1(u + 1, (u0 + 3) % 3, i - 1, first, False)
                up1(u + 2, (u0 + 4) % 3, 1, FFN1_BANK0[1] + i)

            claim(pe, "T", "d0")
            pe.wait_ge(S("br_nsa_read"), 8)
            ffn1_step(1, first=True)
            with pe.Fori(2, DOWN1) as i:
                ffn1_step(i)
            down1(U_FFN1_END - 1, (U_FFN1_END - 1) % 3, DOWN1 - 1, False, True)
            stats(3, sqy)

            run_unit(("dq", 0), operand_gate(2))
            stats(4, sq_ffn)
            claim(pe, "O", "flog")
            pe.wait_ge(S("ws_ready"), 2)
            for tb in range(2):
                for k in range(KC):
                    mm = three(po[:, tb * 64:tb * 64 + 8], ws_hi[:, k * 8:(k + 1) * 8],
                               ws_lo[:, k * 8:(k + 1) * 8], a_hi[:, k, tb * P:(tb + 1) * P],
                               a_lo[:, k, tb * P:(tb + 1) * P], k == 0, k == KC - 1, weights_left=False)
            written(mm, "O")
            claim(pe, "O", "t5")
            o = PCOLS["rel"][0]
            written(pe.matmul(po[0:4, 0:384], prm[0:33, o:o + 4], cst_("onehot")[0:33, :], start=True, stop=True), "O")
            for n in (("dq", 1), ("dk", 0), ("dk", 1), ("dv", 0), ("dv", 1)):
                run_unit(n)

            def d_scores(h):
                claim(pe, "S", f"d{h}")
                if h == 0:
                    pe.wait_ge(S("acc_copied"), 4)
                    for n in (("dq", 0), ("dq", 1), ("dk", 0), ("dk", 1)):
                        await_value(pe, n)
                for mp in range(2):
                    q = slice(mp * 64, mp * 64 + 64)
                    mm = scores(dq[q, h, :], dk[q, h, :], ps[:, mp, :])
                written(mm, "S")

            def d_turn(h):
                claim(pe, "T", f"d{h}")
                pe.wait_ge(S("probs_ready"), 8 + h + 1)
                written(turn(pr2[h % 2][:, 0, :], pt[:, 0, :]), "T")

            def d_apply(h):
                if h % 2 == 0:
                    claim(pe, "O", f"d{h // 2}")
                await_read(pe, "T", f"d{h}")
                if h == 0:
                    await_value(pe, ("dv", 0))
                    await_value(pe, ("dv", 1))
                mm = weigh(po[:, (h % 2) * T:(h % 2 + 1) * T], dv[:, 0, h * P:(h + 1) * P],
                           dv[:, 1, h * P:(h + 1) * P], ptr2[h % 2][:, 0, :])
                if h % 2 == 1:
                    written(mm, "O")

            def f_scores(j):
                claim(pe, "S", f"f{j}")
                if j == 0:
                    for n in (("fq", 0), ("fq", 1), ("fk", 0), ("fk", 1)):
                        await_value(pe, n)
                pe.wait_ge(S("lfle_ready"), j + 1)
                for hb in range(2):
                    q = slice(hb * 64, hb * 64 + 64)
                    o_ = ps[:, hb, :]
                    ll = lfle[j % 2]
                    pe.matmul(o_[:, 0:128], fq[q, j, 0:P], fk[q, j, 0:P], start=True, stop=False)
                    pe.matmul(o_[:, 0:128], ll[:, 0, hb, :], gt, start=False, stop=True)
                    pe.matmul(o_[:, 128:384], fq[q, j, P:T], fk[q, j, 0:T], start=True, stop=False)
                    pe.matmul(o_[:, 128:384], ll[:, 1, hb, :], ones_gt, start=False, stop=True)
                    mm = pe.matmul(o_[:, 128:256], lf[:, 0, 2 * j + hb:2 * j + hb + 1].to_broadcast([P, P]), gt,
                                   start=False, stop=True, skip_group_check=True)
                written(mm, "S")

            def f_apply(j):
                claim(pe, "O", f"f{j}")
                await_read(pe, "T", f"f{j}")
                if j == 0:
                    await_value(pe, ("fv", 0))
                    await_value(pe, ("fv", 1))
                for hb in range(2):
                    c = (2 * j + hb) * 64
                    mm = weigh(po[hb * 64:(hb + 1) * 64, 0:T], fv[:, 0, c:c + 64], fv[:, 1, c:c + 64],
                               ptr2[j % 2][:, hb, :])
                written(mm, "O")

            run_unit(("fq", 0))
            d_scores(0)
            for h, n in enumerate((("fq", 1), ("fk", 0), ("fk", 1), ("fv", 0))):
                run_unit(n)
                d_turn(h)
                if h < 3:
                    d_scores(h + 1)
                if h >= 1:
                    d_apply(h - 1)
            run_unit(("fv", 1))
            d_apply(3)
            f_scores(0)
            claim(pe, "O", "odn")
            pe.wait_ge(S("od_sq_ready"), 1)
            for h in range(4):
                for tb in range(2):
                    mm = pe.matmul(po[:, 2 * h + tb:2 * h + tb + 1], odsq[:, h, tb * P:(tb + 1) * P], ones[:, 0:1],
                                   start=True, stop=True)
            written(mm, "O")
            for j in range(4):
                round_turn(f"f{j}", 12 + j, pr2[j % 2])
                if j < 3:
                    f_scores(j + 1)
                if j >= 1:
                    f_apply(j - 1)
            f_apply(3)
            claim(pe, "S", "odn")
            pe.wait_ge(S("dg8_ready"), 1)
            for q in range(2):
                mm = pe.matmul(ps[:, q, :], ones, dg8[:, 4 * q:4 * q + 4, :], start=True, stop=True)
            written(mm, "S")
            pe.wait_ge(S("mix2_hi"), 5)
            pe.wait_ge(S("mix2_lo"), 1)
            await_read(pe, "O", "f3")
            for i in range(4):
                run_unit(("wo2", i))
            stats(5, sqy)

            def up2(u, slot, b, n, gate=None):
                unit_ready(u)
                bank_free(b, n)
                unit_b(slot, b, 0, gate)

            def down2(u, slot, i, first, last):
                unit_ready(u)
                pe.wait_ge(S("u_hi"), 2 * DOWN1 + i + 1)
                pe.wait_ge(S("u_lo"), 2 * DOWN1 + i + 1)
                down(slot, first, last)

            v0 = U_FFN2
            up2(v0, v0 % 3, 0, FFN2_BANK0[0], operand_gate(3))
            stats(6, sq_ffn)

            def ffn2_step(m, first=False):
                for q in range(3):
                    u = v0 + 1 + m * 6 + 2 * q
                    b = (q + 1) % 3
                    up2(u, (v0 + 1 + 2 * q) % 3, b, m + (FFN2_BANK0[b] + (1 if b == 0 else 0)))
                    down2(u + 1, (v0 + 2 + 2 * q) % 3, m * 3 + q, first and q == 0, False)

            await_read(pe, "S", "odn")
            await_read(pe, "T", "f3")
            ffn2_step(0, first=True)
            with pe.Fori(1, 4) as m:
                ffn2_step(m)
            ffn2_step(4)
            down2(N_UNITS - 1, (N_UNITS - 1) % 3, DOWN2 - 1, False, True)
            stats(7, sqy)
            pe.wait_ge(S("acc_copied"), 8)
            for k in range(KC):
                pe.wait_ge(S("x_final"), k + 1)
                for tb in range(2):
                    mm = transpose((ps, pt)[tb][:, k // 4, (k % 4) * P:(k % 4 + 1) * P], xT[:, k, tb * P:(tb + 1) * P])
                if k % 4 == 3:
                    mm.then_inc(S("out_turned"), 1)

        @block.scalar
        def _(act):
            A = Order(act, "act_order")

            def split(base, m=0):
                slot = base % SLOTS
                act.wait_ge(S(f"w_loaded{slot}"), (m + base // SLOTS + 1) * 16)
                if base >= SLOTS:
                    act.wait_ge(S("unit_done"), m * SLOTS + (base - SLOTS + 1))
                act.activation(w_hi[:, slot, :], w_raw[:, slot, :], ACT.Copy).then_inc(S("w_hi_done"), 1)

            ahead_of = [0]

            def ahead(name_or_u):
                u = UIDX[name_or_u] if isinstance(name_or_u, tuple) else name_or_u
                while ahead_of[0] <= min(u + 2, N_UNITS - 1):
                    split(ahead_of[0])
                    ahead_of[0] += 1
                return u

            def token_major(name, dst):
                u = ahead(name)
                b, _n = BANK[name]
                act.wait_ge(S("unit_done"), u + 1)
                for tb in range(2):
                    ins = act.activation(dst[:, tb, :], pj[b][:, tb * 256:(tb + 1) * 256], ACT.Copy,
                                         scale=rcol[:, tb:tb + 1])
                ins.then_inc(S(f"pj_read{b}"), 1)

            def operand(n, gname, sq_t):
                g = prm_(gname)
                for k in range(KC):
                    act.wait_ge(S("x_ready"), KC * n + k + 1)
                    act.activation(a_hi[:, k, :], xT[:, k, :], ACT.Copy, scale=g[:, k:k + 1]).then_inc(S("opnd_hi"), 1)
                    act.activation(sq_t[:, k, :], xT[:, k, :], ACT.Square).then_inc(S("sq_ready"), 1)

            def root(n):
                await_psum(act, "O", f"norm{n}")
                read(act.activation(rt, po[:, 0:2], ACT.Sqrt, bias=eps_t, scale=1.0 / D), "O")

            act.wait_ge(S("eps_ready"), 1)
            act.wait_ge(S("prm_loaded"), 16)
            split(0)
            ahead_of[0] = 1
            operand(0, "g_mix1", sq)
            ahead(0)
            root(0)
            ahead(("sbk", 1))
            act.wait_ge(S("diag_ready"), 1)
            for i in range(2):
                token_major(("sbv", i), sbv[:, :, i * 256:(i + 1) * 256])

            def conv_first(i):
                ahead(("xbc", i))
                await_value(act, ("xbc", i))
                for m in range(2):
                    blk = 2 * i + m
                    act.activation(xbc[:, blk, :], xc[i % 2][:, m, :], ACT.Identity,
                                   bias=prm_("cb")[:, blk:blk + 1], scale=prm_("cw")[:, 48 + blk:49 + blk])\
                       .then_inc(S("conv_tap3"), 1)

            def sb_logs(p):
                await_psum(act, "S", f"sb{p}")
                A.did(act.activation(sb_l[p], ps[:, :, 0:384], ACT.Abs))
                A.sync()
                A.did(act.activation(sb_ls[p], sb_l[p], ACT.Exp, scale=-1.0))
                A.sync()
                act.activation(sb_l[p], sb_ls[p], ACT.Ln, bias=1.0).then_inc(S("sb_log_ready"), 1)

            def sb_exp(p):
                await_read(act, "T", f"sb{p}")
                act.activation(sb_w[p], sb_ls[p], ACT.Exp).then_inc(S("sb_exp_ready"), 1)

            def sb_hi(p):
                await_psum(act, "O", f"sb{p}")
                for hh in range(2):
                    act.activation(a_hi[:, 16 + 2 * p + hh, :], po[:, hh * T:(hh + 1) * T], ACT.Copy)\
                       .then_inc(S("y_hi"), 1)

            conv_first(0)
            sb_logs(0)
            conv_first(1)
            sb_exp(0)
            sb_logs(1)
            conv_first(2)
            sb_hi(0)
            sb_exp(1)
            conv_first(3)
            sb_hi(1)
            for i in range(4, 8):
                conv_first(i)

            o = PCOLS["ws1"][0]
            act.activation(ws_hi[:, :], prm[:, o:o + 320], ACT.Copy).then_inc(S("ws_hi"), 1)
            await_psum(act, "O", "dt")
            for tb in range(2):
                ins = act.activation(small40[:, tb, :], po[:, tb * 64:tb * 64 + 40], ACT.Copy, scale=rcol[:, tb:tb + 1])
            read(ins, "O")
            act.activation(ea, prm_("a_log"), ACT.Exp).then_inc(S("ea_ready"), 1)
            act.wait_ge(S("dtx_ready"), 1)
            A.did(act.activation(dt_e, dtx, ACT.Abs))
            A.sync()
            A.did(act.activation(dt_e, dt_e, ACT.Exp, scale=-1.0))
            A.sync()
            act.activation(dt_e, dt_e, ACT.Ln, bias=1.0).then_inc(S("dte_ready"), 1)
            ahead(("kk", 0))
            for q in range(4):
                act.wait_ge(S("xbc_conv"), 4 * (q + 1))
                act.activation(xbc[:, 4 * q:4 * q + 4, :], xbc[:, 4 * q:4 * q + 4, :], ACT.Silu)\
                   .then_inc(S("xbc_silu"), 1)
            act.activation(gate, small40[:, :, 16:40], ACT.Tanh, scale=0.5).then_inc(S("gate_tanh"), 1)
            for q in range(4):
                if q % 2 == 0:
                    await_psum(act, "ST"[q // 2], "xs")
                act.activation(xs_tok[:, q // 2, (q % 2) * 512:(q % 2 + 1) * 512], (ps, pt)[q // 2][:, q % 2, :],
                               ACT.Copy).then_inc(S("xs_tok_ready"), 1)
            ahead(("kv", 0))
            await_value(act, ("kv", 0))
            await_psum(act, "S", "cb")
            for g in range(2):
                for half in range(2):
                    act.activation(ck[half * 64:half * 64 + 64, :, g, :], cm[g * 64:g * 64 + 64, :, half:T:2],
                                   ACT.Copy).then_inc(S("ck_ready"), 1)

            def decay(g):
                for region, bank, m in (("S", ps, 0), ("T", pt, 2)):
                    await_psum(act, region, f"seg{g}")
                    read(act.activation(E[:, m:m + 2, :], bank[:, :, 0:384], ACT.Exp), region)

            decay(0)
            token_major(("vv", 0), vv)
            decay(1)
            ahead(("nq", 0))
            decay(2)
            ahead(("nq", 1))
            decay(3)
            ahead(("z", 0))
            await_psum(act, "O", "y3")
            token_major(("z", 0), z[:, :, 0:256])
            token_major(("z", 1), z[:, :, 256:512])
            await_psum(act, "O", "hid")
            act.activation(hid_t[0:64, :, 0:30], po[0:64, 0:128].rearrange("p (v x) -> p v x", v=2)[:, :, 0:30],
                           ACT.Tanh, scale=0.5).then_inc(S("hid_tanh"), 1)
            token_major(("z", 2), z[:, :, 512:768])
            await_psum(act, "O", "kc")
            for hb in range(2):
                act.activation(kct[hb * 64:hb * 64 + 64, :], po[0:64, hb * 16:hb * 16 + 16], ACT.Copy, scale=0.5)
            read(act.activation(vrep, po[:, 64:128], ACT.Copy, scale=0.5), "O")
            token_major(("z", 3), z[:, :, 768:1024])
            for b in set(BANK[("z", i)][0] for i in range(4)):
                act.wait_ge(S(f"pj_read{b}"), max(BANK[("z", i)][1] for i in range(4) if BANK[("z", i)][0] == b) + 1)
            act.activation(z, z, ACT.Silu).then_inc(S("z_silu"), 1)
            act.wait_ge(S("cmp_s_ready"), 1)
            act.activation(cmp_e, cmp_e, ACT.Exp).then_inc(S("cmp_exp"), 1)
            ahead(("gm", 0))
            await_psum(act, "T", "cmp")
            read(act.activation(pct, pt[:, 0, 0:T], ACT.Copy), "T")
            act.wait_ge(S("y_gated"), 1)
            for tb in range(2):
                for g in range(4):
                    A.did(act.activation(y_sq, y_tok[:, tb, g * 256:(g + 1) * 256], ACT.Square,
                                         accum_out=ssy[:, tb, g:g + 1]))
                    A.sync()
            act.activation(ry, ssy, ACT.Sqrt, bias=eps_t, scale=1.0 / 256).then_inc(S("y_root"), 1)

            def gm_tanh(i):
                ahead(("gm", i))
                await_value(act, ("gm", i))
                pair = area[:, gm_at[2 * i] * 256:gm_at[2 * i] * 256 + 512]
                act.activation(pair, pair, ACT.Tanh, scale=0.5).then_inc(S("gm_tanh"), 1)

            gm_tanh(0)
            gm_tanh(1)
            nw = prm_("ssm_norm")
            for k in range(KC):
                if k % 4 == 0:
                    await_psum(act, "ST"[k // 4], "yt")
                act.activation(a_hi[:, 8 + k, :], (ps, pt)[k // 4][:, (k // 2) % 2, (k % 2) * T:(k % 2 + 1) * T],
                               ACT.Copy, scale=nw[:, k:k + 1]).then_inc(S("y_hi"), 1)
            gm_tanh(2)

            def exps(idx, s_, p_):
                act.wait_ge(S("max_ready"), idx + 1)
                for t in range(2):
                    for hb in range(2):
                        c = t * 2 + hb
                        cols = slice(0, 128) if t == 0 else slice(128, 384)
                        act.activation(p_[idx % 2][:, hb, cols], s_[idx % 2][:, hb, cols], ACT.Exp,
                                       bias=mx[idx % 2][:, c:c + 1], accum_out=sums[idx % 2][:, c:c + 1])\
                           .then_inc(S("exp_done"), 1)

            def nsa_out_hi(j):
                await_psum(act, "O", f"n{j}")
                act.activation(a_hi[:, 20 + j, :], po[:, (j % 2) * T:(j % 2 + 1) * T], ACT.Copy).then_inc(S("y_hi"), 1)

            for r in range(8):
                exps(r, sm, pr)
                gm_tanh(3 + r)
                await_psum(act, "T", f"n{r}")
                read(act.activation(ptr[r % 2], pt[:, :, 0:384], ACT.Copy), "T")
                if r in (2, 4, 6):
                    nsa_out_hi(r // 2 - 1)
            gm_tanh(11)
            nsa_out_hi(3)

            for n in range(8):
                ahead(("br", n))
                act.wait_ge(S("mixed_ready"), n + 1)
                act.activation(a_hi[:, n, :], mixt[n % 2][:, 0, :], ACT.Copy, scale=0.5).then_inc(S("mix_hi"), 1)

            def out_units(tag, n):
                for i in range(4):
                    u = ahead((tag, i))
                    b, _n = BANK[(tag, i)]
                    act.wait_ge(S("unit_done"), u + 1)
                    for m in range(2):
                        act.activation(sqy[:, 2 * i + m, :], pj[b][:, m * T:(m + 1) * T], ACT.Square)\
                           .then_inc(S("sq_ready"), 1)
                    act.activation(yT[:, 2 * i:2 * i + 2, :], pj[b][:, :], ACT.Copy).then_inc(S(f"pj_read{b}"), 1)
                root(n)

            def acc_squares(u_last, n):
                act.wait_ge(S("unit_done"), u_last + 1)
                for k in range(KC):
                    act.activation(sqy[:, k, :], (ps, pt)[k // 4][:, (k // 2) % 2, (k % 2) * T:(k % 2 + 1) * T],
                                   ACT.Square).then_inc(S("sq_ready"), 1)
                root(n)

            out_units("wo", 1)
            operand(1, "g_ffn1", sq_ffn)
            root(2)

            fw, fb = PCOLS["fw"][0], PCOLS["fb"][0]

            def up1(c, n, hi_wait):
                act.wait_ge(S(f"pj_read{n[1]}"), n[0] + 1)
                for m in range(2):
                    act.activation(facc[:, m, :], fx[:, m, :], ACT.Identity,
                                   bias=prm[:, bass.ds(c + (fb + m * UP1), 1)],
                                   scale=prm[:, bass.ds(c + (fw + 88 + m * UP1), 1)]).then_inc(S("tap2_done"), 1)
                act.wait_ge(S("ftaps_done"), c * 2 + 1)
                act.activation(fg, facc[:, 0, :], ACT.Gelu_apprx_tanh).then_inc(S("gelu_done"), 1)
                act.wait_ge(S("fu_ready"), c + 1)
                if hi_wait is not None:
                    act.wait_ge(S("unit_done"), hi_wait)

            def u_hi(slot):
                act.activation(a_hi[:, 8 + slot, :], fu[:, 0, :], ACT.Copy).then_inc(S("u_hi"), 1)

            u0 = U_FFN1
            for c in range(2):
                ahead(u0 + c)
                up1(c, (FFN1_BANK0[c], c), None)
                u_hi(c)

            def ffn1_step(i):
                b = u0 + 4
                m = i - 1
                split(b, m)
                up1(i * 2, (i + FFN1_BANK0[0], 0), m * 3 + (u0 + 4))
                u_hi(0)
                split(b + 1, m)
                split(b + 2, m)
                up1(i * 2 + 1, (i + FFN1_BANK0[1], 1), None)
                u_hi(1)

            ffn1_step(1)
            with act.Fori(2, DOWN1) as i:
                ffn1_step(i)
            ahead_of[0] = U_FFN1_END + 1
            ahead(U_FFN1_END - 1)
            acc_squares(U_FFN1_END - 1, 3)
            operand(2, "g_mix2", sq_ffn)

            o2 = PCOLS["ws2"][0]
            act.activation(ws_hi[:, 0:64], prm[:, o2:o2 + 64], ACT.Copy).then_inc(S("ws_hi"), 1)
            root(4)
            act.wait_ge(S("diag_ready"), 5)
            ahead(("dq", 0))
            act.wait_ge(S("lam_sums"), 1)
            act.activation(lamv[:, 2:4], lamv[:, 0:2], ACT.Exp).then_inc(S("lam_exp"), 1)
            await_psum(act, "O", "flog")
            for tb in range(2):
                ins = act.activation(fl[:, tb, :], po[:, tb * 64:tb * 64 + 8], ACT.Copy, scale=rcol[:, tb:tb + 1])
            read(ins, "O")
            await_psum(act, "O", "t5")
            read(act.activation(t5_sb[0:4, :], po[0:4, 0:384], ACT.Copy), "O")
            act.wait_ge(S("flx_ready"), 1)
            A.did(act.activation(lf_e, fl, ACT.Abs))
            A.sync()
            A.did(act.activation(lf_e, lf_e, ACT.Exp, scale=-1.0))
            A.sync()
            act.activation(lf_e, lf_e, ACT.Ln, bias=1.0).then_inc(S("lfe_ready"), 1)
            for i in range(2):
                token_major(("dv", i), dv[:, :, i * 256:(i + 1) * 256])
            ahead(("fq", 0))

            def d_out(p):
                await_psum(act, "O", f"d{p}")
                read(act.activation(od[:, 2 * p:2 * p + 2, :], po[:, :], ACT.Copy), "O")

            for h, n in enumerate((("fq", 1), ("fk", 0), ("fk", 1), ("fv", 0))):
                exps(8 + h, sm2, pr2)
                if n[0] == "fv":
                    token_major(n, fv[:, :, 0:256])
                else:
                    ahead(n)
                await_psum(act, "T", f"d{h}")
                read(act.activation(ptr2[h % 2][:, 0, :], pt[:, 0, 0:384], ACT.Copy), "T")
                if h == 2:
                    d_out(0)
            token_major(("fv", 1), fv[:, :, 256:512])
            d_out(1)
            await_read(act, "O", "d1")
            act.activation(odsq, od, ACT.Square).then_inc(S("od_sq_ready"), 1)
            await_psum(act, "O", "odn")
            act.wait_ge(S("lm_ready"), 1)
            read(act.activation(ods, po[:, 0:8], ACT.Sqrt, bias=lm[:, 2:3], scale=1.0 / 128), "O")

            def f_out_hi(j):
                await_psum(act, "O", f"f{j}")
                act.activation(a_hi[:, 12 + j, :], po[:, 0:T], ACT.Copy).then_inc(S("mix2_hi"), 1)

            for j in range(4):
                exps(12 + j, sm2, pr2)
                await_psum(act, "T", f"f{j}")
                read(act.activation(ptr2[j % 2], pt[:, :, 0:384], ACT.Copy), "T")
                if j >= 1:
                    f_out_hi(j - 1)
            f_out_hi(3)
            act.wait_ge(S("odn_ready"), 1)
            await_read(act, "S", "odn")
            act.activation(a_hi[:, 8:12, :], odn, ACT.Copy, scale=1.0 - LAMBDA_INIT).then_inc(S("mix2_hi"), 1)
            out_units("wo2", 5)
            operand(3, "g_ffn2", sq_ffn)
            root(6)

            def up2(i, hi_wait):
                act.wait_ge(S("fu_ready"), i + UP1 + 1)
                if hi_wait is not None:
                    act.wait_ge(S("unit_done"), hi_wait)
                act.activation(a_hi[:, 8:10, :], fu, ACT.Copy).then_inc(S("u_hi"), 1)

            v0 = U_FFN2
            ahead(v0)
            up2(0, None)

            def ffn2_step(m, last=False):
                for q in range(3):
                    b = v0 + 1 + 2 * q + 2
                    split(b, m * 2)
                    up2(m * 3 + q + 1, m * 6 + (v0 + 3 + 2 * q))
                    if not (last and q == 2):
                        split(b + 1, m * 2)

            ffn2_step(0)
            with act.Fori(1, 4) as m:
                ffn2_step(m)
            ffn2_step(4, last=True)
            acc_squares(N_UNITS - 1, 7)
            for h in range(2):
                act.wait_ge(S("out_turned"), h + 1)
                act.activation(x_tok[:, 0, h * 512:(h + 1) * 512], ps[:, h, :], ACT.Copy).then_inc(S("out_ready"), 1)

        @block.vector
        def _(dve):
            V_ = Order(dve, "dve_order")

            def split(base, m=0):
                slot = base % SLOTS
                dve.wait_ge(S("w_hi_done"), m * SLOTS + (base + 1))
                dve.tensor_tensor(w_lo[:, slot, :], w_raw[:, slot, :], w_hi[:, slot, :].bitcast(F32), ALU.subtract)\
                   .then_inc(S("w_lo_done"), 1)

            ahead_of = [0]

            def ahead(name_or_u):
                u = UIDX[name_or_u] if isinstance(name_or_u, tuple) else name_or_u
                while ahead_of[0] <= min(u + 2, N_UNITS - 1):
                    split(ahead_of[0])
                    ahead_of[0] += 1
                return u

            def tt(o_, a, b, op):
                return dve.tensor_tensor(o_, a, b, op)

            def stt(o_, a, s_, b, op0, op1):
                return dve.scalar_tensor_tensor(out=o_, in0=a, scalar=s_, in1=b, op0=op0, op1=op1)

            def two(bank):
                return bank[:, :].rearrange("p (a t) -> p a t", a=2)

            rbc2 = rbc[:, :].unsqueeze(1).to_broadcast([P, 2, T])

            def channel_major(name, dst, scale=None):
                u = ahead(name)
                b, _n = BANK[name]
                dve.wait_ge(S("unit_done"), u + 1)
                ins = tt(dst, two(pj[b]), rbc2, ALU.mult) if scale is None \
                    else stt(dst, two(pj[b]), scale, rbc2, ALU.mult, ALU.mult)
                ins.then_inc(S(f"pj_read{b}"), 1)

            def operand_lo(n, gname, k):
                g = prm_(gname)
                dve.wait_ge(S("opnd_hi"), KC * n + k + 1)
                stt(a_lo[:, k, :], xT[:, k, :], g[:, k:k + 1], a_hi[:, k, :].bitcast(F32), ALU.mult,
                    ALU.subtract).then_inc(S("opnd_lo"), 1)

            def norm_tail(n):
                await_read(dve, "O", f"norm{n}")
                V_.did(dve.reciprocal(rcol, rt))
                V_.sync()
                dve.tensor_scalar(dgr[:, 0, :], ident, rcol[:, 0:1], None, ALU.mult)
                dve.tensor_scalar(dgr[:, 1, :], ident, rcol[:, 1:2], None, ALU.mult).then_inc(S("diag_ready"), 1)
                await_psum(dve, "O", f"rbc{n}")
                read(dve.tensor_copy(rbc[:, :], po[:, 256:512]), "O")
                await_read(dve, "O", f"rbc{n}")

            dve.memset(eps_t, EPS).then_inc(S("eps_ready"), 1)
            dve.wait_ge(S("prm_loaded"), 16)
            for k in range(KC):
                if k % 4 == 0:
                    await_psum(dve, "ST"[k // 4], "x")
                dve.tensor_copy(xT[:, k, :], (ps, pt)[k // 4][:, (k // 2) % 2, (k % 2) * T:(k % 2 + 1) * T])\
                   .then_inc(S("x_ready"), 1)
            read(dve.memset(hid, 0.0), "S")
            read(dve.memset(hid_t, 0.0), "T")
            split(0)
            ahead_of[0] = 1
            for k in range(KC):
                operand_lo(0, "g_mix1", k)
            ahead(0)
            norm_tail(0)
            for i in range(2):
                channel_major(("sbq", i), sbq[:, 2 * i:2 * i + 2, :], 128.0 ** -0.5)
            for i in range(2):
                channel_major(("sbk", i), sbk[:, 2 * i:2 * i + 2, :])
            ahead(("sbv", 1))

            def conv(i):
                if i >= 2:
                    dve.wait_ge(S("conv_tap3"), 2 * (i - 1))
                channel_major(("xbc", i), xc[i % 2])
                cw = prm_("cw")
                await_value(dve, ("xbc", i))
                dve.wait_ge(S("conv_tap3"), 2 * (i + 1))
                for s_ in (1, 2, 3):
                    for m in range(2):
                        blk = 2 * i + m
                        c = (3 - s_) * 16 + blk
                        ins = stt(xbc[:, blk, s_:T], xc[i % 2][:, m, 0:T - s_], cw[:, c:c + 1], xbc[:, blk, s_:T],
                                  ALU.mult, ALU.add)
                        if s_ == 3:
                            ins.then_inc(S("xbc_conv"), 1)
                        else:
                            V_.did(ins)
                    if s_ < 3:
                        V_.sync()

            def sb_keep(p):
                dve.wait_ge(S("sb_log_ready"), p + 1)
                V_.did(stt(sb_ls[p], ps[:, :, 0:384], 0.0, sb_l[p], ALU.min, ALU.subtract))
                V_.sync()
                read(tt(sb_lk[p], sb_ls[p], ps[:, :, 0:384], ALU.subtract), "S")
                await_read(dve, "S", f"sb{p}")
                tt(sb_lk[p], sb_lk[p], cst_("sbmask").unsqueeze(1).to_broadcast([P, 2, 384]), ALU.mult)\
                    .then_inc(S("sb_lk_ready"), 1)

            def sb_sum(p):
                await_psum(dve, "T", f"sb{p}")
                read(tt(sb_ls[p], sb_ls[p], pt[:, :, 0:384], ALU.add), "T")

            def sb_mask(p):
                dve.wait_ge(S("sb_exp_ready"), p + 1)
                tt(sb_w[p], sb_w[p], cst_("sbmask").unsqueeze(1).to_broadcast([P, 2, 384]), ALU.mult)\
                    .then_inc(S("sb_w_ready"), 1)

            def sb_lo(p):
                dve.wait_ge(S("y_hi"), 2 * p + 2)
                read(tt(a_lo[:, 16 + 2 * p:18 + 2 * p, :], two(po), a_hi[:, 16 + 2 * p:18 + 2 * p, :].bitcast(F32),
                        ALU.subtract), "O")

            conv(0)
            sb_keep(0)
            conv(1)
            sb_sum(0)
            sb_mask(0)
            sb_keep(1)
            conv(2)
            sb_lo(0)
            sb_sum(1)
            sb_mask(1)
            conv(3)
            sb_lo(1)
            for i in range(4, 8):
                conv(i)

            dve.wait_ge(S("ws_hi"), 1)
            o = PCOLS["ws1"][0]
            tt(ws_lo[:, :], prm[:, o:o + 320], ws_hi[:, :].bitcast(F32), ALU.subtract).then_inc(S("ws_ready"), 1)
            await_read(dve, "O", "dt")
            tt(dtx, small40[:, :, 0:16], prm_("dt_bias").unsqueeze(1).to_broadcast([P, 2, 16]), ALU.add)\
                .then_inc(S("dtx_ready"), 1)
            dve.wait_ge(S("dte_ready"), 1)
            dve.wait_ge(S("ea_ready"), 1)
            V_.did(stt(dt_, dtx, 0.0, dt_e, ALU.max, ALU.add))
            V_.sync()
            stt(dta, dt_, -1.0, ea.unsqueeze(1).to_broadcast([P, 2, 16]), ALU.mult, ALU.mult)\
                .then_inc(S("dta_ready"), 1)
            dve.wait_ge(S("gate_tanh"), 1)
            V_.did(dve.tensor_scalar(gate, gate, 0.5, 0.5, ALU.mult, ALU.add))
            channel_major(("kk", 0), kk)
            for q in range(4):
                dve.wait_ge(S("xs_tok_ready"), q + 1)
                ins = tt(xdt[:, q // 2, (q % 2) * 512:(q % 2 + 1) * 512].rearrange("p (h c) -> p h c", h=8),
                         (ps, pt)[q // 2][:, q % 2, :].rearrange("p (h c) -> p h c", h=8),
                         dt_[:, q // 2, (q % 2) * 8:(q % 2) * 8 + 8].unsqueeze(2).to_broadcast([P, 8, 64]), ALU.mult)
                if q % 2:
                    read(ins, "ST"[q // 2])
            channel_major(("kv", 0), cm)
            await_psum(dve, "T", "cb")
            read(tt(cb[:, :, 0:256], pt[:, :, :].rearrange("p a (b t) -> p (a b) t", b=2),
                    cst_("cbmask")[:, 0:256].unsqueeze(1).to_broadcast([P, 4, 256]), ALU.mult), "T")
            await_psum(dve, "S", "cb")
            read(tt(cb[:, :, 256:384], ps[:, 0, :].rearrange("p (g t) -> p g t", g=4),
                    le.unsqueeze(1).to_broadcast([P, 4, P]), ALU.mult), "S")

            def ssm_w(g):
                await_read(dve, "T", "cb")
                await_read(dve, "S", "cb")
                for region, m in (("S", 0), ("T", 2)):
                    await_read(dve, region, f"seg{g}")
                    tt(E[:, m:m + 2, :], E[:, m:m + 2, :], cb[:, g, :].unsqueeze(1).to_broadcast([P, 2, 384]),
                       ALU.mult).then_inc(S("ssm_w_ready"), 1)

            def ssm_out(g):
                await_psum(dve, "O", f"y{g}")
                dve.wait_ge(S("xd_ready"), 1)
                read(tt(y_tok[:, :, g * 256:(g + 1) * 256], two(po), xs_tok[:, :, g * 256:(g + 1) * 256], ALU.add), "O")

            ssm_w(0)
            dve.wait_ge(S("ck_ready"), 4)
            pos = prm_("pos").rearrange("p (v c) -> p v c", v=2)
            for half in range(2):
                for v in range(2):
                    tt(ckp[:, half, v, :].rearrange("p (n c) -> p n c", c=8),
                       ck[:, v, :, :].rearrange("p g t -> p (g t)").rearrange("p (n c) -> p n c", c=8),
                       pos[:, v, half * 8:half * 8 + 8].unsqueeze(1).to_broadcast([P, 32, 8]), ALU.add)\
                        .then_inc(S("ckp_ready"), 1)
            ahead(("vv", 0))
            ssm_out(0)
            ssm_w(1)
            channel_major(("nq", 0), nq[:, 0:2, :], 64.0 ** -0.5)
            ssm_out(1)
            ssm_w(2)
            channel_major(("nq", 1), nq[:, 2:4, :], 64.0 ** -0.5)
            ssm_out(2)
            ssm_w(3)
            ahead(("z", 0))
            ssm_out(3)
            ahead(("z", 1))
            dve.wait_ge(S("hid_tanh"), 1)
            for v in range(2):
                ins = stt(hid[0:64, v, :].rearrange("p (g n) -> p g n", g=2)[:, :, 0:15],
                          hid_t[0:64, v, 0:30].rearrange("p (g n) -> p g n", g=2), 1.0,
                          po[0:64, v * 64:v * 64 + 30].rearrange("p (g n) -> p g n", g=2), ALU.add, ALU.mult)
            read(ins, "O")
            await_read(dve, "O", "hid")
            dve.tensor_copy(hrep[0:64, :].rearrange("p (g h n) -> p g h n", g=2, h=4),
                            hid[0:64, 1, :].rearrange("p (g n) -> p g n", g=2).unsqueeze(2).to_broadcast([64, 2, 4, 16]))\
               .then_inc(S("hid_ready"), 1)
            ahead(("z", 2))
            await_read(dve, "O", "kc")
            tt(vc.rearrange("p j (b d) -> p (j b) d", b=2), vrep.unsqueeze(1).to_broadcast([P, 8, 64]),
               cst_("cmpmask").unsqueeze(2).to_broadcast([P, 8, 64]), ALU.mult).then_inc(S("cmp_v_ready"), 1)
            ahead(("z", 3))
            await_psum(dve, "S", "cmp")
            cb_ = cst_("cmpbias").rearrange("p (t x) -> p t x", t=2)
            for hb in range(2):
                ins = tt(cmp_e[:, :, hb * 64:(hb + 1) * 64], ps[:, hb, 0:128].rearrange("p (t x) -> p t x", t=2),
                         cb_[:, :, hb * 64:(hb + 1) * 64], ALU.add)
            read(ins, "S")
            await_read(dve, "S", "cmp")
            ce = cmp_e.rearrange("p t x -> p (t x)").rearrange("p (h n) -> p h n", n=16)
            V_.did(dve.tensor_reduce(cmx, ce, AX.X, ALU.max))
            V_.sync()
            tt(ce, ce, cmx.unsqueeze(2).to_broadcast([P, 16, 16]), ALU.subtract).then_inc(S("cmp_s_ready"), 1)
            dve.wait_ge(S("cmp_exp"), 1)
            V_.did(dve.tensor_reduce(csm, ce, AX.X, ALU.add))
            V_.sync()
            V_.did(dve.reciprocal(crc, csm))
            V_.sync()
            crc2 = crc.rearrange("p (t h) -> p t h", t=2)
            V_.did(tt(crc2, crc2, gate[:, :, 0:8], ALU.mult))
            V_.sync()
            V_.did(tt(crc2, crc2, cst_("rowvalid").unsqueeze(2).to_broadcast([P, 2, 8]), ALU.mult))
            V_.sync()
            tt(ce, ce, crc.unsqueeze(2).to_broadcast([P, 16, 16]), ALU.mult).then_inc(S("cmp_p_ready"), 1)
            dve.wait_ge(S("z_silu"), 1)
            await_read(dve, "O", "y3")
            tt(y_tok, y_tok, z, ALU.mult).then_inc(S("y_gated"), 1)

            def gm_copy(i):
                b, _n = BANK[("gm", i)]
                channel_major(("gm", i), area[:, gm_at[2 * i] * 256:gm_at[2 * i] * 256 + 512]
                              .rearrange("p (a t) -> p a t", a=2))

            ahead(("gm", 0))
            await_read(dve, "O", "kc")
            gm_copy(0)
            dve.wait_ge(S("y_root"), 1)
            V_.did(dve.reciprocal(ssy, ry))
            V_.sync()
            yv = y_tok.rearrange("p t (g c) -> p (t g) c", g=4)
            tt(yv, yv, ssy.rearrange("p t g -> p (t g)").unsqueeze(2).to_broadcast([P, 8, 256]), ALU.mult)\
                .then_inc(S("y_normed"), 1)
            gm_copy(1)
            nw = prm_("ssm_norm")
            for k in range(KC):
                dve.wait_ge(S("y_hi"), 4 + (k | 1) + 1)
                ins = stt(a_lo[:, 8 + k, :], (ps, pt)[k // 4][:, (k // 2) % 2, (k % 2) * T:(k % 2 + 1) * T],
                          nw[:, k:k + 1], a_hi[:, 8 + k, :].bitcast(F32), ALU.mult, ALU.subtract)
                if k % 4 == 3:
                    read(ins, "ST"[k // 4])
            gm_copy(2)

            def maxima(idx, s_):
                m_, t_ = mx[idx % 2], s_[idx % 2]
                dve.tensor_reduce(m_[:, 0:2], t_[:, :, 0:128], AX.X, ALU.max, negate=True)
                dve.tensor_reduce(m_[:, 2:4], t_[:, :, 128:384], AX.X, ALU.max, negate=True)\
                   .then_inc(S("max_ready"), 1)

            def inverse_sums(idx):
                dve.wait_ge(S("exp_done"), 4 * (idx + 1))
                V_.did(dve.reciprocal(rcp[idx % 2], sums[idx % 2]))
                V_.sync()

            def scale_probs(idx, p_):
                for t in range(2):
                    cols = slice(0, 128) if t == 0 else slice(128, 384)
                    for hb in range(2):
                        c = t * 2 + hb
                        ins = dve.tensor_scalar(p_[idx % 2][:, hb, cols], p_[idx % 2][:, hb, cols],
                                                rcp[idx % 2][:, c:c + 1], None, ALU.mult)
                ins.then_inc(S("probs_ready"), 1)

            def nsa_soft(r):
                j = r // 2
                await_psum(dve, "S", f"n{r}")
                for hb in range(2):
                    ins = stt(sm[r % 2][:, hb, :], cst_("alibi"), SLOPES[hb * 4 + j], ps[:, hb, 0:384], ALU.mult, ALU.add)
                read(ins, "S")
                await_read(dve, "S", f"n{r}")
                maxima(r, sm)

            def nsa_probs(r):
                j, b = r // 2, r % 2
                inverse_sums(r)
                rv = rcp[r % 2].rearrange("p (t h) -> p t h", t=2)
                c = 8 * (b + 1) + j
                V_.did(tt(rv, rv, gate[:, :, c:c + 5:4], ALU.mult))
                V_.sync()
                scale_probs(r, pr)

            def nsa_out_lo(j):
                dve.wait_ge(S("y_hi"), 12 + j + 1)
                read(tt(a_lo[:, 20 + j, :], po[:, (j % 2) * T:(j % 2 + 1) * T], a_hi[:, 20 + j, :].bitcast(F32),
                        ALU.subtract), "O")

            nsa_soft(0)
            for r in range(8):
                nsa_probs(r)
                gm_copy(3 + r)
                if r < 7:
                    nsa_soft(r + 1)
                if r in (2, 4, 6):
                    nsa_out_lo(r // 2 - 1)
            gm_copy(11)
            nsa_out_lo(3)

            def mixed_lo(n):
                dve.wait_ge(S("mix_hi"), n + 1)
                stt(a_lo[:, n, :], mixt[n % 2][:, 0, :], 0.5, a_hi[:, n, :].bitcast(F32), ALU.mult, ALU.subtract)\
                    .then_inc(S("mix_lo"), 1)

            dve.wait_ge(S("gm_tanh"), 12)
            for n in range(8):
                u = ahead(("br", n))
                b, _n = BANK[("br", n)]
                dve.wait_ge(S("unit_done"), u + 1)
                m_ = mixt[n % 2]
                V_.did(stt(m_[:, 0, :], gm[n], 1.0, pj[b][:, 0:T], ALU.add, ALU.mult))
                stt(m_[:, 1, :], gm[8 + n], 1.0, pj[b][:, T:2 * T], ALU.add, ALU.mult).then_inc(S(f"pj_read{b}"), 1)
                stt(m_[:, 2, :], gm[16 + n], 1.0, ps[:, n % 2, 0:T], ALU.add, ALU.mult).then_inc(S("br_nsa_read"), 1)
                dve.wait_ge(S("br_nsa_read"), n + 1)
                V_.did(tt(m_[:, 0, :], m_[:, 0, :], m_[:, 1, :], ALU.add))
                V_.sync()
                tt(m_[:, 0, :], m_[:, 0, :], m_[:, 2, :], ALU.add).then_inc(S("mixed_ready"), 1)
                mixed_lo(n)

            def post(n, gname, ready, nxt=None):
                g = prm_(gname)
                for k in range(KC):
                    V_.did(tt(upd[k % 2], yT[:, k, :], rbc[:, :], ALU.mult))
                    V_.sync()
                    stt(xT[:, k, :], upd[k % 2], g[:, k:k + 1], xT[:, k, :], ALU.mult, ALU.add)\
                        .then_inc(S(ready), 1)
                    if nxt and k:
                        operand_lo(nxt[0], nxt[1], k - 1)
                if nxt:
                    operand_lo(nxt[0], nxt[1], KC - 1)

            for i in range(4):
                ahead(("wo", i))
            norm_tail(1)
            for i in range(4):
                await_value(dve, ("wo", i))
            post(1, "g_postmix1", "x_ready", (1, "g_ffn1"))
            norm_tail(2)

            fw = PCOLS["fw"][0]

            def up1(c, n, b, u_done):
                dve.wait_ge(S("unit_done"), u_done)
                tt(fx, two(pj[b]), rbc2, ALU.mult).then_inc(S(f"pj_read{b}"), 1)
                dve.wait_ge(S("tap2_done"), c * 2 + 2)
                for s_, signal in ((1, "ftap1_done"), (2, "ftaps_done")):
                    for m in range(2):
                        w = prm[:, bass.ds(c + (fw + (2 - s_) * 2 * UP1 + m * UP1), 1)]
                        stt(facc[:, m, s_:T], fx[:, m, 0:T - s_], w, facc[:, m, s_:T], ALU.mult, ALU.add)\
                            .then_inc(S(signal), 1)
                    if s_ == 1:
                        dve.wait_ge(S("ftap1_done"), c * 2 + 2)
                dve.wait_ge(S("ftaps_done"), c * 2 + 2)
                dve.wait_ge(S("gelu_done"), c + 1)
                tt(fu[:, 0, :], fg, facc[:, 1, :], ALU.mult).then_inc(S("fu_ready"), 1)

            def up1_lo(c, chunk):
                dve.wait_ge(S("u_hi"), c + 1)
                tt(a_lo[:, 8 + chunk, :], fu[:, 0, :], a_hi[:, 8 + chunk, :].bitcast(F32), ALU.subtract)\
                    .then_inc(S("u_lo"), 1)

            u0 = U_FFN1
            for c in range(2):
                ahead(u0 + c)
                up1(c, FFN1_BANK0[c], c, u0 + c + 1)
                up1_lo(c, c)

            def ffn1_step(i):
                m = i - 1
                split(u0 + 4, m)
                up1(i * 2, i + FFN1_BANK0[0], 0, m * 3 + (u0 + 3))
                up1_lo(i * 2, 0)
                split(u0 + 5, m)
                split(u0 + 6, m)
                up1(i * 2 + 1, i + FFN1_BANK0[1], 1, m * 3 + (u0 + 5))
                up1_lo(i * 2 + 1, 1)

            ffn1_step(1)
            with dve.Fori(2, DOWN1) as i:
                ffn1_step(i)
            ahead_of[0] = U_FFN1_END + 1

            def acc_copy(n):
                for q in range(4):
                    dve.wait_ge(S("sq_ready"), KC * n + 2 * q + 2)
                    dve.tensor_copy(yT[:, 2 * q:2 * q + 2, :], (ps, pt)[q // 2][:, q % 2, :]
                                    .rearrange("p (a t) -> p a t", a=2)).then_inc(S("acc_copied"), 1)

            ahead(U_FFN1_END - 1)
            acc_copy(3)
            norm_tail(3)
            dve.wait_ge(S("acc_copied"), 4)
            post(3, "g_postffn1", "x_ready", (2, "g_mix2"))

            dve.wait_ge(S("ws_hi"), 2)
            o2 = PCOLS["ws2"][0]
            tt(ws_lo[:, 0:64], prm[:, o2:o2 + 64], ws_hi[:, 0:64].bitcast(F32), ALU.subtract)\
                .then_inc(S("ws_ready"), 1)
            lv = prm_("lam").rearrange("p (a b d) -> p a b d", a=2, b=2)
            lt_ = lamt.rearrange("p (a d) -> p a d", a=2)
            V_.did(tt(lt_, lv[:, :, 0, :], lv[:, :, 1, :], ALU.mult))
            V_.sync()
            dve.tensor_reduce(lamv[:, 0:2], lt_, AX.X, ALU.add).then_inc(S("lam_sums"), 1)
            norm_tail(4)
            channel_major(("dq", 0), dq[:, 0:2, :], 64.0 ** -0.5)
            await_read(dve, "O", "flog")
            tt(fl, fl, prm_("b_f").unsqueeze(1).to_broadcast([P, 2, 8]), ALU.add).then_inc(S("flx_ready"), 1)
            dve.wait_ge(S("lam_exp"), 1)
            V_.did(stt(lamv[:, 4:5], lamv[:, 2:3], LAMBDA_INIT, lamv[:, 3:4], ALU.add, ALU.subtract))
            V_.sync()
            V_.did(dve.tensor_scalar(lamv[:, 5:6], lamv[:, 4:5], -1.0, None, ALU.mult))
            V_.sync()
            V_.did(stt(lamv[:, 6:7], lamv[:, 4:5], 1.0, lamv[:, 5:6], ALU.max, ALU.max))
            V_.sync()
            V_.did(dve.reciprocal(lm[:, 0:1], lamv[:, 6:7]))
            V_.sync()
            tt(lm[:, 1:2], lamv[:, 5:6], lm[:, 0:1], ALU.mult)
            stt(lm[:, 2:3], lm[:, 0:1], EPS, lm[:, 0:1], ALU.mult, ALU.mult).then_inc(S("lm_ready"), 1)
            channel_major(("dq", 1), dq[:, 2:4, :], 64.0 ** -0.5)
            dve.wait_ge(S("lfe_ready"), 1)
            stt(lf, fl, 0.0, lf_e, ALU.min, ALU.subtract).then_inc(S("lf_ready"), 1)
            for i in range(2):
                channel_major(("dk", i), dk[:, 2 * i:2 * i + 2, :])
            ahead(("dv", 1))
            channel_major(("fq", 0), fq[:, 0:2, :], 64.0 ** -0.5)

            def d_soft(h):
                await_psum(dve, "S", f"d{h}")
                dve.wait_ge(S("t5_ready"), 8 * 16)
                read(tt(sm2[h % 2], ps[:, :, 0:384], t5[:, h, :].unsqueeze(1).to_broadcast([P, 2, 384]), ALU.add), "S")
                await_read(dve, "S", f"d{h}")
                maxima(8 + h, sm2)

            def d_probs(h):
                idx = 8 + h
                inverse_sums(idx)
                if h == 0:
                    dve.wait_ge(S("lm_ready"), 1)
                rv = rcp[h % 2].rearrange("p (t m) -> p t m", t=2)
                V_.did(tt(rv, rv, lm[:, 0:2].unsqueeze(1).to_broadcast([P, 2, 2]), ALU.mult))
                V_.sync()
                p_, r_ = pr2[h % 2], rcp[h % 2]
                halves = (slice(0, 128), slice(128, 384))
                for t, cols in enumerate(halves):
                    V_.did(dve.tensor_scalar(p_[:, 0, cols], p_[:, 0, cols], r_[:, 2 * t:2 * t + 1], None, ALU.mult))
                V_.sync()
                for t, cols in enumerate(halves):
                    ins = stt(p_[:, 0, cols], p_[:, 1, cols], r_[:, 2 * t + 1:2 * t + 2], p_[:, 0, cols],
                              ALU.mult, ALU.add)
                ins.then_inc(S("probs_ready"), 1)

            d_soft(0)
            for h, n in enumerate((("fq", 1), ("fk", 0), ("fk", 1), ("fv", 0))):
                d_probs(h)
                if n[0] == "fv":
                    ahead(n)
                elif n[0] == "fq":
                    channel_major(n, fq[:, 2:4, :], 64.0 ** -0.5)
                else:
                    channel_major(n, fk[:, 2 * n[1]:2 * n[1] + 2, :])
                if h < 3:
                    d_soft(h + 1)
            ahead(("fv", 1))

            def f_soft(j):
                await_psum(dve, "S", f"f{j}")
                read(tt(sm2[j % 2], ps[:, :, 0:384], cst_("causal").unsqueeze(1).to_broadcast([P, 2, 384]), ALU.add),
                     "S")
                await_read(dve, "S", f"f{j}")
                maxima(12 + j, sm2)

            def f_out_lo(j):
                dve.wait_ge(S("mix2_hi"), j + 1)
                read(tt(a_lo[:, 12 + j, :], po[:, 0:T], a_hi[:, 12 + j, :].bitcast(F32), ALU.subtract), "O")

            f_soft(0)
            await_read(dve, "O", "odn")
            V_.did(dve.reciprocal(ods, ods))
            V_.sync()
            tt(dg8, ident.unsqueeze(1).to_broadcast([P, 8, P]), ods.unsqueeze(2).to_broadcast([P, 8, P]), ALU.mult)\
                .then_inc(S("dg8_ready"), 1)
            for j in range(4):
                inverse_sums(12 + j)
                scale_probs(12 + j, pr2)
                if j < 3:
                    f_soft(j + 1)
                if j >= 1:
                    f_out_lo(j - 1)
            await_psum(dve, "S", "odn")
            for q in range(2):
                ins = stt(odn[:, 2 * q:2 * q + 2, :], od[:, 2 * q:2 * q + 2, :], prm_("subln"),
                          ps[:, q, :].rearrange("p (a t) -> p a t", a=2), ALU.mult, ALU.mult)
                if q == 0:
                    ins.then_inc(S("odn_ready"), 1)
            read(ins, "S")
            f_out_lo(3)
            dve.wait_ge(S("mix2_hi"), 5)
            await_read(dve, "S", "odn")
            stt(a_lo[:, 8:12, :], odn, 1.0 - LAMBDA_INIT, a_hi[:, 8:12, :].bitcast(F32), ALU.mult, ALU.subtract)\
                .then_inc(S("mix2_lo"), 1)
            for i in range(4):
                ahead(("wo2", i))
            norm_tail(5)
            for i in range(4):
                await_value(dve, ("wo2", i))
            post(5, "g_postmix2", "x_ready", (3, "g_ffn2"))
            norm_tail(6)

            def up2(i, n, b, u_done):
                dve.wait_ge(S("unit_done"), u_done)
                tt(fx, two(pj[b]), rbc2, ALU.mult).then_inc(S(f"pj_read{b}"), 1)
                dve.wait_ge(S(f"pj_read{b}"), n + 1)
                stt(fu, fx, 0.0, fx, ALU.max, ALU.mult).then_inc(S("fu_ready"), 1)
                dve.wait_ge(S("u_hi"), i + UP1 + 1)
                tt(a_lo[:, 8:10, :], fu, a_hi[:, 8:10, :].bitcast(F32), ALU.subtract).then_inc(S("u_lo"), 1)

            v0 = U_FFN2
            ahead(v0)
            up2(0, FFN2_BANK0[0], 0, v0 + 1)

            def ffn2_step(m, last=False):
                for q in range(3):
                    b = (q + 1) % 3
                    split(v0 + 3 + 2 * q, m * 2)
                    up2(m * 3 + q + 1, m + (FFN2_BANK0[b] + (1 if b == 0 else 0)), b, m * 6 + (v0 + 2 + 2 * q))
                    if not (last and q == 2):
                        split(v0 + 4 + 2 * q, m * 2)

            ffn2_step(0)
            with dve.Fori(1, 4) as m:
                ffn2_step(m)
            ffn2_step(4, last=True)
            acc_copy(7)
            norm_tail(7)
            dve.wait_ge(S("acc_copied"), 8)
            post(7, "g_postffn2", "x_final")
            for h in range(2):
                dve.wait_ge(S("out_turned"), h + 1)
                dve.tensor_copy(x_tok[:, 1, h * 512:(h + 1) * 512], pt[:, h, :]).then_inc(S("out_ready"), 1)


def pack(v):
    def cols(w, c, n=256):
        return w[:, c:c + n].reshape(KC, P, n).transpose(1, 0, 2).reshape(P, KC * n)

    def parts(w, at):
        return cols(np.concatenate([w[:, a:a + n] for a, n in at], axis=1), 0)

    def down(w, m):
        return w[m * 256:(m + 1) * 256].reshape(2, P, D).transpose(1, 0, 2).reshape(P, 2 * D)

    w, w2 = v["w_in"][0], v["w_in_2"][0]
    up, dn, up2, dn2 = v["ffn_w_up"][0], v["ffn_w_down"][0], v["w_up_2"][0], v["w_down_2"][0]
    z0, xbc0, dt0, sb0, nq0 = 0, D, 3 * D, 3 * D + SSM_H, 3 * D + SSM_H + 1536
    kv0 = nq0 + 512
    gate0 = kv0 + 768
    gm0 = gate0 + 24
    nsa = v["w_br_nsa"][0].reshape(2, 4, 64, D).transpose(1, 0, 2, 3).reshape(512, D)
    br = np.concatenate([v["w_br_ssm"][0], v["w_br_sb"][0], nsa])

    def unit(name):
        kind, i = name
        if kind in ("sbq", "sbk", "sbv"):
            return cols(w, sb0 + 512 * ("sbq", "sbk", "sbv").index(kind) + 256 * i)
        if kind in ("xbc", "z", "gm"):
            return cols(w, {"xbc": xbc0, "z": z0, "gm": gm0}[kind] + 256 * i)
        if kind in ("kk", "kv", "vv"):
            a, b = {"kk": (2, 4), "kv": (0, 1), "vv": (3, 5)}[kind]
            return parts(w, [(kv0 + 128 * a, 128), (kv0 + 128 * b, 128)])
        if kind == "nq":
            return parts(w, [(nq0 + 64 * h, 64) for j in (2 * i, 2 * i + 1) for h in (j, 4 + j)])
        if kind == "br":
            return br[:, 128 * i:128 * (i + 1)].reshape(16, P, P).transpose(1, 0, 2).reshape(P, UNIT)
        if kind == "wo":
            return cols(v["w_out"][0], 256 * i)
        if kind == "wo2":
            return cols(v["w_out_2"][0], 256 * i)
        return cols(w2, 512 * ("dq", "dk", "dv", "fq", "fk", "fv").index(kind) + 256 * i)

    def up1(j):
        return parts(up, [(P * j, P), (FF1 + P * j, P)])

    units = [unit(n) for n in UNITS] + [up1(0), up1(1)]
    for i in range(1, DOWN1):
        units += [up1(2 * i), down(dn, i - 1), up1(2 * i + 1)]
    units += [down(dn, DOWN1 - 1)] + [unit(n) for n in UNITS2] + [cols(up2, 0)]
    for i in range(1, UP2):
        units += [cols(up2, 256 * i), down(dn2, i - 1)]
    units.append(down(dn2, DOWN2 - 1))
    stream = np.stack(units)

    prm = np.zeros((P, PW), np.float32)

    def put(name, a):
        o, n = PCOLS[name]
        prm[:a.shape[0], o:o + n] = a

    def spread(a):
        return a.reshape(-1, P).T

    for name, key in (("g_mix1", "pre_mix_norm"), ("g_postmix1", "post_mix_norm"), ("g_ffn1", "pre_ffn_norm"),
                      ("g_postffn1", "post_ffn_norm"), ("g_mix2", "ln_attn_pre_2"),
                      ("g_postmix2", "ln_attn_post_2"), ("g_ffn2", "ln_mlp_pre_2"),
                      ("g_postffn2", "ln_mlp_post_2"), ("cw", "ssm_conv_w"), ("cb", "ssm_conv_b"),
                      ("ssm_norm", "ssm_norm"), ("fw", "ffn_conv_w"), ("fb", "ffn_conv_b")):
        put(name, spread(v[key]))
    for name, key in (("dt_bias", "ssm_dt_bias"), ("a_log", "ssm_a_log"), ("ssm_d", "ssm_d"), ("b_f", "b_f_2")):
        put(name, np.broadcast_to(v[key].reshape(1, -1), (P, v[key].size)))
    put("pos", np.hstack([spread(v["cmp_pos_k"]), spread(v["cmp_pos_v"])]))
    put("w2", np.hstack([v["cmp_w2_k"][0], v["cmp_w2_v"][0]]))
    put("subln", v["subln_g_2"].reshape(P, 1))
    lam = np.concatenate([v[n].reshape(-1) for n in ("lam_q1_2", "lam_k1_2", "lam_q2_2", "lam_k2_2")])
    put("lam", np.broadcast_to(lam, (P, 256)))
    put("rel", np.concatenate([v["rel_bias_2"], np.full((1, 4), NEG, np.float32)]))
    put("ws1", cols(np.concatenate([w[:, dt0:dt0 + 16], w[:, gate0:gate0 + 24]], axis=1), 0, 40))
    put("ws2", cols(w2, 6 * 512, 8))
    cmpw = np.stack([v[n][0].reshape(16, P, 64).transpose(1, 0, 2) for n in ("cmp_w1_k", "cmp_w1_v")])
    return {"stream": stream, "params": prm, "consts": constants(), "cmpw": cmpw, "x_in": v["x"]}


def kernel(**inputs):
    import concourse.bacc as bacc
    from concourse.bass_utils import run_bass_kernel_spmd

    nc = bacc.Bacc("TRN2", target_bir_lowering=False, num_devices=1)
    arrays = {n: np.ascontiguousarray(a) for n, a in pack({k: np.asarray(a) for k, a in inputs.items()}).items()}
    aps = {n: nc.dram_tensor(n, a.shape, mybir.dt.from_np(a.dtype), kind="ExternalInput").ap()
           for n, a in arrays.items()}
    out = nc.dram_tensor("out", (1, T, D), F32, kind="ExternalOutput").ap()
    program(nc, aps["stream"], aps["params"], aps["consts"], aps["cmpw"], aps["x_in"], out)
    r = run_bass_kernel_spmd(nc, [arrays], core_ids=[0])
    return r.results[0]["out"]
```

```python
import math
from contextlib import ExitStack

import numpy as np

import concourse.bass as bass
from concourse import mybir

F32 = mybir.dt.float32
F32R = mybir.dt.float32r
ALU = mybir.AluOpType
ACT = mybir.ActivationFunctionType
AX = mybir.AxisListType

T, D, P = 256, 1024, 128
KC = D // P
UNIT = 2048
NEG = -1e30
EPS = 1e-6
SSM_H, SB_H, NSA_H, CMP_N = 16, 4, 8, 15
FF1, FF2 = 2816, 4096
UP1, DOWN1 = FF1 // P, FF1 // (2 * P)
UP2, DOWN2 = FF2 // (2 * P), FF2 // (2 * P)
WARM = (2, 6)
SLOTS = 3
LAMBDA_INIT = 0.8 - 0.6 * math.exp(0.0)
SLOPES = [2.0 ** (-8.0 * (h + 1) / NSA_H) for h in range(NSA_H)]

UNITS = ([("sbq", i) for i in range(2)] + [("sbk", i) for i in range(2)] + [("sbv", i) for i in range(2)]
         + [("xbc", i) for i in range(8)] + [("kk", 0), ("kv", 0), ("vv", 0), ("nq", 0), ("nq", 1)]
         + [("z", i) for i in range(4)] + [("gm", i) for i in range(12)] + [("br", i) for i in range(8)]
         + [("wo", i) for i in range(4)])
U_FFN1 = len(UNITS)
U_FFN1_END = U_FFN1 + UP1 + DOWN1
UNITS2 = ([(n, i) for i in range(2) for n in ("dq", "dk", "dv")]
          + [(n, i) for i in range(2) for n in ("fq", "fk")] + [("fv", i) for i in range(2)] + [("wo2", i) for i in range(4)])
U_FFN2 = U_FFN1_END + len(UNITS2)
N_UNITS = U_FFN2 + UP2 + DOWN2
UIDX = {name: i for i, name in enumerate(UNITS)}
UIDX.update({name: U_FFN1_END + i for i, name in enumerate(UNITS2)})

BANK, _uses = {}, [0, 0, 0]
for _n, _name in enumerate(UNITS):
    BANK[_name] = (_n % 3, _uses[_n % 3])
    _uses[_n % 3] += 1
FFN1_BANK0 = list(_uses)
_uses[0] += UP1 // 2
_uses[1] += UP1 // 2
for _n, _name in enumerate(UNITS2):
    BANK[_name] = (_n % 3, _uses[_n % 3])
    _uses[_n % 3] += 1
FFN2_BANK0 = list(_uses)

PCOLS, PW = {}, 0
for _name, _w in (("g_mix1", 8), ("g_postmix1", 8), ("g_ffn1", 8), ("g_postffn1", 8), ("g_mix2", 8),
                  ("g_postmix2", 8), ("g_ffn2", 8), ("g_postffn2", 8), ("cw", 64), ("cb", 16), ("ssm_norm", 8),
                  ("dt_bias", 16), ("a_log", 16), ("ssm_d", 16), ("fw", 132), ("fb", 44), ("pos", 32),
                  ("w2", 128), ("subln", 1), ("lam", 256), ("b_f", 8), ("rel", 4), ("ws1", 320), ("ws2", 64)):
    PCOLS[_name] = (PW, _w)
    PW += _w

CCOLS, CW = {}, 0
for _name, _w in (("ident", 128), ("le", 128), ("ones", 128), ("gt", 128), ("sbmask", 384), ("cbmask", 384),
                  ("causal", 384), ("alibi", 384), ("cmpbias", 256), ("rowvalid", 2), ("cmpmask", 8),
                  ("onehot", 384)):
    CCOLS[_name] = (CW, _w)
    CW += _w


def constants():
    c = np.zeros((P, CW), np.float32)
    p, i = np.arange(P)[:, None], np.arange(P)[None, :]

    def put(name, a):
        o, w = CCOLS[name]
        c[:a.shape[0], o:o + w] = a

    le, gt, lt = p <= i, p > i, p < i
    one = np.ones((P, P))
    put("ident", p == i)
    put("le", le)
    put("ones", one)
    put("gt", gt)
    put("sbmask", np.hstack([lt, one, lt]))
    put("cbmask", np.hstack([le, one, le]))
    dist = np.hstack([p - i, P + p - np.arange(T)[None, :]]).astype(np.float64)
    put("causal", np.where(dist >= 0, 0.0, NEG))
    put("alibi", np.where(dist >= 0, -dist, NEG))
    cmp_bias = np.full((P, 2, 2, 4, 16), NEG)
    for tb in range(2):
        for hb in range(2):
            for j in range(4):
                for n in range(CMP_N):
                    d = tb * P + np.arange(P) - (16 * n + 31)
                    cmp_bias[:, tb, hb, j, n] = np.where(d >= 0, -SLOPES[hb * 4 + j] * d, NEG)
    put("cmpbias", cmp_bias.reshape(P, -1))
    put("rowvalid", np.hstack([p >= 31, p >= 0]))
    mask = np.zeros((P, 4, 2))
    for q in range(P):
        mask[q, (q // 16) % 4, q // 64] = 1.0
    put("cmpmask", mask.reshape(P, 8))
    hot = np.zeros((33, 384))
    for m in range(383):
        d = 255 - m
        if d < 0:
            hot[32, m] = 1.0
        elif d < 16:
            hot[d, m] = 1.0
        else:
            hot[min(16 + int(math.log(d / 16) / math.log(8) * 16), 31), m] = 1.0
    put("onehot", hot)
    return c


def program(nc, stream, params, consts, cmpw, x_in, out):
    ctx = ExitStack()
    with ctx:
        sems = {}

        def S(name):
            if name not in sems:
                sems[name] = ctx.enter_context(nc.semaphore(name))
            return sems[name]

        def sb(name, shape, dt=F32):
            return ctx.enter_context(nc.sbuf_tensor(name, shape, dt))

        def pb(name, shape):
            return ctx.enter_context(nc.psum_tensor(name, shape, F32))

        w_raw = sb("w_raw", [P, SLOTS, UNIT])
        w_hi = sb("w_hi", [P, SLOTS, UNIT], F32R)
        w_lo = sb("w_lo", [P, SLOTS, UNIT], F32R)
        a_hi = sb("a_hi", [P, 24, T], F32R)
        a_lo = sb("a_lo", [P, 24, T], F32R)
        xT = sb("xT", [P, KC, T])
        prm = sb("prm", [P, PW])
        cst = sb("cst", [P, CW])
        area = sb("area", [P, 58 * 256])
        tiny = sb("tiny", [P, 1024])
        ws_hi = a_hi[:, 22:24, :].rearrange("p a b -> p (a b)")[:, 0:320]
        ws_lo = a_lo[:, 22:24, :].rearrange("p a b -> p (a b)")[:, 0:320]
        rbc = sb("rbc", [P, T])
        scratch = nc.dram_tensor("t5_rows", (4, P, 384), F32, kind="Internal").ap()

        pj = [pb(f"pj{i}", [P, 512]) for i in range(3)]
        ps = pb("ps", [P, 2, 512])
        pt = pb("pt", [P, 2, 512])
        po = pb("po", [P, 512])

        def V(kib, *dims):
            n = int(np.prod(dims))
            o = int(kib * 256)
            ap = area[:, o:o + n]
            if len(dims) == 1:
                return ap
            names = "abcd"[:len(dims)]
            return ap.rearrange(f"p ({' '.join(names)}) -> p {' '.join(names)}",
                                **dict(zip(names[1:], dims[1:])))

        _t = [0]

        def small(*dims):
            n = int(np.prod(dims))
            ap = tiny[:, _t[0]:_t[0] + n]
            _t[0] += n
            if len(dims) == 1:
                return ap
            names = "abcd"[:len(dims)]
            return ap.rearrange(f"p ({' '.join(names)}) -> p {' '.join(names)}",
                                **dict(zip(names[1:], dims[1:])))

        def prm_(name):
            o, w = PCOLS[name]
            return prm[:, o:o + w]

        def cst_(name):
            o, w = CCOLS[name]
            return cst[:, o:o + w]

        ident, ones, gt, le = cst_("ident"), cst_("ones"), cst_("gt"), cst_("le")
        o_le = CCOLS["le"][0]
        le_ones = cst[:, o_le:o_le + 256]
        ones_gt = cst[:, o_le + 128:o_le + 384]

        x_tok, sq = V(0, 2, D), V(8, KC, T)
        sbq, sbk, sbv = V(0, 4, T), V(4, 4, T), V(8, 2, 512)
        sb_l = [V(12, 2, 384), V(24, 2, 384)]
        sb_ls = [V(15, 2, 384), V(27, 2, 384)]
        sb_lk = [V(18, 2, 384), V(30, 2, 384)]
        sb_w = [V(21, 2, 384), V(33, 2, 384)]
        xbc = V(36, 16, T)
        xc = [V(52, 2, T), V(54, 2, T)]
        xs_tok, xdt = V(0, 2, D), V(8, 2, D)
        gdt, E = V(16, 2, 4, P), V(20, 4, 384)
        cmp_w1 = V(26, 2, 16, 64)
        nq, cb = V(34, 4, T), V(38, 4, 384)
        kk, cm, vv = V(52, 2, T), V(54, 2, T), V(56, 2, T)
        ck, ckp = V(44, 2, 2, P), V(46, 2, 2, 2 * P)
        z = V(8, 2, D)
        vc, pct, cmp_e, y_sq = V(46, 4, P), V(48, T), V(49, 2, P), V(50, T)
        sm = [V(16, 2, 384), V(19, 2, 384)]
        pr = [V(22, 2, 384), V(25, 2, 384)]
        ptr = [V(28, 2, 384), V(31, 2, 384)]
        gm_at = list(range(38, 46)) + list(range(8, 16)) + list(range(0, 8))
        gm = [V(k, T) for k in gm_at]
        mixt = [V(16, 3, T), V(19, 3, T)]
        yT, sqy = V(20, KC, T), V(28, KC, T)
        sq_ffn = V(36, KC, T)
        fx, facc, fg, fu = V(0, 2, T), V(4, 2, T), V(8, T), V(10, 2, T)
        upd = [V(16, T), V(17, T)]
        dq, dk, dv = V(0, 4, T), V(4, 4, T), V(8, 2, 512)
        fq, fk, fv = V(12, 4, T), V(16, 4, T), V(20, 2, 512)
        t5 = V(44, 4, 384)
        sm2 = [V(30, 2, 384), V(33, 2, 384)]
        pr2 = [V(36, 2, 384), V(39, 2, 384)]
        ptr2 = [V(24, 2, 384), V(27, 2, 384)]
        od, odsq, dg8, odn = V(50, 4, T), V(0, 4, T), V(4, 8, P), V(0, 4, T)
        lfle = [V(54, 2, 2, P), V(56, 2, 2, P)]
        t5_sb, narrow = V(12, 384), V(12, T)
        tap, conv_tap, conv_tap0 = V(14, 2, T), V(57, T), V(56, T)
        ssq, ssq_last = V(18, T), V(19, T)
        y_tok = x_tok

        rt, rcol, eps_t, warm = small(2), small(2), small(1), small(1)
        dgr = sb("dgr", [P, 2, P])
        small40 = small(2, 40)
        dtx, dt_, dta = small(2, 16), small(2, 16), small(2, 16)
        dt_e, ea = small(2, 16), small(16)
        gate = small(2, 24)
        ssy, ry = small(2, 4), small(2, 4)
        hid, hid_t = small(2, 32), small(2, 64)
        hrep = small(P)
        kct = small(16)
        vrep = small(64)
        cmx, csm, crc = small(16), small(16), small(16)
        mx = [small(4), small(4)]
        sums = [small(4), small(4)]
        rcp = [small(4), small(4)]
        lamt = small(128)
        lamv, lm = small(8), small(4)
        lf, lf_e, fl = small(2, 8), small(2, 8), small(2, 8)
        ods = small(8)
        assert _t[0] <= 1024

        class Order:

            def __init__(self, eng, name):
                self.eng, self.sem, self.n = eng, S(name), 0

            def did(self, ins):
                ins.then_inc(self.sem, 1)
                self.n = self.n + 1

            def sync(self):
                self.eng.wait_ge(self.sem, self.n)

        S_USE = ["x", "sb0", "sb1", "xs", "cb", "seg0", "seg1", "seg2", "seg3", "cmp", "yt"] \
            + [f"n{r}" for r in range(8)] + [f"d{r}" for r in range(4)] \
            + [f"f{r}" for r in range(4)] + ["odn"]
        T_USE = ["x", "sb0", "sb1", "xs", "cb", "seg0", "seg1", "seg2", "seg3", "cmp", "yt"] \
            + [f"n{r}" for r in range(8)] + [f"d{r}" for r in range(4)] + [f"f{r}" for r in range(4)]
        O_USE = ["norm0", "rbc0", "sb0", "sb1", "dt", "dt_tok", "y0", "y1", "y2", "y3", "hid", "kc"] \
            + [f"n{j}" for j in range(4)] + ["norm1", "rbc1", "norm2", "rbc2", "t5", "norm3", "rbc3", "norm4", "rbc4",
               "flog", "flog_tok", "d0", "d1", "odn", "f0", "f1", "f2", "f3", "norm5", "rbc5", "norm6", "rbc6",
               "norm7", "rbc7"]
        USE = {"S": S_USE, "T": T_USE, "O": O_USE}

        def claim(pe, region, name):
            k = USE[region].index(name)
            if k:
                pe.wait_ge(S(f"{region}_read"), k)

        def written(ins, region):
            ins.then_inc(S(f"{region}_written"), 1)

        def await_psum(eng, region, name):
            eng.wait_ge(S(f"{region}_written"), USE[region].index(name) + 1)

        def read(ins, region):
            ins.then_inc(S(f"{region}_read"), 1)

        def await_read(eng, region, name):
            eng.wait_ge(S(f"{region}_read"), USE[region].index(name) + 1)

        def await_value(eng, name):
            b, n = BANK[name]
            eng.wait_ge(S(f"pj_read{b}"), n + 1)

        block = ctx.enter_context(nc.Block())

        @block.sync
        def _(sp):
            x_rows = x_in.rearrange("b (tb p) d -> (b p) tb d", p=P)
            o_g, o_c = PCOLS["cw"][0], CCOLS["sbmask"][0]

            def first_load(u):
                sp.dma_start(w_raw[:, u, :], stream[u]).then_inc(S(f"w_loaded{u}"), 16)

            sp.dma_start(x_tok[:, 0, :], x_rows[:, 0, :]).then_inc(S("x_loaded0"), 16)
            sp.dma_start(cst[:, 0:o_c], consts[:, 0:o_c]).then_inc(S("base_loaded"), 16)
            sp.dma_start(x_tok[:, 1, :], x_rows[:, 1, :]).then_inc(S("x_loaded1"), 16)
            sp.dma_start(prm[:, 0:o_g], params[:, 0:o_g]).then_inc(S("gains_loaded"), 16)
            first_load(0)
            first_load(1)
            sp.dma_start(prm[:, o_g:PW], params[:, o_g:PW]).then_inc(S("prm_loaded"), 16)
            first_load(2)
            sp.dma_start(cst[:, o_c:CW], consts[:, o_c:CW]).then_inc(S("cst_loaded"), 16)
            rounds = N_UNITS // SLOTS
            with sp.Fori(1, rounds) as i:
                for r in range(SLOTS):
                    sp.wait_ge(S("w_hi_done"), i * SLOTS + (r - SLOTS + 1))
                    sp.wait_ge(S("w_lo_done"), i * SLOTS + (r - SLOTS + 1))
                    sp.dma_start(w_raw[:, r, :], stream[bass.ds(i * SLOTS + r, 1), :, :].rearrange("a p n -> (a p) n"))\
                      .then_inc(S(f"w_loaded{r}"), 16)
            for u in range(rounds * SLOTS, N_UNITS):
                sp.wait_ge(S("w_hi_done"), u - SLOTS + 1)
                sp.wait_ge(S("w_lo_done"), u - SLOTS + 1)
                sp.dma_start(w_raw[:, u % SLOTS, :], stream[u]).then_inc(S(f"w_loaded{u % SLOTS}"), 16)
            out_rows = out.rearrange("b (tb p) d -> (b p) tb d", p=P)
            for h in range(2):
                cols = slice(h * 512, (h + 1) * 512)
                sp.wait_ge(S(f"out_ready{h}"), 2)
                sp.dma_start(out_rows[:, :, cols], x_tok[:, :, cols]).then_inc(S("out_stored"), 16)
            sp.wait_ge(S("out_stored"), 32)

        @block.gpsimd
        def _(gp):
            G = Order(gp, "pool_order")

            def sum_squares(n, sq_t):
                for k in range(1, 6):
                    gp.wait_ge(S("sq_ready"), KC * n + k + 1)
                    ins = gp.tensor_tensor(ssq, sq_t[:, 0, :] if k == 1 else ssq, sq_t[:, k, :], ALU.add)
                    if k < 5:
                        G.did(ins)
                        G.sync()
                ins.then_inc(S("ssq_ready"), 1)

            def scale_y(n):
                await_read(gp, "O", f"rbc{n}")
                if n in (3, 7):
                    gp.wait_ge(S("acc_copied"), 4 if n == 3 else 8)
                else:
                    for i in range(4):
                        await_value(gp, ("wo" if n == 1 else "wo2", i))
                for k in range(2, KC):
                    gp.tensor_tensor(yT[:, k, :], yT[:, k, :], rbc[:, :], ALU.mult).then_inc(S("y_scaled"), 1)


            def conv_odd(i):
                await_value(gp, ("xbc", i))
                gp.wait_ge(S("conv_tap3"), 2 * i + 2)
                if i:
                    gp.wait_ge(S("conv_odd"), i)
                blk = 2 * i + 1
                for s_ in (1, 2, 3):
                    c = (3 - s_) * 16 + blk
                    if s_ == 3:
                        gp.wait_ge(S("tap3_product"), i + 1)
                        gp.tensor_tensor(xbc[:, blk, s_:T], xbc[:, blk, s_:T], conv_tap0[:, 0:T - s_], ALU.add)\
                            .then_inc(S("conv_odd"), 1)
                        continue
                    G.did(gp.tensor_scalar(conv_tap, xc[i % 2][:, 1, :], prm_("cw")[:, c:c + 1], None,
                                           ALU.mult))
                    G.sync()
                    G.did(gp.tensor_tensor(xbc[:, blk, s_:T], xbc[:, blk, s_:T], conv_tap[:, 0:T - s_], ALU.add))
                    G.sync()

            sum_squares(0, sq)
            gp.wait_ge(S("prm_loaded"), 16)
            for i in range(8):
                conv_odd(i)
            await_psum(gp, "O", "sb1")
            gp.dma_start(cmp_w1, cmpw.rearrange("v p c e -> p v c e")).then_inc(S("cmpw_loaded"), 16)
            for g in range(4):
                if g == 0:
                    gp.wait_ge(S("dta_ready"), 1)
                else:
                    gp.wait_ge(S("T_written"), USE["T"].index(f"seg{g - 1}") + 1)
                gp.tensor_tensor(gdt, gt.unsqueeze(1).unsqueeze(1).to_broadcast([P, 2, 4, P]),
                                 dta[:, :, 4 * g:4 * g + 4].unsqueeze(3).to_broadcast([P, 2, 4, P]),
                                 ALU.mult).then_inc(S("gdt_ready"), 1)
                if g == 0:
                    gp.wait_ge(S("xdt_ready"), 2)
                    gp.tensor_tensor(xs_tok.rearrange("p t (h c) -> p t h c", h=SSM_H),
                                 xs_tok.rearrange("p t (h c) -> p t h c", h=SSM_H),
                                 prm_("ssm_d").unsqueeze(1).unsqueeze(3).to_broadcast([P, 2, SSM_H, 64]),
                                 ALU.mult).then_inc(S("xd_ready"), 1)
            for n in range(8):
                m_ = mixt[n % 2]
                gp.wait_ge(S("br_ssm_read"), n + 1)
                await_value(gp, ("br", n))
                G.did(gp.tensor_tensor(m_[:, 0, :], m_[:, 0, :], m_[:, 1, :], ALU.add))
                G.sync()
                gp.wait_ge(S("br_nsa_read"), n + 1)
                gp.tensor_tensor(m_[:, 0, :], m_[:, 0, :], m_[:, 2, :], ALU.add).then_inc(S("mixed_ready"), 1)
            sum_squares(1, sqy)
            scale_y(1)
            sum_squares(2, sq_ffn)

            def value_taps(c):
                gp.wait_ge(S("value_tap2"), c + 1)
                for s_ in (1, 2):
                    gp.wait_ge(S("tap_product"), c * 2 + s_)
                    if s_ == 2:
                        gp.wait_ge(S("value_tap1"), c + 1)
                    gp.tensor_tensor(facc[:, 1, s_:T], facc[:, 1, s_:T], tap[:, s_ - 1, 0:T - s_], ALU.add)\
                        .then_inc(S("value_tap1" if s_ == 1 else "value_taps"), 1)

            value_taps(0)
            await_read(gp, "O", "t5")
            gp.dma_start(scratch, t5_sb[0:4, :].unsqueeze(1).to_broadcast([4, P, 384])).then_inc(S("t5_scratch"), 16)
            with gp.Fori(1, UP1) as c:
                value_taps(c)
            sum_squares(3, sqy)
            scale_y(3)
            sum_squares(4, sq_ffn)
            gp.wait_ge(S("t5_scratch"), 16)
            gp.dma_start(t5[:, :, 128:384], bass.AP(scratch.tensor, 127, [[383, P], [P * 384, 4], [1, 256]]))\
              .then_inc(S("t5_ready"), 16)
            gp.dma_start(t5[:, :, 0:128], bass.AP(scratch.tensor, 255, [[383, P], [P * 384, 4], [1, 128]]))\
              .then_inc(S("t5_ready"), 16)
            for j in range(4):
                if j == 0:
                    gp.wait_ge(S("lf_ready"), 1)
                elif j >= 2:
                    gp.wait_ge(S("S_written"), USE["S"].index(f"f{j - 2}") + 1)
                gp.tensor_tensor(lfle[j % 2], le.unsqueeze(1).unsqueeze(1).to_broadcast([P, 2, 2, P]),
                                 lf[:, :, 2 * j:2 * j + 2].unsqueeze(3).to_broadcast([P, 2, 2, P]),
                                 ALU.mult).then_inc(S("lfle_ready"), 1)
            sum_squares(5, sqy)
            scale_y(5)
            sum_squares(6, sq_ffn)
            sum_squares(7, sqy)
            scale_y(7)

        @block.tensor
        def _(pe):
            def unit_ready(u):
                pe.wait_ge(S("w_hi_done"), u + 1)
                pe.wait_ge(S("w_lo_done"), u + 1)

            def bank_free(b, n):
                if isinstance(n, int) and n == 0:
                    return
                pe.wait_ge(S(f"pj_read{b}"), n)

            def three(out_, wh, wl, ah, al, first, last, weights_left=True):
                a, b = ((wh, ah), (wl, al)) if weights_left else ((ah, wh), (al, wl))
                pe.matmul(out_, a[0], a[1], start=first, stop=False)
                if weights_left:
                    pe.matmul(out_, wh, al, start=False, stop=False)
                    return pe.matmul(out_, wl, ah, start=False, stop=last)
                pe.matmul(out_, ah, wl, start=False, stop=False)
                return pe.matmul(out_, al, wh, start=False, stop=last)

            def unit_b(slot, b, koff=0, gate=None):
                for nb in range(2):
                    for k in range(KC):
                        if gate and nb == 0:
                            gate(k)
                        c = k * 256 + nb * P
                        mm = three(pj[b][:, nb * T:(nb + 1) * T], w_hi[:, slot, c:c + P], w_lo[:, slot, c:c + P],
                                   a_hi[:, koff + k, :], a_lo[:, koff + k, :], k == 0, k == KC - 1)
                mm.then_inc(S("unit_done"), 1)

            def unit_a(slot, b):
                for tb in range(2):
                    for k in range(KC):
                        c = k * 256
                        mm = three(pj[b][:, tb * 256:(tb + 1) * 256], w_hi[:, slot, c:c + 256],
                                   w_lo[:, slot, c:c + 256], a_hi[:, k, tb * P:(tb + 1) * P],
                                   a_lo[:, k, tb * P:(tb + 1) * P], k == 0, k == KC - 1, weights_left=False)
                mm.then_inc(S("unit_done"), 1)

            def run_unit(name, gate=None):
                u = UIDX[name]
                b, n = BANK[name]
                unit_ready(u)
                bank_free(b, n)
                if name[0] in ("sbv", "vv", "z", "dv", "fv"):
                    unit_a(u % SLOTS, b)
                else:
                    unit_b(u % SLOTS, b, 8 if name[0] == "wo2" else 0, gate)

            def transpose(out_, in_):
                return pe.transpose(out_, in_, ident[0:in_.shape[0], 0:in_.shape[0]])

            def stat(n):
                claim(pe, "O", f"norm{n}")
                for part, (tile, ready) in enumerate(((ssq, "ssq_ready"), (ssq_last, "ssq_last_ready"))):
                    pe.wait_ge(S(ready), n + 1)
                    for tb in range(2):
                        mm = pe.matmul(po[:, tb:tb + 1], tile[:, tb * P:(tb + 1) * P], ones[:, 0:1],
                                       start=(part == 0 and tb == 0), stop=(part == 1), skip_group_check=True)
                written(mm, "O")

            def spread(n):
                claim(pe, "O", f"rbc{n}")
                pe.wait_ge(S("diag_ready"), n + 1)
                written(pe.matmul(po[:, 256:512], ones, dgr[:, :, :], start=True, stop=True), "O")

            def keep_warm(b, n=1):
                for _i in range(n):
                    pe.matmul(pj[b][:, 0:256], ident, le_ones, start=True, stop=True)

            def operand_gate(n):
                def gate(k):
                    pe.wait_ge(S("opnd_hi"), KC * n + k + 1)
                    pe.wait_ge(S("opnd_lo"), KC * n + k + 1)
                return gate

            def first_pair(n, u, b):
                gate = operand_gate(n // 2)
                for j in range(2):
                    unit_ready(u + j)
                    bank_free(b[j][0], b[j][1])
                for k in range(KC):
                    gate(k)
                    for j in range(2):
                        slot = (u + j) % SLOTS
                        for nb in range(2):
                            mm = three_acc(pj[b[j][0]][:, nb * T:(nb + 1) * T], slot, k * 256 + nb * P, k,
                                           k == 0 and nb == 0, k == KC - 1)
                        if k == KC - 1:
                            mm.then_inc(S("unit_done"), 1)
                    if k == 6:
                        stat(n)
                spread(n)

            def three_acc(o_, slot, c, k, first, last):
                pe.matmul(o_, w_hi[:, slot, c:c + P], a_hi[:, k, :], start=first, stop=False, skip_group_check=True)
                pe.matmul(o_, w_hi[:, slot, c:c + P], a_lo[:, k, :], start=False, stop=False, skip_group_check=True)
                return pe.matmul(o_, w_lo[:, slot, c:c + P], a_hi[:, k, :], start=False, stop=last,
                                 skip_group_check=True)

            pe.wait_ge(S("base_loaded"), 16)
            claim(pe, "S", "x")
            for tb in range(2):
                pe.wait_ge(S(f"x_loaded{tb}"), 16)
                for k in range(KC):
                    o = (k % 2) * T + tb * P
                    mm = transpose((ps, pt)[k // 4][:, (k // 2) % 2, o:o + P], x_tok[:, tb, k * P:(k + 1) * P])
                    if tb == 1 and k == 3:
                        written(mm, "S")
            written(mm, "T")

            def scores(q, kT_, o, kpart=slice(0, P)):
                pe.matmul(o[:, 0:128], q[:, 0:P], kT_[:, 0:P], start=True, stop=True)
                return pe.matmul(o[:, 128:384], q[:, P:T], kT_[:, 0:T], start=True, stop=True)

            def turn(src, region_bank):
                transpose(region_bank[:, 0:128], src[:, 0:128])
                transpose(region_bank[:, 128:256], src[:, 128:256])
                return transpose(region_bank[:, 256:384], src[:, 256:384])

            def weigh(o, v0, v1, p, first=True, last=True):
                pe.matmul(o, v0, p[:, 0:256], start=first, stop=last, skip_group_check=True)
                return pe.matmul(o[:, 128:256], v1, p[:, 256:384], start=False, stop=last, skip_group_check=True)

            def narrow_products(n):
                for k in range(KC):
                    mm = three(po[0:n, 0:T], ws_hi[:, k * n:(k + 1) * n], ws_lo[:, k * n:(k + 1) * n],
                               a_hi[:, k, :], a_lo[:, k, :], k == 0, k == KC - 1)
                written(mm, "O")

            def narrow_turn(use, n):
                claim(pe, "O", use)
                await_read(pe, "O", "dt" if n == 40 else "flog")
                for tb in range(2):
                    mm = transpose(po[:, tb * 64:tb * 64 + n], narrow[0:n, tb * P:(tb + 1) * P])
                written(mm, "O")

            def sb_scores(p):
                claim(pe, "S", f"sb{p}")
                for hh in range(2):
                    h = 2 * p + hh
                    pe.matmul(ps[:, hh, 0:256], sbk[:, h, 0:P], sbq[:, h, :], start=True, stop=True)
                    mm = pe.matmul(ps[:, hh, 256:384], sbk[:, h, P:T], sbq[:, h, P:T], start=True, stop=True)
                written(mm, "S")

            def sb_later(p):
                claim(pe, "T", f"sb{p}")
                pe.wait_ge(S("sb_lk_ready"), p + 1)
                for hh in range(2):
                    pe.matmul(pt[:, hh, 0:256], gt, sb_lk[p][:, hh, 0:256], start=True, stop=True)
                    pe.matmul(pt[:, hh, 128:256], ones, sb_lk[p][:, hh, 256:384], start=False, stop=True,
                              skip_group_check=True)
                    mm = pe.matmul(pt[:, hh, 256:384], gt, sb_lk[p][:, hh, 256:384], start=True, stop=True)
                written(mm, "T")

            def sb_apply(p):
                claim(pe, "O", f"sb{p}")
                pe.wait_ge(S("sb_w_ready"), p + 1)
                for hh in range(2):
                    h = 2 * p + hh
                    mm = weigh(po[:, hh * T:(hh + 1) * T], sbv[:, 0, h * P:(h + 1) * P],
                               sbv[:, 1, h * P:(h + 1) * P], sb_w[p][:, hh, :])
                written(mm, "O")

            run_unit(("sbq", 0), operand_gate(0))
            stat(0)
            run_unit(("sbq", 1))
            spread(0)
            for n in (("sbk", 0), ("sbk", 1), ("sbv", 0), ("sbv", 1), ("xbc", 0)):
                run_unit(n)
            for n in (("sbq", 0), ("sbq", 1), ("sbk", 0), ("sbk", 1)):
                await_value(pe, n)
            sb_scores(0)
            run_unit(("xbc", 1))
            run_unit(("xbc", 2))
            sb_later(0)
            sb_scores(1)
            run_unit(("xbc", 3))
            await_value(pe, ("sbv", 0))
            await_value(pe, ("sbv", 1))
            sb_apply(0)
            run_unit(("xbc", 4))
            sb_later(1)
            run_unit(("xbc", 5))
            sb_apply(1)
            run_unit(("xbc", 6))

            claim(pe, "O", "dt")
            pe.wait_ge(S("ws_ready"), 1)
            narrow_products(40)
            run_unit(("xbc", 7))
            pe.wait_ge(S("xbc_silu"), 2)
            claim(pe, "S", "xs")
            claim(pe, "T", "xs")
            for q in range(4):
                for m in range(4):
                    blk = (q % 2) * 4 + m
                    mm = transpose((ps, pt)[q // 2][:, q % 2, m * P:(m + 1) * P],
                                   xbc[:, blk, (q // 2) * P:(q // 2 + 1) * P])
                if q == 1:
                    written(mm, "S")
            written(mm, "T")
            run_unit(("kk", 0))
            narrow_turn("dt_tok", 40)
            run_unit(("kv", 0))
            claim(pe, "T", "cb")
            claim(pe, "S", "cb")
            pe.wait_ge(S("xbc_silu"), 4)
            for g in range(4):
                mm = pe.matmul(pt[:, g // 2, (g % 2) * T:(g % 2 + 1) * T], xbc[:, 8 + g, 0:P], xbc[:, 12 + g, :],
                               start=True, stop=True)
            written(mm, "T")
            for g in range(4):
                mm = pe.matmul(ps[:, 0, g * P:(g + 1) * P], xbc[:, 8 + g, P:T], xbc[:, 12 + g, P:T],
                               start=True, stop=True)
            written(mm, "S")

            def seg(g):
                claim(pe, "S", f"seg{g}")
                claim(pe, "T", f"seg{g}")
                pe.wait_ge(S("gdt_ready"), g + 1)
                for m in range(4):
                    bank = (ps, pt)[m // 2][:, m % 2, :]
                    pe.matmul(bank[:, 0:256], gdt[:, 0, m, :], le_ones, start=True, stop=True)
                    pe.matmul(bank[:, 128:256], dta[:, 1, 4 * g + m:4 * g + m + 1].to_broadcast([P, P]), le,
                              start=False, stop=True, skip_group_check=True)
                    mm = pe.matmul(bank[:, 256:384], gdt[:, 1, m, :], le, start=True, stop=True)
                    if m == 1:
                        written(mm, "S")
                written(mm, "T")

            def ssm_y(g):
                claim(pe, "O", f"y{g}")
                pe.wait_ge(S("ssm_w_ready"), 2 * (g + 1))
                if g == 0:
                    pe.wait_ge(S("xdt_ready"), 2)
                for m in range(4):
                    c = (4 * g + m) * 64
                    pe.matmul(po[:, m * 64:(m + 1) * 64], E[:, m, 0:128], xdt[:, 0, c:c + 64], start=True, stop=True)
                    pe.matmul(po[:, 256 + m * 64:256 + (m + 1) * 64], E[:, m, 128:256], xdt[:, 0, c:c + 64],
                              start=True, stop=False)
                    mm = pe.matmul(po[:, 256 + m * 64:256 + (m + 1) * 64], E[:, m, 256:384], xdt[:, 1, c:c + 64],
                                   start=False, stop=True)
                written(mm, "O")

            seg(0)
            for g, n in enumerate((("vv", 0), ("nq", 0), ("nq", 1), ("z", 0))):
                run_unit(n)
                ssm_y(g)
                if g < 3:
                    seg(g + 1)
            run_unit(("z", 1))

            claim(pe, "O", "hid")
            pe.wait_ge(S("prm_loaded"), 16)
            pe.wait_ge(S("ckp_ready"), 4)
            pe.wait_ge(S("cmpw_loaded"), 16)
            for v in range(2):
                for c in range(16):
                    src = ckp[:, c // 8, v, :].rearrange("p (g n c) -> p g n c", g=2, c=8)
                    rhs = src[:, :, 0:15, c] if c < 8 else src[:, :, 1:16, c - 8]
                    mm = pe.matmul(po[0:64, v * 64:v * 64 + 30], cmp_w1[:, v, c, :], rhs, start=(c == 0),
                                   stop=(c == 15))
            written(mm, "O")
            run_unit(("z", 2))
            claim(pe, "O", "kc")
            pe.wait_ge(S("hid_ready"), 1)
            o = PCOLS["w2"][0]
            pe.matmul(po[0:64, 0:32], prm[0:64, o:o + 64], hid[0:64, 0, :], start=True, stop=True)
            written(pe.matmul(po[:, 64:128], hrep[0:64, :], prm[0:64, o + 64:o + 128], start=True, stop=True), "O")
            run_unit(("z", 3))
            claim(pe, "S", "cmp")
            await_read(pe, "O", "kc")
            await_value(pe, ("nq", 0))
            await_value(pe, ("nq", 1))
            for tb in range(2):
                for hb in range(2):
                    for j in range(4):
                        mm = pe.matmul(ps[:, hb, tb * 64 + j * 16:tb * 64 + (j + 1) * 16],
                                       nq[hb * 64:hb * 64 + 64, j, tb * P:(tb + 1) * P],
                                       kct[hb * 64:hb * 64 + 64, :], start=True, stop=True)
            written(mm, "S")
            run_unit(("gm", 0))
            claim(pe, "T", "cmp")
            pe.wait_ge(S("cmp_p_ready"), 1)
            for tb in range(2):
                mm = transpose(pt[:, 0, tb * P:(tb + 1) * P], cmp_e[:, tb, :])
            written(mm, "T")
            run_unit(("gm", 1))
            run_unit(("gm", 2))
            claim(pe, "S", "yt")
            claim(pe, "T", "yt")
            pe.wait_ge(S("y_normed"), 1)
            for k in range(KC):
                for tb in range(2):
                    mm = transpose((ps, pt)[k // 4][:, (k // 2) % 2, (k % 2) * T + tb * P:(k % 2) * T + (tb + 1) * P],
                                   y_tok[:, tb, k * P:(k + 1) * P])
                if k == 3:
                    written(mm, "S")
            written(mm, "T")

            def nsa_scores(r):
                j, b = r // 2, r % 2
                claim(pe, "S", f"n{r}")
                if r == 0:
                    await_value(pe, ("kk", 0))
                for hb in range(2):
                    q = slice(hb * 64, hb * 64 + 64)
                    mm = scores(nq[q, j, :], kk[q, b, :], ps[:, hb, :])
                written(mm, "S")

            def round_turn(name, idx, probs):
                claim(pe, "T", name)
                pe.wait_ge(S("probs_ready"), idx + 1)
                for hb in range(2):
                    mm = turn(probs[:, hb, :], pt[:, hb, :])
                written(mm, "T")

            def nsa_apply(r):
                j, b = r // 2, r % 2
                o_ = po[:, (j % 2) * T:(j % 2 + 1) * T]
                if b == 0:
                    claim(pe, "O", f"n{j}")
                    if j == 0:
                        pe.wait_ge(S("cmp_v_ready"), 1)
                        await_read(pe, "T", "cmp")
                        await_value(pe, ("vv", 0))
                    pe.matmul(o_, vc[:, j, :], pct, start=True, stop=False, skip_group_check=True)
                await_read(pe, "T", f"n{r}")
                for hb in range(2):
                    c = b * P + hb * 64
                    mm = weigh(o_[hb * 64:(hb + 1) * 64, :], vv[:, 0, c:c + 64], vv[:, 1, c:c + 64],
                               ptr[r % 2][:, hb, :], first=False, last=(b == 1))
                if b == 1:
                    written(mm, "O")

            nsa_scores(0)
            run_unit(("gm", 3))
            for r in range(8):
                run_unit(("gm", 4 + r))
                round_turn(f"n{r}", r, pr[r % 2])
                if r < 7:
                    nsa_scores(r + 1)
                if r >= 1:
                    nsa_apply(r - 1)
            nsa_apply(7)

            for n in range(8):
                name = ("br", n)
                u = UIDX[name]
                b, k0 = BANK[name]
                unit_ready(u)
                bank_free(b, k0)
                if n == 0:
                    pe.wait_ge(S("y_hi"), 12)
                    await_read(pe, "T", "yt")
                    await_read(pe, "S", "yt")
                    await_read(pe, "O", "sb1")
                for part, (k_lo, k_hi) in enumerate(((0, 8), (8, 12), (12, 16))):
                    if part == 2 and n == 0:
                        pe.wait_ge(S("y_hi"), 16)
                        await_read(pe, "O", "n3")
                        claim(pe, "S", "d0")
                    elif part == 2 and n >= 2:
                        pe.wait_ge(S("br_nsa_read"), n - 1)
                    o_ = ps[:, n % 2, 0:T] if part == 2 else pj[b][:, part * T:(part + 1) * T]
                    for k in range(k_lo, k_hi):
                        mm = three(o_, w_hi[:, u % SLOTS, k * P:(k + 1) * P], w_lo[:, u % SLOTS, k * P:(k + 1) * P],
                                   a_hi[:, 8 + k, :], a_lo[:, 8 + k, :], k == k_lo, k == k_hi - 1)
                mm.then_inc(S("unit_done"), 1)

            def mixed_gate(k):
                pe.wait_ge(S("mix_hi"), k + 1)
                pe.wait_ge(S("mix_lo"), k + 1)

            def out_products(tag, n, gate=None):
                for i in range(4):
                    run_unit((tag, i), gate if i == 0 else None)
                stat(n)
                await_value(pe, (tag, 1))
                keep_warm(BANK[(tag, 1)][0], WARM[0])
                spread(n)
                keep_warm(BANK[(tag, 1)][0], WARM[1])

            out_products("wo", 1, mixed_gate)

            acc = [ps[:, 0, :], ps[:, 1, :], pt[:, 0, :], pt[:, 1, :]]

            def block_out(nb):
                return acc[nb // 2][:, (nb % 2) * T:(nb % 2 + 1) * T]

            def down(slot, chunk, first=False):
                for kc in range(2):
                    for nb in range(8):
                        mm = three_acc(block_out(nb), slot, kc * D + nb * P, chunk + kc,
                                       first and kc == 0 and nb % 2 == 0, False)
                mm.then_inc(S("unit_done"), 1)

            def last_down(slot, chunk, n):
                for nb in range(8):
                    for kc in range(2):
                        mm = three_acc(block_out(nb), slot, kc * D + nb * P, chunk + kc, False, kc == 1)
                    if nb % 2:
                        mm.then_inc(S("unit_done" if nb == 7 else "acc_bank_done"), 1)
                stat(n)
                keep_warm(2, WARM[0])
                spread(n)
                keep_warm(2, WARM[1])

            def up1(u, slot, parity, n, gate=None):
                unit_ready(u)
                bank_free(parity, n)
                unit_b(slot, parity, 0, gate)

            u0 = U_FFN1
            first_pair(2, u0, ((0, FFN1_BANK0[0]), (1, FFN1_BANK0[1])))
            claim(pe, "O", "t5")
            o = PCOLS["rel"][0]
            written(pe.matmul(po[0:4, 0:384], prm[0:33, o:o + 4], cst_("onehot")[0:33, :], start=True, stop=True), "O")

            def hidden_ready(n):
                pe.wait_ge(S("u_hi"), n)
                pe.wait_ge(S("u_lo"), n)

            def ffn1_step(i, odd, first=False):
                u = i * 3 + (u0 - 1)
                up1(u, (u0 + 2) % 3, 0, i + FFN1_BANK0[0])
                up1(u + 1, (u0 + 3) % 3, 1, i + FFN1_BANK0[1])
                unit_ready(u + 2)
                hidden_ready(i * 2)
                down((u0 + 4) % 3, 8 if odd else 10, first)

            claim(pe, "T", "d0")
            pe.wait_ge(S("br_nsa_read"), 8)
            ffn1_step(1, True, first=True)
            ffn1_step(2, False)
            with pe.Fori(1, DOWN1 // 2) as j:
                ffn1_step(j * 2 + 1, True)
                ffn1_step(j * 2 + 2, False)
            unit_ready(U_FFN1_END - 1)
            hidden_ready(UP1)
            last_down((U_FFN1_END - 1) % 3, 8, 3)

            first_pair(4, U_FFN1_END, (BANK[("dq", 0)], BANK[("dk", 0)]))
            claim(pe, "O", "flog")
            pe.wait_ge(S("ws_ready"), 2)
            narrow_products(8)
            run_unit(("dv", 0))
            narrow_turn("flog_tok", 8)

            def d_scores(h):
                claim(pe, "S", f"d{h}")
                if h == 0:
                    pe.wait_ge(S("acc_copied"), 4)
                if h % 2 == 0:
                    await_value(pe, ("dq", h // 2))
                    await_value(pe, ("dk", h // 2))
                for mp in range(2):
                    q = slice(mp * 64, mp * 64 + 64)
                    mm = scores(dq[q, h, :], dk[q, h, :], ps[:, mp, :])
                written(mm, "S")

            def d_turn(h):
                claim(pe, "T", f"d{h}")
                pe.wait_ge(S("probs_ready"), 8 + h + 1)
                written(turn(pr2[h % 2][:, 0, :], pt[:, 0, :]), "T")

            def d_apply(h):
                if h % 2 == 0:
                    claim(pe, "O", f"d{h // 2}")
                await_read(pe, "T", f"d{h}")
                if h % 2 == 0:
                    await_value(pe, ("dv", h // 2))
                mm = weigh(po[:, (h % 2) * T:(h % 2 + 1) * T], dv[:, 0, h * P:(h + 1) * P],
                           dv[:, 1, h * P:(h + 1) * P], ptr2[h % 2][:, 0, :])
                if h % 2 == 1:
                    written(mm, "O")

            def f_scores(j):
                claim(pe, "S", f"f{j}")
                if j % 2 == 0:
                    await_value(pe, ("fq", j // 2))
                    await_value(pe, ("fk", j // 2))
                pe.wait_ge(S("lfle_ready"), j + 1)
                for hb in range(2):
                    q = slice(hb * 64, hb * 64 + 64)
                    o_ = ps[:, hb, :]
                    ll = lfle[j % 2]
                    pe.matmul(o_[:, 0:128], fq[q, j, 0:P], fk[q, j, 0:P], start=True, stop=False)
                    pe.matmul(o_[:, 0:128], ll[:, 0, hb, :], gt, start=False, stop=True)
                    pe.matmul(o_[:, 128:384], fq[q, j, P:T], fk[q, j, 0:T], start=True, stop=False)
                    pe.matmul(o_[:, 128:384], ll[:, 1, hb, :], ones_gt, start=False, stop=True)
                    mm = pe.matmul(o_[:, 128:256], lf[:, 0, 2 * j + hb:2 * j + hb + 1].to_broadcast([P, P]), gt,
                                   start=False, stop=True, skip_group_check=True)
                written(mm, "S")

            def f_apply(j):
                claim(pe, "O", f"f{j}")
                await_read(pe, "T", f"f{j}")
                if j % 2 == 0:
                    await_value(pe, ("fv", j // 2))
                for hb in range(2):
                    c = (2 * j + hb) * 64
                    mm = weigh(po[hb * 64:(hb + 1) * 64, 0:T], fv[:, 0, c:c + 64], fv[:, 1, c:c + 64],
                               ptr2[j % 2][:, hb, :])
                written(mm, "O")

            def f_turn(j):
                round_turn(f"f{j}", 12 + j, pr2[j % 2])

            d_scores(0)
            run_unit(("dq", 1))
            d_turn(0)
            d_scores(1)
            run_unit(("dk", 1))
            d_apply(0)
            d_turn(1)
            run_unit(("dv", 1))
            d_apply(1)
            d_scores(2)
            run_unit(("fq", 0))
            d_turn(2)
            d_scores(3)
            run_unit(("fk", 0))
            d_apply(2)
            d_turn(3)
            run_unit(("fq", 1))
            d_apply(3)
            f_scores(0)
            run_unit(("fk", 1))
            f_turn(0)
            f_scores(1)
            claim(pe, "O", "odn")
            pe.wait_ge(S("od_sq_ready"), 1)
            for h in range(4):
                for tb in range(2):
                    mm = pe.matmul(po[:, 2 * h + tb:2 * h + tb + 1], odsq[:, h, tb * P:(tb + 1) * P], ones[:, 0:1],
                                   start=True, stop=True)
            written(mm, "O")
            run_unit(("fv", 0))
            f_turn(1)
            f_scores(2)
            run_unit(("fv", 1))
            f_apply(0)
            f_turn(2)
            f_scores(3)
            f_apply(1)
            claim(pe, "S", "odn")
            pe.wait_ge(S("dg8_ready"), 1)
            for q in range(2):
                mm = pe.matmul(ps[:, q, :], ones, dg8[:, 4 * q:4 * q + 4, :], start=True, stop=True)
            written(mm, "S")
            f_apply(2)
            f_turn(3)
            f_apply(3)
            pe.wait_ge(S("mix2_hi"), 4)
            pe.wait_ge(S("odn_hi"), 1)
            pe.wait_ge(S("odn_lo"), 1)
            await_read(pe, "O", "f3")
            out_products("wo2", 5)

            def up2(u, slot, b, n, gate=None):
                unit_ready(u)
                bank_free(b, n)
                unit_b(slot, b, 0, gate)

            v0 = U_FFN2
            first_pair(6, v0, ((0, FFN2_BANK0[0]), (1, FFN2_BANK0[1])))
            await_read(pe, "S", "odn")
            await_read(pe, "T", "f3")

            def down2(u, slot, i, chunk, first=False):
                unit_ready(u)
                hidden_ready(i + (UP1 + 1))
                down(slot, chunk, first)

            def ffn2_step(i, m, q, first=False):
                up2(i * 2 + (v0 - 2), (v0 - 2 + 2 * q) % 3, q, m + FFN2_BANK0[q])
                down2(i * 2 + (v0 - 1), (v0 - 1 + 2 * q) % 3, i - 2, 8 + 2 * ((q + 1) % 3), first)

            ffn2_step(2, 0, 2, first=True)
            with pe.Fori(1, UP2 // 3) as m:
                for q in range(3):
                    ffn2_step(m * 3 + q, m, q)
            ffn2_step(UP2 - 1, UP2 // 3, 0)
            down2(N_UNITS - 2, (N_UNITS - 2) % 3, UP2 - 2, 8 + 2 * ((UP2 - 2) % 3))
            unit_ready(N_UNITS - 1)
            hidden_ready(UP1 + UP2)
            last_down((N_UNITS - 1) % 3, 8, 7)
            pe.wait_ge(S("acc_copied"), 8)
            for k in range(KC):
                pe.wait_ge(S("x_final"), k + 1)
                for tb in range(2):
                    mm = transpose((ps, pt)[tb][:, k // 4, (k % 4) * P:(k % 4 + 1) * P], xT[:, k, tb * P:(tb + 1) * P])
                if k % 4 == 3:
                    mm.then_inc(S("out_turned"), 1)

        @block.scalar
        def _(act):
            A = Order(act, "act_order")

            def split(base, m=0):
                slot = base % SLOTS
                act.wait_ge(S(f"w_loaded{slot}"), (m + base // SLOTS + 1) * 16)
                if base >= SLOTS:
                    act.wait_ge(S("unit_done"), m * SLOTS + (base - SLOTS + 1))
                act.activation(w_hi[:, slot, :], w_raw[:, slot, :], ACT.Copy).then_inc(S("w_hi_done"), 1)

            ahead_of = [0]

            def ahead(name_or_u):
                u = UIDX[name_or_u] if isinstance(name_or_u, tuple) else name_or_u
                while ahead_of[0] <= min(u + 2, N_UNITS - 1):
                    split(ahead_of[0])
                    ahead_of[0] += 1
                return u

            def token_major(name, dst):
                u = ahead(name)
                b, _n = BANK[name]
                act.wait_ge(S("unit_done"), u + 1)
                for tb in range(2):
                    ins = act.activation(dst[:, tb, :], pj[b][:, tb * 256:(tb + 1) * 256], ACT.Copy,
                                         scale=rcol[:, tb:tb + 1])
                ins.then_inc(S(f"pj_read{b}"), 1)

            def operand(n, gname, sq_t):
                g = prm_(gname)
                for k in range(KC):
                    act.wait_ge(S("x_ready"), KC * n + k + 1)
                    act.activation(a_hi[:, k, :], xT[:, k, :], ACT.Copy, scale=g[:, k:k + 1]).then_inc(S("opnd_hi"), 1)
                    act.activation(sq_t[:, k, :], xT[:, k, :], ACT.Square).then_inc(S("sq_ready"), 1)

            def root(n):
                await_psum(act, "O", f"norm{n}")
                read(act.activation(rt, po[:, 0:2], ACT.Sqrt, bias=eps_t, scale=1.0 / D), "O")

            def warm_root():
                act.activation(warm, eps_t, ACT.Sqrt)

            act.wait_ge(S("eps_ready"), 1)
            warm_root()
            act.wait_ge(S("gains_loaded"), 16)
            split(0)
            ahead_of[0] = 1
            operand(0, "g_mix1", sq)
            split(1)
            ahead_of[0] = 2
            root(0)
            ahead(0)
            ahead(("sbk", 1))
            act.wait_ge(S("diag_ready"), 1)
            for i in range(2):
                token_major(("sbv", i), sbv[:, :, i * 256:(i + 1) * 256])

            def conv_first(i):
                ahead(("xbc", i))
                await_value(act, ("xbc", i))
                for m in range(2):
                    blk = 2 * i + m
                    act.activation(xbc[:, blk, :], xc[i % 2][:, m, :], ACT.Identity,
                                   bias=prm_("cb")[:, blk:blk + 1], scale=prm_("cw")[:, 48 + blk:49 + blk])\
                       .then_inc(S("conv_tap3"), 1)
                if i:
                    act.wait_ge(S("conv_odd"), i)
                act.activation(conv_tap0, xc[i % 2][:, 1, :], ACT.Copy, scale=prm_("cw")[:, blk:blk + 1])\
                   .then_inc(S("tap3_product"), 1)

            def sb_logs(p):
                await_psum(act, "S", f"sb{p}")
                A.did(act.activation(sb_l[p], ps[:, :, 0:384], ACT.Abs))
                A.sync()
                A.did(act.activation(sb_ls[p], sb_l[p], ACT.Exp, scale=-1.0))
                A.sync()
                act.activation(sb_l[p], sb_ls[p], ACT.Ln, bias=1.0).then_inc(S("sb_log_ready"), 1)

            def sb_exp(p):
                await_read(act, "T", f"sb{p}")
                act.activation(sb_w[p], sb_ls[p], ACT.Exp).then_inc(S("sb_exp_ready"), 1)

            def sb_hi(p):
                await_psum(act, "O", f"sb{p}")
                for hh in range(2):
                    act.activation(a_hi[:, 16 + 2 * p + hh, :], po[:, hh * T:(hh + 1) * T], ACT.Copy)\
                       .then_inc(S("y_hi"), 1)

            act.wait_ge(S("prm_loaded"), 16)
            conv_first(0)
            sb_logs(0)
            conv_first(1)
            conv_first(2)
            sb_exp(0)
            sb_logs(1)
            conv_first(3)
            sb_hi(0)
            conv_first(4)
            sb_exp(1)
            conv_first(5)
            sb_hi(1)
            o = PCOLS["ws1"][0]
            act.activation(ws_hi, prm[:, o:o + 320], ACT.Copy).then_inc(S("ws_hi"), 1)

            def silu(q):
                act.wait_ge(S("conv_even"), 2 * (q + 1))
                act.wait_ge(S("conv_odd"), 2 * (q + 1))
                act.activation(xbc[:, 4 * q:4 * q + 4, :], xbc[:, 4 * q:4 * q + 4, :], ACT.Silu)\
                   .then_inc(S("xbc_silu"), 1)

            silu(0)
            silu(1)
            conv_first(6)
            conv_first(7)
            for q in range(4):
                if q % 2 == 0:
                    await_psum(act, "ST"[q // 2], "xs")
                ins = act.activation(xs_tok[:, q // 2, (q % 2) * 512:(q % 2 + 1) * 512], (ps, pt)[q // 2][:, q % 2, :],
                                     ACT.Copy)
                if q % 2:
                    read(ins, "ST"[q // 2])
                else:
                    ins.then_inc(S("xs_half"), 1)
            ahead(("kk", 0))
            silu(2)
            await_psum(act, "O", "dt_tok")
            read(act.activation(small40, po[:, 0:128].rearrange("p (b x) -> p b x", b=2)[:, :, 0:40], ACT.Copy), "O")
            act.activation(ea, prm_("a_log"), ACT.Exp).then_inc(S("ea_ready"), 1)
            act.wait_ge(S("dtx_ready"), 1)
            A.did(act.activation(dt_e, dtx, ACT.Abs))
            A.sync()
            A.did(act.activation(dt_e, dt_e, ACT.Exp, scale=-1.0))
            A.sync()
            act.activation(dt_e, dt_e, ACT.Ln, bias=1.0).then_inc(S("dte_ready"), 1)
            silu(3)
            act.activation(gate, small40[:, :, 16:40], ACT.Tanh, scale=0.5).then_inc(S("gate_tanh"), 1)
            ahead(("kv", 0))
            await_value(act, ("kv", 0))
            await_psum(act, "S", "cb")
            for g in range(2):
                for half in range(2):
                    act.activation(ck[half * 64:half * 64 + 64, :, g, :], cm[g * 64:g * 64 + 64, :, half:T:2],
                                   ACT.Copy).then_inc(S("ck_ready"), 1)

            def decay(g):
                for region, bank, m in (("S", ps, 0), ("T", pt, 2)):
                    await_psum(act, region, f"seg{g}")
                    read(act.activation(E[:, m:m + 2, :], bank[:, :, 0:384], ACT.Exp), region)

            decay(0)
            token_major(("vv", 0), vv)
            decay(1)
            ahead(("nq", 0))
            decay(2)
            ahead(("nq", 1))
            decay(3)
            ahead(("z", 0))
            await_psum(act, "O", "y3")
            token_major(("z", 0), z[:, :, 0:256])
            token_major(("z", 1), z[:, :, 256:512])
            await_psum(act, "O", "hid")
            act.activation(hid_t[0:64, :, 0:30], po[0:64, 0:128].rearrange("p (v x) -> p v x", v=2)[:, :, 0:30],
                           ACT.Tanh, scale=0.5).then_inc(S("hid_tanh"), 1)
            token_major(("z", 2), z[:, :, 512:768])
            await_psum(act, "O", "kc")
            for hb in range(2):
                act.activation(kct[hb * 64:hb * 64 + 64, :], po[0:64, hb * 16:hb * 16 + 16], ACT.Copy, scale=0.5)
            read(act.activation(vrep, po[:, 64:128], ACT.Copy, scale=0.5), "O")
            token_major(("z", 3), z[:, :, 768:1024])
            for b in set(BANK[("z", i)][0] for i in range(4)):
                act.wait_ge(S(f"pj_read{b}"), max(BANK[("z", i)][1] for i in range(4) if BANK[("z", i)][0] == b) + 1)
            act.activation(z, z, ACT.Silu).then_inc(S("z_silu"), 1)
            act.wait_ge(S("cmp_s_ready"), 1)
            act.activation(cmp_e, cmp_e, ACT.Exp).then_inc(S("cmp_exp"), 1)
            ahead(("gm", 0))
            await_psum(act, "T", "cmp")
            read(act.activation(pct, pt[:, 0, 0:T], ACT.Copy), "T")
            act.wait_ge(S("y_gated"), 1)
            for tb in range(2):
                for g in range(4):
                    A.did(act.activation(y_sq, y_tok[:, tb, g * 256:(g + 1) * 256], ACT.Square,
                                         accum_out=ssy[:, tb, g:g + 1]))
                    A.sync()
            act.activation(ry, ssy, ACT.Sqrt, bias=eps_t, scale=1.0 / 256).then_inc(S("y_root"), 1)

            def gm_tanh(i):
                ahead(("gm", i))
                await_value(act, ("gm", i))
                pair = area[:, gm_at[2 * i] * 256:gm_at[2 * i] * 256 + 512]
                act.activation(pair, pair, ACT.Tanh, scale=0.5).then_inc(S("gm_tanh"), 1)

            gm_tanh(0)
            gm_tanh(1)
            nw = prm_("ssm_norm")
            for k in range(KC):
                if k % 4 == 0:
                    await_psum(act, "ST"[k // 4], "yt")
                act.activation(a_hi[:, 8 + k, :], (ps, pt)[k // 4][:, (k // 2) % 2, (k % 2) * T:(k % 2 + 1) * T],
                               ACT.Copy, scale=nw[:, k:k + 1]).then_inc(S("y_hi"), 1)
            gm_tanh(2)

            def exps(idx, s_, p_):
                act.wait_ge(S("max_ready"), idx + 1)
                for t in range(2):
                    for hb in range(2):
                        c = t * 2 + hb
                        cols = slice(0, 128) if t == 0 else slice(128, 384)
                        act.activation(p_[idx % 2][:, hb, cols], s_[idx % 2][:, hb, cols], ACT.Exp,
                                       bias=mx[idx % 2][:, c:c + 1], accum_out=sums[idx % 2][:, c:c + 1])\
                           .then_inc(S("exp_done"), 1)

            def nsa_out_hi(j):
                await_psum(act, "O", f"n{j}")
                act.activation(a_hi[:, 20 + j, :], po[:, (j % 2) * T:(j % 2 + 1) * T], ACT.Copy).then_inc(S("y_hi"), 1)

            gm_tanh(3)
            for r in range(8):
                exps(r, sm, pr)
                gm_tanh(4 + r)
                await_psum(act, "T", f"n{r}")
                read(act.activation(ptr[r % 2], pt[:, :, 0:384], ACT.Copy), "T")
                if r in (2, 4, 6):
                    nsa_out_hi(r // 2 - 1)
            nsa_out_hi(3)

            for n in range(8):
                ahead(("br", n))
                act.wait_ge(S("mixed_ready"), n + 1)
                act.activation(a_hi[:, n, :], mixt[n % 2][:, 0, :], ACT.Copy, scale=0.5).then_inc(S("mix_hi"), 1)

            def out_units(tag, n):
                warm_root()
                for i in range(4):
                    u = ahead((tag, i))
                    b, _n = BANK[(tag, i)]
                    act.wait_ge(S("unit_done"), u + 1)
                    for m in range(2):
                        act.activation(sqy[:, 2 * i + m, :], pj[b][:, m * T:(m + 1) * T], ACT.Square)\
                           .then_inc(S("sq_ready"), 1)
                    act.activation(yT[:, 2 * i:2 * i + 2, :], pj[b][:, :], ACT.Copy).then_inc(S(f"pj_read{b}"), 1)
                root(n)

            def acc_squares(u_last, n):
                warm_root()
                for k in range(KC):
                    if k == 6:
                        act.wait_ge(S("unit_done"), u_last + 1)
                    elif k % 2 == 0:
                        act.wait_ge(S("acc_bank_done"), (0 if n == 3 else 3) + k // 2 + 1)
                    act.activation(sqy[:, k, :], (ps, pt)[k // 4][:, (k // 2) % 2, (k % 2) * T:(k % 2 + 1) * T],
                                   ACT.Square).then_inc(S("sq_ready"), 1)
                root(n)

            out_units("wo", 1)
            operand(1, "g_ffn1", sq_ffn)
            ahead(U_FFN1)
            root(2)

            fw, fb = PCOLS["fw"][0], PCOLS["fb"][0]

            def up1_taps(c, b, n, first=False):
                act.wait_ge(S(f"pj_read{b}"), n + 1)
                for m in range(2):
                    act.activation(facc[:, m, :], fx[:, m, :], ACT.Identity,
                                   bias=prm[:, bass.ds(c + (fb + m * UP1), 1)],
                                   scale=prm[:, bass.ds(c + (fw + 4 * UP1 + m * UP1), 1)])\
                       .then_inc(S("gate_tap2" if m == 0 else "value_tap2"), 1)
                if not first:
                    act.wait_ge(S("value_taps"), c)
                for s_ in (1, 2):
                    act.activation(tap[:, s_ - 1, :], fx[:, 1, :], ACT.Copy,
                                   scale=prm[:, bass.ds(c + (fw + (2 - s_) * 2 * UP1 + UP1), 1)])\
                       .then_inc(S("tap_product"), 1)

            def up1_gelu(c):
                act.wait_ge(S("gate_taps"), c * 2 + 2)
                act.activation(fg, facc[:, 0, :], ACT.Gelu_apprx_tanh).then_inc(S("gelu_done"), 1)

            def up1_hi(c, chunk):
                act.wait_ge(S("fu_ready"), c + 1)
                act.activation(a_hi[:, chunk, :], fu[:, 0, :], ACT.Copy).then_inc(S("u_hi"), 1)

            u0 = U_FFN1
            for c in range(2):
                ahead(u0 + 1 + c)
                up1_taps(c, c, FFN1_BANK0[c], first=(c == 0))
                up1_gelu(c)
                up1_hi(c, 8 + c)
                if c == 0:
                    await_psum(act, "O", "t5")
                    read(act.activation(t5_sb[0:4, :], po[0:4, 0:384], ACT.Copy), "O")

            def ffn1_step(i, odd, first=False):
                m, chunk = i - 1, 10 if odd else 8
                if not first:
                    split(u0 + 4, m)
                split(u0 + 5, m)
                up1_taps(i * 2, 0, i + FFN1_BANK0[0])
                up1_gelu(i * 2)
                up1_hi(i * 2, chunk)
                split(u0 + 6, m)
                up1_taps(i * 2 + 1, 1, i + FFN1_BANK0[1])
                up1_gelu(i * 2 + 1)
                up1_hi(i * 2 + 1, chunk + 1)

            ffn1_step(1, True, first=True)
            ffn1_step(2, False)
            with act.Fori(1, DOWN1 // 2) as j:
                ffn1_step(j * 2 + 1, True)
                ffn1_step(j * 2 + 2, False)
            ahead_of[0] = U_FFN1_END + 1
            ahead(U_FFN1_END - 1)
            acc_squares(U_FFN1_END - 1, 3)
            operand(2, "g_mix2", sq_ffn)

            o2 = PCOLS["ws2"][0]
            act.activation(ws_hi[:, 0:64], prm[:, o2:o2 + 64], ACT.Copy).then_inc(S("ws_hi"), 1)
            ahead(("dq", 0))
            root(4)
            act.wait_ge(S("diag_ready"), 5)
            ahead(("dk", 0))
            act.wait_ge(S("lam_sums"), 1)
            act.activation(lamv[:, 2:4], lamv[:, 0:2], ACT.Exp).then_inc(S("lam_exp"), 1)
            token_major(("dv", 0), dv[:, :, 0:256])
            await_psum(act, "O", "flog_tok")
            read(act.activation(fl, po[:, 0:128].rearrange("p (b x) -> p b x", b=2)[:, :, 0:8], ACT.Copy), "O")
            act.wait_ge(S("flx_ready"), 1)
            A.did(act.activation(lf_e, fl, ACT.Abs))
            A.sync()
            A.did(act.activation(lf_e, lf_e, ACT.Exp, scale=-1.0))
            A.sync()
            act.activation(lf_e, lf_e, ACT.Ln, bias=1.0).then_inc(S("lfe_ready"), 1)

            def d_out(p):
                await_psum(act, "O", f"d{p}")
                read(act.activation(od[:, 2 * p:2 * p + 2, :], po[:, :], ACT.Copy), "O")

            def d_turned(h):
                await_psum(act, "T", f"d{h}")
                read(act.activation(ptr2[h % 2][:, 0, :], pt[:, 0, 0:384], ACT.Copy), "T")

            def f_turned(j):
                await_psum(act, "T", f"f{j}")
                read(act.activation(ptr2[j % 2], pt[:, :, 0:384], ACT.Copy), "T")

            def f_out_hi(j):
                await_psum(act, "O", f"f{j}")
                act.activation(a_hi[:, 12 + j, :], po[:, 0:T], ACT.Copy).then_inc(S("mix2_hi"), 1)

            ahead(("dq", 1))
            exps(8, sm2, pr2)
            d_turned(0)
            ahead(("dk", 1))
            exps(9, sm2, pr2)
            d_turned(1)
            token_major(("dv", 1), dv[:, :, 256:512])
            d_out(0)
            ahead(("fq", 0))
            exps(10, sm2, pr2)
            d_turned(2)
            ahead(("fk", 0))
            exps(11, sm2, pr2)
            d_turned(3)
            ahead(("fq", 1))
            d_out(1)
            await_read(act, "O", "d1")
            act.activation(odsq, od, ACT.Square).then_inc(S("od_sq_ready"), 1)
            ahead(("fk", 1))
            exps(12, sm2, pr2)
            f_turned(0)
            await_psum(act, "O", "odn")
            act.wait_ge(S("lm_ready"), 1)
            read(act.activation(ods, po[:, 0:8], ACT.Sqrt, bias=lm[:, 2:3], scale=1.0 / 128), "O")
            exps(13, sm2, pr2)
            token_major(("fv", 0), fv[:, :, 0:256])
            f_turned(1)
            exps(14, sm2, pr2)
            token_major(("fv", 1), fv[:, :, 256:512])
            f_out_hi(0)
            f_turned(2)
            f_out_hi(1)
            exps(15, sm2, pr2)
            f_out_hi(2)
            f_turned(3)
            act.wait_ge(S("odn_ready"), 1)
            await_read(act, "S", "odn")
            act.activation(a_hi[:, 8:12, :], odn, ACT.Copy, scale=1.0 - LAMBDA_INIT).then_inc(S("odn_hi"), 1)
            f_out_hi(3)
            out_units("wo2", 5)
            operand(3, "g_ffn2", sq_ffn)
            ahead(U_FFN2)
            root(6)

            def up2_hi(i, chunk):
                act.wait_ge(S("fu_ready"), i + (UP1 + 1))
                act.activation(a_hi[:, chunk:chunk + 2, :], fu, ACT.Copy).then_inc(S("u_hi"), 1)

            v0 = U_FFN2
            for i in range(2):
                split(v0 + 3 + i)
                up2_hi(i, 8 + 2 * i)

            def ffn2_step(i, m, q, first=False):
                if not first:
                    split(v0 + 2 * q, m * 2)
                up2_hi(i, 8 + 2 * q)
                split(v0 + 1 + 2 * q, m * 2)

            ffn2_step(2, 0, 2, first=True)
            with act.Fori(1, UP2 // 3) as m:
                for q in range(3):
                    ffn2_step(m * 3 + q, m, q)
            ffn2_step(UP2 - 1, UP2 // 3, 0)
            acc_squares(N_UNITS - 1, 7)
            act.wait_ge(S("out_turned"), 1)
            for tb in range(2):
                act.activation(x_tok[:, tb, 0:512], (ps, pt)[tb][:, 0, :], ACT.Copy).then_inc(S("out_ready0"), 1)
            act.wait_ge(S("out_turned"), 2)
            act.activation(x_tok[:, 0, 512:1024], ps[:, 1, :], ACT.Copy).then_inc(S("out_ready1"), 1)

        @block.vector
        def _(dve):
            V_ = Order(dve, "dve_order")

            def split(base, m=0):
                slot = base % SLOTS
                dve.wait_ge(S("w_hi_done"), m * SLOTS + (base + 1))
                dve.tensor_tensor(w_lo[:, slot, :], w_raw[:, slot, :], w_hi[:, slot, :].bitcast(F32), ALU.subtract)\
                   .then_inc(S("w_lo_done"), 1)

            ahead_of = [0]

            def ahead(name_or_u):
                u = UIDX[name_or_u] if isinstance(name_or_u, tuple) else name_or_u
                while ahead_of[0] <= min(u + 2, N_UNITS - 1):
                    split(ahead_of[0])
                    ahead_of[0] += 1
                return u

            def tt(o_, a, b, op):
                return dve.tensor_tensor(o_, a, b, op)

            def stt(o_, a, s_, b, op0, op1):
                return dve.scalar_tensor_tensor(out=o_, in0=a, scalar=s_, in1=b, op0=op0, op1=op1)

            def two(bank):
                return bank[:, :].rearrange("p (a t) -> p a t", a=2)

            rbc2 = rbc[:, :].unsqueeze(1).to_broadcast([P, 2, T])

            def channel_major(name, dst, scale=None):
                b, _n = BANK[name]
                dve.wait_ge(S("unit_done"), UIDX[name] + 1)
                ins = tt(dst, two(pj[b]), rbc2, ALU.mult) if scale is None \
                    else stt(dst, two(pj[b]), scale, rbc2, ALU.mult, ALU.mult)
                ins.then_inc(S(f"pj_read{b}"), 1)
                ahead(name)

            def operand_lo(n, gname, k):
                g = prm_(gname)
                dve.wait_ge(S("opnd_hi"), KC * n + k + 1)
                stt(a_lo[:, k, :], xT[:, k, :], g[:, k:k + 1], a_hi[:, k, :].bitcast(F32), ALU.mult,
                    ALU.subtract).then_inc(S("opnd_lo"), 1)

            def norm_tail(n, sq_t, before_root=None, before_rbc=None, gname=None, ready="x_ready", nxt=None):
                dve.wait_ge(S("sq_ready"), KC * (n + 1))
                tt(ssq_last, sq_t[:, 6, :], sq_t[:, 7, :], ALU.add).then_inc(S("ssq_last_ready"), 1)
                if before_root:
                    before_root()
                await_read(dve, "O", f"norm{n}")
                V_.did(dve.reciprocal(rcol, rt))
                V_.sync()
                dve.tensor_scalar(dgr[:, 0, :], ident, rcol[:, 0:1], None, ALU.mult)
                dve.tensor_scalar(dgr[:, 1, :], ident, rcol[:, 1:2], None, ALU.mult).then_inc(S("diag_ready"), 1)
                if before_rbc:
                    before_rbc()
                await_psum(dve, "O", f"rbc{n}")
                if not gname:
                    read(dve.tensor_copy(rbc[:, :], po[:, 256:512]), "O")
                    await_read(dve, "O", f"rbc{n}")
                    return
                V_.did(tt(upd[0], yT[:, 0, :], po[:, 256:512], ALU.mult))
                V_.sync()
                stt(xT[:, 0, :], upd[0], prm_(gname)[:, 0:1], xT[:, 0, :], ALU.mult, ALU.add)\
                    .then_inc(S(ready), 1)
                read(dve.tensor_copy(rbc[:, :], po[:, 256:512]), "O")
                await_read(dve, "O", f"rbc{n}")
                V_.did(tt(upd[1], yT[:, 1, :], rbc[:, :], ALU.mult))
                if nxt:
                    operand_lo(nxt[0], nxt[1], 0)
                V_.sync()
                for k in range(1, KC):
                    if k >= 2:
                        dve.wait_ge(S("y_scaled"), 6 * (n // 2) + k - 1)
                    stt(xT[:, k, :], upd[1] if k == 1 else yT[:, k, :], prm_(gname)[:, k:k + 1], xT[:, k, :],
                        ALU.mult, ALU.add).then_inc(S(ready), 1)
                    if nxt and k > 1:
                        operand_lo(nxt[0], nxt[1], k - 1)
                if nxt:
                    operand_lo(nxt[0], nxt[1], KC - 1)

            dve.memset(eps_t, EPS).then_inc(S("eps_ready"), 1)
            dve.wait_ge(S("gains_loaded"), 16)
            for k in range(KC):
                if k % 4 == 0:
                    await_psum(dve, "ST"[k // 4], "x")
                dve.tensor_copy(xT[:, k, :], (ps, pt)[k // 4][:, (k // 2) % 2, (k % 2) * T:(k % 2 + 1) * T])\
                   .then_inc(S("x_ready"), 1)
            read(dve.memset(hid, 0.0), "S")
            read(dve.memset(hid_t, 0.0), "T")
            split(0)
            ahead_of[0] = 1
            for k in range(KC):
                operand_lo(0, "g_mix1", k)

            def second_split():
                split(1)
                ahead_of[0] = 2

            norm_tail(0, sq, second_split, lambda: ahead(0))
            for i in range(2):
                channel_major(("sbq", i), sbq[:, 2 * i:2 * i + 2, :], 128.0 ** -0.5)
            for i in range(2):
                channel_major(("sbk", i), sbk[:, 2 * i:2 * i + 2, :])
            ahead(("sbv", 1))

            def narrow_out(use, n):
                await_psum(dve, "O", use)
                read(tt(narrow[0:n, :], po[0:n, 0:T], rbc[0:n, :], ALU.mult), "O")

            def conv(i):
                if i >= 2:
                    dve.wait_ge(S("conv_tap3"), 2 * (i - 1))
                    dve.wait_ge(S("conv_odd"), i - 1)
                channel_major(("xbc", i), xc[i % 2])
                await_value(dve, ("xbc", i))
                dve.wait_ge(S("conv_tap3"), 2 * i + 1)
                if i == 0:
                    dve.wait_ge(S("prm_loaded"), 16)
                for s_ in (1, 2, 3):
                    blk = 2 * i
                    c = (3 - s_) * 16 + blk
                    ins = stt(xbc[:, blk, s_:T], xc[i % 2][:, 0, 0:T - s_], prm_("cw")[:, c:c + 1], xbc[:, blk, s_:T],
                              ALU.mult, ALU.add)
                    if s_ == 3:
                        ins.then_inc(S("conv_even"), 1)
                    else:
                        V_.did(ins)
                        V_.sync()

            def sb_keep(p):
                dve.wait_ge(S("sb_log_ready"), p + 1)
                V_.did(stt(sb_ls[p], ps[:, :, 0:384], 0.0, sb_l[p], ALU.min, ALU.subtract))
                V_.sync()
                read(tt(sb_lk[p], sb_ls[p], ps[:, :, 0:384], ALU.subtract), "S")
                await_read(dve, "S", f"sb{p}")
                tt(sb_lk[p], sb_lk[p], cst_("sbmask").unsqueeze(1).to_broadcast([P, 2, 384]), ALU.mult)\
                    .then_inc(S("sb_lk_ready"), 1)

            def sb_sum(p):
                await_psum(dve, "T", f"sb{p}")
                read(tt(sb_ls[p], sb_ls[p], pt[:, :, 0:384], ALU.add), "T")

            def sb_mask(p):
                dve.wait_ge(S("sb_exp_ready"), p + 1)
                tt(sb_w[p], sb_w[p], cst_("sbmask").unsqueeze(1).to_broadcast([P, 2, 384]), ALU.mult)\
                    .then_inc(S("sb_w_ready"), 1)

            def sb_lo(p):
                dve.wait_ge(S("y_hi"), 2 * p + 2)
                read(tt(a_lo[:, 16 + 2 * p:18 + 2 * p, :], two(po), a_hi[:, 16 + 2 * p:18 + 2 * p, :].bitcast(F32),
                        ALU.subtract), "O")

            conv(0)
            dve.wait_ge(S("cst_loaded"), 16)
            sb_keep(0)
            conv(1)
            conv(2)
            sb_sum(0)
            sb_mask(0)
            sb_keep(1)
            conv(3)
            sb_lo(0)
            conv(4)
            sb_sum(1)
            sb_mask(1)
            conv(5)
            sb_lo(1)
            dve.wait_ge(S("ws_hi"), 1)
            o = PCOLS["ws1"][0]
            tt(ws_lo, prm[:, o:o + 320], ws_hi.bitcast(F32), ALU.subtract).then_inc(S("ws_ready"), 1)
            conv(6)
            narrow_out("dt", 40)
            conv(7)
            await_read(dve, "O", "dt_tok")
            tt(dtx, small40[:, :, 0:16], prm_("dt_bias").unsqueeze(1).to_broadcast([P, 2, 16]), ALU.add)\
                .then_inc(S("dtx_ready"), 1)
            dve.wait_ge(S("dte_ready"), 1)
            dve.wait_ge(S("ea_ready"), 1)
            V_.did(stt(dt_, dtx, 0.0, dt_e, ALU.max, ALU.add))
            V_.sync()
            stt(dta, dt_, -1.0, ea.unsqueeze(1).to_broadcast([P, 2, 16]), ALU.mult, ALU.mult)\
                .then_inc(S("dta_ready"), 1)
            dve.wait_ge(S("xs_half"), 2)
            await_read(dve, "S", "xs")
            await_read(dve, "T", "xs")
            for tb in range(2):
                tt(xdt[:, tb, :].rearrange("p (h c) -> p h c", h=SSM_H),
                   xs_tok[:, tb, :].rearrange("p (h c) -> p h c", h=SSM_H),
                   dt_[:, tb, :].unsqueeze(2).to_broadcast([P, SSM_H, 64]), ALU.mult).then_inc(S("xdt_ready"), 1)
            dve.wait_ge(S("gate_tanh"), 1)
            V_.did(dve.tensor_scalar(gate, gate, 0.5, 0.5, ALU.mult, ALU.add))
            channel_major(("kk", 0), kk)
            await_psum(dve, "T", "cb")
            read(tt(cb[:, :, 0:256], pt[:, :, :].rearrange("p a (b t) -> p (a b) t", b=2),
                    cst_("cbmask")[:, 0:256].unsqueeze(1).to_broadcast([P, 4, 256]), ALU.mult), "T")
            await_psum(dve, "S", "cb")
            read(tt(cb[:, :, 256:384], ps[:, 0, :].rearrange("p (g t) -> p g t", g=4),
                    le.unsqueeze(1).to_broadcast([P, 4, P]), ALU.mult), "S")

            channel_major(("kv", 0), cm)

            def ssm_w(g):
                await_read(dve, "T", "cb")
                await_read(dve, "S", "cb")
                for region, m in (("S", 0), ("T", 2)):
                    await_read(dve, region, f"seg{g}")
                    tt(E[:, m:m + 2, :], E[:, m:m + 2, :], cb[:, g, :].unsqueeze(1).to_broadcast([P, 2, 384]),
                       ALU.mult).then_inc(S("ssm_w_ready"), 1)

            def ssm_out(g):
                await_psum(dve, "O", f"y{g}")
                dve.wait_ge(S("xd_ready"), 1)
                read(tt(y_tok[:, :, g * 256:(g + 1) * 256], two(po), xs_tok[:, :, g * 256:(g + 1) * 256], ALU.add), "O")

            ssm_w(0)
            dve.wait_ge(S("ck_ready"), 4)
            pos = prm_("pos").rearrange("p (v c) -> p v c", v=2)
            for half in range(2):
                for v in range(2):
                    tt(ckp[:, half, v, :].rearrange("p (n c) -> p n c", c=8),
                       ck[:, v, :, :].rearrange("p g t -> p (g t)").rearrange("p (n c) -> p n c", c=8),
                       pos[:, v, half * 8:half * 8 + 8].unsqueeze(1).to_broadcast([P, 32, 8]), ALU.add)\
                        .then_inc(S("ckp_ready"), 1)
            ahead(("vv", 0))
            ssm_out(0)
            ssm_w(1)
            channel_major(("nq", 0), nq[:, 0:2, :], 64.0 ** -0.5)
            ssm_out(1)
            ssm_w(2)
            channel_major(("nq", 1), nq[:, 2:4, :], 64.0 ** -0.5)
            ssm_out(2)
            ssm_w(3)
            ahead(("z", 0))
            ssm_out(3)
            ahead(("z", 1))
            dve.wait_ge(S("hid_tanh"), 1)
            for v in range(2):
                ins = stt(hid[0:64, v, :].rearrange("p (g n) -> p g n", g=2)[:, :, 0:15],
                          hid_t[0:64, v, 0:30].rearrange("p (g n) -> p g n", g=2), 1.0,
                          po[0:64, v * 64:v * 64 + 30].rearrange("p (g n) -> p g n", g=2), ALU.add, ALU.mult)
            read(ins, "O")
            await_read(dve, "O", "hid")
            dve.tensor_copy(hrep[0:64, :].rearrange("p (g h n) -> p g h n", g=2, h=4),
                            hid[0:64, 1, :].rearrange("p (g n) -> p g n", g=2).unsqueeze(2).to_broadcast([64, 2, 4, 16]))\
               .then_inc(S("hid_ready"), 1)
            ahead(("z", 2))
            await_read(dve, "O", "kc")
            tt(vc.rearrange("p j (b d) -> p (j b) d", b=2), vrep.unsqueeze(1).to_broadcast([P, 8, 64]),
               cst_("cmpmask").unsqueeze(2).to_broadcast([P, 8, 64]), ALU.mult).then_inc(S("cmp_v_ready"), 1)
            ahead(("z", 3))
            await_psum(dve, "S", "cmp")
            cb_ = cst_("cmpbias").rearrange("p (t x) -> p t x", t=2)
            for hb in range(2):
                ins = tt(cmp_e[:, :, hb * 64:(hb + 1) * 64], ps[:, hb, 0:128].rearrange("p (t x) -> p t x", t=2),
                         cb_[:, :, hb * 64:(hb + 1) * 64], ALU.add)
            read(ins, "S")
            await_read(dve, "S", "cmp")
            ce = cmp_e.rearrange("p t x -> p (t x)").rearrange("p (h n) -> p h n", n=16)
            V_.did(dve.tensor_reduce(cmx, ce, AX.X, ALU.max))
            V_.sync()
            tt(ce, ce, cmx.unsqueeze(2).to_broadcast([P, 16, 16]), ALU.subtract).then_inc(S("cmp_s_ready"), 1)
            dve.wait_ge(S("cmp_exp"), 1)
            V_.did(dve.tensor_reduce(csm, ce, AX.X, ALU.add))
            V_.sync()
            V_.did(dve.reciprocal(crc, csm))
            V_.sync()
            crc2 = crc.rearrange("p (t h) -> p t h", t=2)
            V_.did(tt(crc2, crc2, gate[:, :, 0:8], ALU.mult))
            V_.sync()
            V_.did(tt(crc2, crc2, cst_("rowvalid").unsqueeze(2).to_broadcast([P, 2, 8]), ALU.mult))
            V_.sync()
            tt(ce, ce, crc.unsqueeze(2).to_broadcast([P, 16, 16]), ALU.mult).then_inc(S("cmp_p_ready"), 1)
            dve.wait_ge(S("z_silu"), 1)
            await_read(dve, "O", "y3")
            tt(y_tok, y_tok, z, ALU.mult).then_inc(S("y_gated"), 1)

            def gm_copy(i):
                b, _n = BANK[("gm", i)]
                channel_major(("gm", i), area[:, gm_at[2 * i] * 256:gm_at[2 * i] * 256 + 512]
                              .rearrange("p (a t) -> p a t", a=2))

            ahead(("gm", 0))
            await_read(dve, "O", "kc")
            gm_copy(0)
            dve.wait_ge(S("y_root"), 1)
            V_.did(dve.reciprocal(ssy, ry))
            V_.sync()
            yv = y_tok.rearrange("p t (g c) -> p (t g) c", g=4)
            tt(yv, yv, ssy.rearrange("p t g -> p (t g)").unsqueeze(2).to_broadcast([P, 8, 256]), ALU.mult)\
                .then_inc(S("y_normed"), 1)
            gm_copy(1)
            nw = prm_("ssm_norm")
            for k in range(KC):
                dve.wait_ge(S("y_hi"), 4 + (k | 1) + 1)
                ins = stt(a_lo[:, 8 + k, :], (ps, pt)[k // 4][:, (k // 2) % 2, (k % 2) * T:(k % 2 + 1) * T],
                          nw[:, k:k + 1], a_hi[:, 8 + k, :].bitcast(F32), ALU.mult, ALU.subtract)
                if k % 4 == 3:
                    read(ins, "ST"[k // 4])
            gm_copy(2)

            def maxima(idx, s_):
                m_, t_ = mx[idx % 2], s_[idx % 2]
                dve.tensor_reduce(m_[:, 0:2], t_[:, :, 0:128], AX.X, ALU.max, negate=True)
                dve.tensor_reduce(m_[:, 2:4], t_[:, :, 128:384], AX.X, ALU.max, negate=True)\
                   .then_inc(S("max_ready"), 1)

            def inverse_sums(idx):
                dve.wait_ge(S("exp_done"), 4 * (idx + 1))
                V_.did(dve.reciprocal(rcp[idx % 2], sums[idx % 2]))
                V_.sync()

            def scale_probs(idx, p_):
                for t in range(2):
                    cols = slice(0, 128) if t == 0 else slice(128, 384)
                    for hb in range(2):
                        c = t * 2 + hb
                        ins = dve.tensor_scalar(p_[idx % 2][:, hb, cols], p_[idx % 2][:, hb, cols],
                                                rcp[idx % 2][:, c:c + 1], None, ALU.mult)
                ins.then_inc(S("probs_ready"), 1)

            def nsa_soft(r):
                j = r // 2
                await_psum(dve, "S", f"n{r}")
                for hb in range(2):
                    ins = stt(sm[r % 2][:, hb, :], cst_("alibi"), SLOPES[hb * 4 + j], ps[:, hb, 0:384], ALU.mult, ALU.add)
                read(ins, "S")
                await_read(dve, "S", f"n{r}")
                maxima(r, sm)

            def nsa_probs(r):
                j, b = r // 2, r % 2
                inverse_sums(r)
                rv = rcp[r % 2].rearrange("p (t h) -> p t h", t=2)
                c = 8 * (b + 1) + j
                V_.did(tt(rv, rv, gate[:, :, c:c + 5:4], ALU.mult))
                V_.sync()
                scale_probs(r, pr)

            def nsa_out_lo(j):
                dve.wait_ge(S("y_hi"), 12 + j + 1)
                read(tt(a_lo[:, 20 + j, :], po[:, (j % 2) * T:(j % 2 + 1) * T], a_hi[:, 20 + j, :].bitcast(F32),
                        ALU.subtract), "O")

            nsa_soft(0)
            gm_copy(3)
            for r in range(8):
                nsa_probs(r)
                gm_copy(4 + r)
                if r < 7:
                    nsa_soft(r + 1)
                if r in (2, 4, 6):
                    nsa_out_lo(r // 2 - 1)
            nsa_out_lo(3)

            def mixed_lo(n):
                dve.wait_ge(S("mix_hi"), n + 1)
                stt(a_lo[:, n, :], mixt[n % 2][:, 0, :], 0.5, a_hi[:, n, :].bitcast(F32), ALU.mult, ALU.subtract)\
                    .then_inc(S("mix_lo"), 1)

            dve.wait_ge(S("gm_tanh"), 12)
            for n in range(8):
                b, _n = BANK[("br", n)]
                dve.wait_ge(S("unit_done"), UIDX[("br", n)] + 1)
                m_ = mixt[n % 2]
                if n >= 2:
                    dve.wait_ge(S("mix_lo"), n - 1)
                stt(m_[:, 0, :], gm[n], 1.0, pj[b][:, 0:T], ALU.add, ALU.mult).then_inc(S("br_ssm_read"), 1)
                stt(m_[:, 1, :], gm[8 + n], 1.0, pj[b][:, T:2 * T], ALU.add, ALU.mult).then_inc(S(f"pj_read{b}"), 1)
                stt(m_[:, 2, :], gm[16 + n], 1.0, ps[:, n % 2, 0:T], ALU.add, ALU.mult).then_inc(S("br_nsa_read"), 1)
                if n:
                    mixed_lo(n - 1)
                ahead(("br", n))
            mixed_lo(7)

            for i in range(4):
                ahead(("wo", i))
            for i in range(4):
                await_value(dve, ("wo", i))
            norm_tail(1, sqy, gname="g_postmix1", nxt=(1, "g_ffn1"))
            norm_tail(2, sq_ffn, lambda: ahead(U_FFN1))

            fw = PCOLS["fw"][0]

            def up1_out(b, u_done):
                dve.wait_ge(S("unit_done"), u_done)
                tt(fx, two(pj[b]), rbc2, ALU.mult).then_inc(S(f"pj_read{b}"), 1)

            def up1_taps(c):
                dve.wait_ge(S("gate_tap2"), c + 1)
                for s_ in (1, 2):
                    w = prm[:, bass.ds(c + (fw + (2 - s_) * 2 * UP1), 1)]
                    stt(facc[:, 0, s_:T], fx[:, 0, 0:T - s_], w, facc[:, 0, s_:T], ALU.mult, ALU.add)\
                        .then_inc(S("gate_taps"), 1)
                    if s_ == 1:
                        dve.wait_ge(S("gate_taps"), c * 2 + 1)

            def up1_product(c):
                dve.wait_ge(S("value_taps"), c + 1)
                dve.wait_ge(S("gelu_done"), c + 1)
                tt(fu[:, 0, :], fg, facc[:, 1, :], ALU.mult).then_inc(S("fu_ready"), 1)

            def up1_lo(c, chunk):
                dve.wait_ge(S("u_hi"), c + 1)
                tt(a_lo[:, chunk, :], fu[:, 0, :], a_hi[:, chunk, :].bitcast(F32), ALU.subtract)\
                    .then_inc(S("u_lo"), 1)

            u0 = U_FFN1
            for c in range(2):
                up1_out(c, u0 + 2)
                ahead(u0 + 1 + c)
                up1_taps(c)
                up1_product(c)
                up1_lo(c, 8 + c)

            def ffn1_step(i, odd, first=False):
                m, chunk = i - 1, 10 if odd else 8
                up1_out(0, i * 3 + u0)
                if not first:
                    split(u0 + 4, m)
                up1_taps(i * 2)
                split(u0 + 5, m)
                up1_product(i * 2)
                up1_lo(i * 2, chunk)
                up1_out(1, i * 3 + (u0 + 1))
                split(u0 + 6, m)
                up1_taps(i * 2 + 1)
                up1_product(i * 2 + 1)
                up1_lo(i * 2 + 1, chunk + 1)

            ffn1_step(1, True, first=True)
            ffn1_step(2, False)
            with dve.Fori(1, DOWN1 // 2) as j:
                ffn1_step(j * 2 + 1, True)
                ffn1_step(j * 2 + 2, False)
            ahead_of[0] = U_FFN1_END + 1

            def acc_copy(n, *banks):
                for q in banks:
                    dve.wait_ge(S("sq_ready"), KC * n + 2 * q + 2)
                    dve.tensor_copy(yT[:, 2 * q:2 * q + 2, :], (ps, pt)[q // 2][:, q % 2, :]
                                    .rearrange("p (a t) -> p a t", a=2)).then_inc(S("acc_copied"), 1)

            ahead(U_FFN1_END - 1)
            acc_copy(3, 0, 1, 2)
            norm_tail(3, sqy, lambda: (acc_copy(3, 3), dve.wait_ge(S("acc_copied"), 4)),
                      gname="g_postffn1", nxt=(2, "g_mix2"))

            dve.wait_ge(S("ws_hi"), 2)
            o2 = PCOLS["ws2"][0]
            tt(ws_lo[:, 0:64], prm[:, o2:o2 + 64], ws_hi[:, 0:64].bitcast(F32), ALU.subtract)\
                .then_inc(S("ws_ready"), 1)
            lv = prm_("lam").rearrange("p (a b d) -> p a b d", a=2, b=2)
            lt_ = lamt.rearrange("p (a d) -> p a d", a=2)
            V_.did(tt(lt_, lv[:, :, 0, :], lv[:, :, 1, :], ALU.mult))
            V_.sync()
            dve.tensor_reduce(lamv[:, 0:2], lt_, AX.X, ALU.add).then_inc(S("lam_sums"), 1)
            norm_tail(4, sq_ffn, lambda: ahead(("dq", 0)))
            channel_major(("dq", 0), dq[:, 0:2, :], 64.0 ** -0.5)
            channel_major(("dk", 0), dk[:, 0:2, :])
            dve.wait_ge(S("t5_scratch"), 16)
            narrow_out("flog", 8)
            dve.wait_ge(S("lam_exp"), 1)
            V_.did(stt(lamv[:, 4:5], lamv[:, 2:3], LAMBDA_INIT, lamv[:, 3:4], ALU.add, ALU.subtract))
            V_.sync()
            V_.did(dve.tensor_scalar(lamv[:, 5:6], lamv[:, 4:5], -1.0, None, ALU.mult))
            V_.sync()
            V_.did(stt(lamv[:, 6:7], lamv[:, 4:5], 1.0, lamv[:, 5:6], ALU.max, ALU.max))
            V_.sync()
            V_.did(dve.reciprocal(lm[:, 0:1], lamv[:, 6:7]))
            V_.sync()
            tt(lm[:, 1:2], lamv[:, 5:6], lm[:, 0:1], ALU.mult)
            stt(lm[:, 2:3], lm[:, 0:1], EPS, lm[:, 0:1], ALU.mult, ALU.mult).then_inc(S("lm_ready"), 1)
            ahead(("dv", 0))
            await_read(dve, "O", "flog_tok")
            tt(fl, fl, prm_("b_f").unsqueeze(1).to_broadcast([P, 2, 8]), ALU.add).then_inc(S("flx_ready"), 1)

            def d_soft(h):
                await_psum(dve, "S", f"d{h}")
                dve.wait_ge(S("t5_ready"), 2 * 16)
                read(tt(sm2[h % 2], ps[:, :, 0:384], t5[:, h, :].unsqueeze(1).to_broadcast([P, 2, 384]), ALU.add), "S")
                await_read(dve, "S", f"d{h}")
                maxima(8 + h, sm2)

            def d_probs(h):
                idx = 8 + h
                inverse_sums(idx)
                if h == 0:
                    dve.wait_ge(S("lm_ready"), 1)
                rv = rcp[h % 2].rearrange("p (t m) -> p t m", t=2)
                V_.did(tt(rv, rv, lm[:, 0:2].unsqueeze(1).to_broadcast([P, 2, 2]), ALU.mult))
                V_.sync()
                p_, r_ = pr2[h % 2], rcp[h % 2]
                halves = (slice(0, 128), slice(128, 384))
                for t, cols in enumerate(halves):
                    V_.did(dve.tensor_scalar(p_[:, 0, cols], p_[:, 0, cols], r_[:, 2 * t:2 * t + 1], None, ALU.mult))
                V_.sync()
                for t, cols in enumerate(halves):
                    ins = stt(p_[:, 0, cols], p_[:, 1, cols], r_[:, 2 * t + 1:2 * t + 2], p_[:, 0, cols],
                              ALU.mult, ALU.add)
                ins.then_inc(S("probs_ready"), 1)

            def f_soft(j):
                await_psum(dve, "S", f"f{j}")
                read(tt(sm2[j % 2], ps[:, :, 0:384], cst_("causal").unsqueeze(1).to_broadcast([P, 2, 384]), ALU.add),
                     "S")
                await_read(dve, "S", f"f{j}")
                maxima(12 + j, sm2)

            def f_out_lo(j):
                dve.wait_ge(S("mix2_hi"), j + 1)
                read(tt(a_lo[:, 12 + j, :], po[:, 0:T], a_hi[:, 12 + j, :].bitcast(F32), ALU.subtract), "O")

            def f_probs(j):
                inverse_sums(12 + j)
                scale_probs(12 + j, pr2)

            d_soft(0)
            dve.wait_ge(S("lfe_ready"), 1)
            stt(lf, fl, 0.0, lf_e, ALU.min, ALU.subtract).then_inc(S("lf_ready"), 1)
            ahead(("dq", 1))
            d_probs(0)
            channel_major(("dq", 1), dq[:, 2:4, :], 64.0 ** -0.5)
            d_soft(1)
            ahead(("dk", 1))
            d_probs(1)
            channel_major(("dk", 1), dk[:, 2:4, :])
            ahead(("dv", 1))
            d_soft(2)
            ahead(("fq", 0))
            d_probs(2)
            channel_major(("fq", 0), fq[:, 0:2, :], 64.0 ** -0.5)
            d_soft(3)
            ahead(("fk", 0))
            d_probs(3)
            channel_major(("fk", 0), fk[:, 0:2, :])
            ahead(("fq", 1))
            channel_major(("fq", 1), fq[:, 2:4, :], 64.0 ** -0.5)
            f_soft(0)
            ahead(("fk", 1))
            f_probs(0)
            channel_major(("fk", 1), fk[:, 2:4, :])
            f_soft(1)
            await_read(dve, "O", "odn")
            V_.did(dve.reciprocal(ods, ods))
            V_.sync()
            tt(dg8, ident.unsqueeze(1).to_broadcast([P, 8, P]), ods.unsqueeze(2).to_broadcast([P, 8, P]), ALU.mult)\
                .then_inc(S("dg8_ready"), 1)
            f_probs(1)
            ahead(("fv", 0))
            f_soft(2)
            f_probs(2)
            ahead(("fv", 1))
            f_out_lo(0)
            f_soft(3)
            f_out_lo(1)
            f_probs(3)
            f_out_lo(2)
            await_psum(dve, "S", "odn")
            for q in range(2):
                ins = stt(odn[:, 2 * q:2 * q + 2, :], od[:, 2 * q:2 * q + 2, :], prm_("subln"),
                          ps[:, q, :].rearrange("p (a t) -> p a t", a=2), ALU.mult, ALU.mult)
                if q == 0:
                    ins.then_inc(S("odn_ready"), 1)
            read(ins, "S")
            dve.wait_ge(S("odn_hi"), 1)
            await_read(dve, "S", "odn")
            stt(a_lo[:, 8:12, :], odn, 1.0 - LAMBDA_INIT, a_hi[:, 8:12, :].bitcast(F32), ALU.mult, ALU.subtract)\
                .then_inc(S("odn_lo"), 1)
            f_out_lo(3)
            for i in range(4):
                ahead(("wo2", i))
            for i in range(4):
                await_value(dve, ("wo2", i))
            norm_tail(5, sqy, gname="g_postmix2", nxt=(3, "g_ffn2"))
            norm_tail(6, sq_ffn, lambda: ahead(U_FFN2))

            def up2_out(n, b, u_done):
                dve.wait_ge(S("unit_done"), u_done)
                tt(fx, two(pj[b]), rbc2, ALU.mult).then_inc(S(f"pj_read{b}"), 1)
                dve.wait_ge(S(f"pj_read{b}"), n + 1)
                stt(fu, fx, 0.0, fx, ALU.max, ALU.mult).then_inc(S("fu_ready"), 1)

            def up2_lo(i, chunk):
                dve.wait_ge(S("u_hi"), i + (UP1 + 1))
                tt(a_lo[:, chunk:chunk + 2, :], fu, a_hi[:, chunk:chunk + 2, :].bitcast(F32), ALU.subtract)\
                    .then_inc(S("u_lo"), 1)

            v0 = U_FFN2
            for i in range(2):
                up2_out(FFN2_BANK0[i], i, v0 + 2)
                split(v0 + 3 + i)
                up2_lo(i, 8 + 2 * i)

            def ffn2_step(i, m, q, first=False):
                if not first:
                    split(v0 + 2 * q, m * 2)
                up2_out(m + FFN2_BANK0[q], q, i * 2 + (v0 - 1))
                up2_lo(i, 8 + 2 * q)
                split(v0 + 1 + 2 * q, m * 2)

            ffn2_step(2, 0, 2, first=True)
            with dve.Fori(1, UP2 // 3) as m:
                for q in range(3):
                    ffn2_step(m * 3 + q, m, q)
            ffn2_step(UP2 - 1, UP2 // 3, 0)
            acc_copy(7, 0, 1, 2)
            norm_tail(7, sqy, lambda: (acc_copy(7, 3), dve.wait_ge(S("acc_copied"), 8)),
                      gname="g_postffn2", ready="x_final")
            dve.wait_ge(S("out_turned"), 2)
            dve.tensor_copy(x_tok[:, 1, 512:1024], pt[:, 1, :]).then_inc(S("out_ready1"), 1)


def pack(v):
    def cols(w, c, n=256):
        return w[:, c:c + n].reshape(KC, P, n).transpose(1, 0, 2).reshape(P, KC * n)

    def parts(w, at):
        return cols(np.concatenate([w[:, a:a + n] for a, n in at], axis=1), 0)

    def down(w, m):
        return w[m * 256:(m + 1) * 256].reshape(2, P, D).transpose(1, 0, 2).reshape(P, 2 * D)

    w, w2 = v["w_in"][0], v["w_in_2"][0]
    up, dn, up2, dn2 = v["ffn_w_up"][0], v["ffn_w_down"][0], v["w_up_2"][0], v["w_down_2"][0]
    z0, xbc0, dt0, sb0, nq0 = 0, D, 3 * D, 3 * D + SSM_H, 3 * D + SSM_H + 1536
    kv0 = nq0 + 512
    gate0 = kv0 + 768
    gm0 = gate0 + 24
    nsa = v["w_br_nsa"][0].reshape(2, 4, 64, D).transpose(1, 0, 2, 3).reshape(512, D)
    br = np.concatenate([v["w_br_ssm"][0], v["w_br_sb"][0], nsa])

    def unit(name):
        kind, i = name
        if kind in ("sbq", "sbk", "sbv"):
            return cols(w, sb0 + 512 * ("sbq", "sbk", "sbv").index(kind) + 256 * i)
        if kind in ("xbc", "z", "gm"):
            return cols(w, {"xbc": xbc0, "z": z0, "gm": gm0}[kind] + 256 * i)
        if kind in ("kk", "kv", "vv"):
            a, b = {"kk": (2, 4), "kv": (0, 1), "vv": (3, 5)}[kind]
            return parts(w, [(kv0 + 128 * a, 128), (kv0 + 128 * b, 128)])
        if kind == "nq":
            return parts(w, [(nq0 + 64 * h, 64) for j in (2 * i, 2 * i + 1) for h in (j, 4 + j)])
        if kind == "br":
            return br[:, 128 * i:128 * (i + 1)].reshape(16, P, P).transpose(1, 0, 2).reshape(P, UNIT)
        if kind == "wo":
            return cols(v["w_out"][0], 256 * i)
        if kind == "wo2":
            return cols(v["w_out_2"][0], 256 * i)
        return cols(w2, 512 * ("dq", "dk", "dv", "fq", "fk", "fv").index(kind) + 256 * i)

    def up1(j):
        return parts(up, [(P * j, P), (FF1 + P * j, P)])

    units = [unit(n) for n in UNITS] + [up1(0), up1(1)]
    for i in range(1, DOWN1):
        units += [up1(2 * i), up1(2 * i + 1), down(dn, i - 1)]
    units += [down(dn, DOWN1 - 1)] + [unit(n) for n in UNITS2] + [cols(up2, 0), cols(up2, 256)]
    for i in range(2, UP2):
        units += [cols(up2, 256 * i), down(dn2, i - 2)]
    units += [down(dn2, DOWN2 - 2), down(dn2, DOWN2 - 1)]
    stream = np.stack(units)

    prm = np.zeros((P, PW), np.float32)

    def put(name, a):
        o, n = PCOLS[name]
        prm[:a.shape[0], o:o + n] = a

    def spread(a):
        return a.reshape(-1, P).T

    for name, key in (("g_mix1", "pre_mix_norm"), ("g_postmix1", "post_mix_norm"), ("g_ffn1", "pre_ffn_norm"),
                      ("g_postffn1", "post_ffn_norm"), ("g_mix2", "ln_attn_pre_2"),
                      ("g_postmix2", "ln_attn_post_2"), ("g_ffn2", "ln_mlp_pre_2"),
                      ("g_postffn2", "ln_mlp_post_2"), ("cw", "ssm_conv_w"), ("cb", "ssm_conv_b"),
                      ("ssm_norm", "ssm_norm"), ("fw", "ffn_conv_w"), ("fb", "ffn_conv_b")):
        put(name, spread(v[key]))
    for name, key in (("dt_bias", "ssm_dt_bias"), ("a_log", "ssm_a_log"), ("ssm_d", "ssm_d"), ("b_f", "b_f_2")):
        put(name, np.broadcast_to(v[key].reshape(1, -1), (P, v[key].size)))
    put("pos", np.hstack([spread(v["cmp_pos_k"]), spread(v["cmp_pos_v"])]))
    put("w2", np.hstack([v["cmp_w2_k"][0], v["cmp_w2_v"][0]]))
    put("subln", v["subln_g_2"].reshape(P, 1))
    lam = np.concatenate([v[n].reshape(-1) for n in ("lam_q1_2", "lam_k1_2", "lam_q2_2", "lam_k2_2")])
    put("lam", np.broadcast_to(lam, (P, 256)))
    put("rel", np.concatenate([v["rel_bias_2"], np.full((1, 4), NEG, np.float32)]))
    put("ws1", cols(np.concatenate([w[:, dt0:dt0 + 16], w[:, gate0:gate0 + 24]], axis=1), 0, 40))
    put("ws2", cols(w2, 6 * 512, 8))
    cmpw = np.stack([v[n][0].reshape(16, P, 64).transpose(1, 0, 2) for n in ("cmp_w1_k", "cmp_w1_v")])
    return {"stream": stream, "params": prm, "consts": constants(), "cmpw": cmpw, "x_in": v["x"]}


def kernel(**inputs):
    import concourse.bacc as bacc
    from concourse.bass_utils import run_bass_kernel_spmd

    nc = bacc.Bacc("TRN2", target_bir_lowering=False, num_devices=1)
    arrays = {n: np.ascontiguousarray(a) for n, a in pack({k: np.asarray(a) for k, a in inputs.items()}).items()}
    aps = {n: nc.dram_tensor(n, a.shape, mybir.dt.from_np(a.dtype), kind="ExternalInput").ap()
           for n, a in arrays.items()}
    out = nc.dram_tensor("out", (1, T, D), F32, kind="ExternalOutput").ap()
    program(nc, aps["stream"], aps["params"], aps["consts"], aps["cmpw"], aps["x_in"], out)
    r = run_bass_kernel_spmd(nc, [arrays], core_ids=[0])
    return r.results[0]["out"]
```
